# Optimizing a Trainium2 kernel written in Bass

```python
import jax, jax.numpy as jnp
from jax import lax
import numpy as np
import math

D_MODEL = 1024
BATCH = 1
SEQ = 256
DEPTH = 2

N_A_LAYERS = DEPTH // 2
N_B_LAYERS = DEPTH - N_A_LAYERS
CHUNK = 128
A_EXPAND = 2
A_WIDTH = A_EXPAND * D_MODEL
A_GROUPS = 16
A_GROUP_DIM = A_WIDTH // A_GROUPS
HEAD_DIM = 64
N_Q_HEADS = D_MODEL // HEAD_DIM
N_KV_HEADS = max(1, N_Q_HEADS // 8)
Q_PER_KV = N_Q_HEADS // N_KV_HEADS
B_WIDTH = N_Q_HEADS * HEAD_DIM
KV_WIDTH = N_KV_HEADS * HEAD_DIM
WINDOW = 128
ROPE_THETA = 10000.0
EPS = 1e-5


def rms_norm(x, g):
    xf = x.astype(jnp.float32)
    y = xf * lax.rsqrt(jnp.mean(xf * xf, axis=-1, keepdims=True) + EPS) * g.astype(jnp.float32)
    return y.astype(x.dtype)

def layer_norm(x, g, b):
    xf = x.astype(jnp.float32)
    mu = jnp.mean(xf, axis=-1, keepdims=True)
    xc = xf - mu
    var = jnp.mean(xc * xc, axis=-1, keepdims=True)
    y = xc * lax.rsqrt(var + EPS) * g.astype(jnp.float32) + b.astype(jnp.float32)
    return y.astype(x.dtype)

def rotary(x, pos):
    dh = x.shape[-1]
    inv_freq = ROPE_THETA ** (-jnp.arange(0, dh, 2, dtype=jnp.float32) / dh)
    ang = pos[:, None] * inv_freq[None, :]
    cos = jnp.cos(ang)[None, :, None, :].astype(x.dtype)
    sin = jnp.sin(ang)[None, :, None, :].astype(x.dtype)
    x1, x2 = jnp.split(x, 2, axis=-1)
    return jnp.concatenate([x1 * cos - x2 * sin, x2 * cos + x1 * sin], axis=-1)

def band(t):
    b, s, h, d = t.shape
    blk = t.reshape(b, s // CHUNK, CHUNK, h, d)
    prev = jnp.concatenate([jnp.zeros_like(blk[:, :1]), blk[:, :-1]], axis=1)
    return jnp.concatenate([prev, blk], axis=2)

def gmlp_mixer(h, w_in, ln_g, ln_b, ws, bs, w_out):
    b, s, _ = h.shape
    nc = s // CHUNK
    z = h @ w_in
    u, v, g = jnp.split(z, 3, axis=-1)
    v = layer_norm(v, ln_g, ln_b)
    v = v.reshape(b, nc, CHUNK, A_GROUPS, A_GROUP_DIM)
    causal = jnp.tril(jnp.ones((CHUNK, CHUNK), dtype=bool))
    wsm = jnp.where(causal[None], ws, jnp.zeros_like(ws)).astype(v.dtype)
    sv = jnp.einsum('gts,bcsgd->bctgd', wsm, v) + bs.T[:, :, None].astype(v.dtype)
    sv = sv.reshape(b, s, A_WIDTH)
    y = u * sv * jax.nn.silu(g)
    return y @ w_out

def swa_mixer(h, k_band, v_band, pos, w_in, b_q, sinks, w_out):
    b, s, _ = h.shape
    nb = s // CHUNK
    z = h @ w_in
    q, g = jnp.split(z, 2, axis=-1)
    q = (q + b_q).reshape(b, s, N_Q_HEADS, HEAD_DIM)
    q = rotary(q, pos).reshape(b, nb, CHUNK, N_KV_HEADS, Q_PER_KV, HEAD_DIM)
    scores = jnp.einsum('bnqhrd,bnkhd->bnhrqk', q, k_band).astype(jnp.float32) * (HEAD_DIM ** -0.5)
    qi = jnp.arange(CHUNK)[:, None]
    kj = jnp.arange(2 * CHUNK)[None, :]
    rel = kj - CHUNK - qi
    in_window = (rel <= 0) & (rel > -WINDOW)
    key_valid = (jnp.arange(nb)[:, None] * CHUNK + jnp.arange(2 * CHUNK)[None, :] - CHUNK) >= 0
    mask = in_window[None] & key_valid[:, None, :]
    scores = jnp.where(mask[None, :, None, None], scores, -jnp.inf)
    sink = sinks.astype(jnp.float32).reshape(N_KV_HEADS, Q_PER_KV)[None, None, :, :, None, None]
    m = jnp.maximum(jnp.max(scores, axis=-1, keepdims=True), sink)
    p = jnp.exp(scores - m)
    denom = jnp.sum(p, axis=-1, keepdims=True) + jnp.exp(sink - m)
    p = (p / denom).astype(v_band.dtype)
    o = jnp.einsum('bnhrqk,bnkhd->bnqhrd', p, v_band).reshape(b, s, B_WIDTH)
    y = o * jax.nn.silu(g)
    return y @ w_out

def first_inputs(seed: int = 0) -> dict:
    key = jax.random.key(seed)
    ks = jax.random.split(key, 20)
    f32 = jnp.float32
    nrm = lambda k, shp, sc: jax.random.normal(k, shp, f32) * sc
    return {
        "x": nrm(ks[0], (BATCH, SEQ, D_MODEL), 1.0),
        "a_norm_g": 1.0 + nrm(ks[1], (N_A_LAYERS, D_MODEL), 0.02),
        "a_w_in": nrm(ks[2], (N_A_LAYERS, D_MODEL, 3 * A_WIDTH), D_MODEL ** -0.5),
        "a_ln_g": 1.0 + nrm(ks[3], (N_A_LAYERS, A_WIDTH), 0.02),
        "a_ln_b": nrm(ks[4], (N_A_LAYERS, A_WIDTH), 0.02),
        "a_ws": nrm(ks[5], (N_A_LAYERS, A_GROUPS, CHUNK, CHUNK), 0.5 * CHUNK ** -0.5),
        "a_bs": 1.0 + nrm(ks[6], (N_A_LAYERS, A_GROUPS, CHUNK), 0.02),
        "a_w_out": nrm(ks[7], (N_A_LAYERS, A_WIDTH, D_MODEL), 0.5 * A_WIDTH ** -0.5),
        "kv_norm_g": 1.0 + nrm(ks[8], (D_MODEL,), 0.02),
        "w_kv": nrm(ks[9], (D_MODEL, 2 * KV_WIDTH), D_MODEL ** -0.5),
        "b_kv": nrm(ks[10], (2 * KV_WIDTH,), 0.02),
        "b_norm_g": 1.0 + nrm(ks[11], (N_B_LAYERS, D_MODEL), 0.02),
        "b_w_in": nrm(ks[12], (N_B_LAYERS, D_MODEL, 2 * B_WIDTH), D_MODEL ** -0.5),
        "b_bq": nrm(ks[13], (N_B_LAYERS, B_WIDTH), 0.02),
        "b_sinks": nrm(ks[14], (N_B_LAYERS, N_Q_HEADS), 1.0),
        "b_w_out": nrm(ks[15], (N_B_LAYERS, B_WIDTH, D_MODEL), B_WIDTH ** -0.5),
        "final_norm_g": 1.0 + nrm(ks[16], (D_MODEL,), 0.02),
    }

def first_block(x, a_norm_g, a_w_in, a_ln_g, a_ln_b, a_ws, a_bs, a_w_out, kv_norm_g, w_kv, b_kv,
              b_norm_g, b_w_in, b_bq, b_sinks, b_w_out, final_norm_g):
    b, s, _ = x.shape
    pos = jnp.arange(s, dtype=jnp.float32)
    h = x
    k_band = None
    v_band = None
    for l in range(DEPTH):
        if l < N_A_LAYERS:
            i = l
            h = h + gmlp_mixer(rms_norm(h, a_norm_g[i]), a_w_in[i], a_ln_g[i], a_ln_b[i],
                               a_ws[i], a_bs[i], a_w_out[i])
        else:
            if l == N_A_LAYERS:
                kv = rms_norm(h, kv_norm_g) @ w_kv + b_kv
                k, v = jnp.split(kv, 2, axis=-1)
                k = rotary(k.reshape(b, s, N_KV_HEADS, HEAD_DIM), pos)
                v = v.reshape(b, s, N_KV_HEADS, HEAD_DIM)
                k_band = band(k)
                v_band = band(v)
            i = l - N_A_LAYERS
            h = h + swa_mixer(rms_norm(h, b_norm_g[i]), k_band, v_band, pos,
                              b_w_in[i], b_bq[i], b_sinks[i], b_w_out[i])
    return rms_norm(h, final_norm_g)


N_MIXERS = 2
N_RET_LAYERS = (DEPTH + 1) // 2
N_MLA_LAYERS = DEPTH // 2
DN_ALPHA = (2.0 * DEPTH) ** 0.25
DN_BETA = (8.0 * DEPTH) ** -0.25
LN_EPS = 1e-5
ROPE_BASE = 10000.0

RET_HEADS = 4
RET_DK = D_MODEL // RET_HEADS
RET_DV = 2 * RET_DK
RET_HK = RET_HEADS * RET_DK
RET_HV = RET_HEADS * RET_DV
RET_IN = 2 * RET_HK + 2 * RET_HV
RET_CHUNK = 128

MLA_HEADS = 8
MLA_NOPE = 128
MLA_ROPE = 64
MLA_VDIM = 128
MLA_Q_RANK = 384
MLA_KV_RANK = 256
MLA_IN = MLA_Q_RANK + MLA_KV_RANK + MLA_ROPE
MLA_QBLOCK = 128

PEER_HEADS = 8
PEER_NKEYS = 128
PEER_EXPERTS = PEER_NKEYS * PEER_NKEYS
PEER_DKEY = 256
PEER_HALF = PEER_DKEY // 2
PEER_TOPK = 16
PEER_TOKEN_BLOCK = 128


def layer_norm_2(x, g, b):
    xf = x.astype(jnp.float32)
    mu = jnp.mean(xf, axis=-1, keepdims=True)
    var = jnp.mean(jnp.square(xf - mu), axis=-1, keepdims=True)
    return ((xf - mu) * lax.rsqrt(var + LN_EPS) * g.astype(jnp.float32) + b.astype(jnp.float32)).astype(x.dtype)

def rms_norm_2(x, g):
    xf = x.astype(jnp.float32)
    ms = jnp.mean(jnp.square(xf), axis=-1, keepdims=True)
    return (xf * lax.rsqrt(ms + LN_EPS) * g.astype(jnp.float32)).astype(x.dtype)

def rotary_2(x, positions):
    d = x.shape[-1]
    inv_freq = ROPE_BASE ** (-jnp.arange(0, d, 2, dtype=jnp.float32) / d)
    ang = positions.astype(jnp.float32)[..., None] * inv_freq
    cos = jnp.cos(ang)[:, :, None, :]
    sin = jnp.sin(ang)[:, :, None, :]
    x1, x2 = jnp.split(x.astype(jnp.float32), 2, axis=-1)
    return jnp.concatenate([x1 * cos - x2 * sin, x1 * sin + x2 * cos], axis=-1).astype(x.dtype)

def retention_scan(q, k, v, log_gamma, strict):
    B, S, H, dk = q.shape
    dv = v.shape[-1]
    C = RET_CHUNK
    n_chunks = S // C
    dt = q.dtype
    idx = jnp.arange(C, dtype=jnp.float32)
    diff = idx[:, None] - idx[None, :]
    keep = (diff > 0) if strict else (diff >= 0)
    lg = log_gamma[:, None, None]
    decay = jnp.where(keep[None], jnp.exp(jnp.maximum(diff, 0.0)[None] * lg), 0.0).astype(dt)
    xi = jnp.exp((idx + 1.0)[None, :] * log_gamma[:, None]).astype(dt)
    zeta = jnp.exp((C - 1.0 - idx)[None, :] * log_gamma[:, None]).astype(dt)
    gamma_c = jnp.exp(C * log_gamma).astype(dt)[None, :, None, None]

    def to_chunks(t):
        return t.reshape(B, n_chunks, C, H, t.shape[-1]).transpose(1, 0, 3, 2, 4)

    def step(state, inp):
        qi, ki, vi = inp
        inner = jnp.einsum('bhnm,bhmv->bhnv', jnp.einsum('bhnd,bhmd->bhnm', qi, ki) * decay[None], vi)
        cross = jnp.einsum('bhnd,bhdv->bhnv', qi, state) * xi[None, :, :, None]
        state = gamma_c * state + jnp.einsum('bhmd,bhmv->bhdv', ki * zeta[None, :, :, None], vi)
        return state, inner + cross

    state0 = jnp.zeros((B, H, dk, dv), dt)
    _, out = lax.scan(step, state0, (to_chunks(q), to_chunks(k), to_chunks(v)))
    return out.transpose(1, 0, 3, 2, 4).reshape(B, S, H, dv)

def retention_mixer(x, positions, w_in, log1m_decay, gn_g, gn_b, w_out):
    B, S, _ = x.shape
    proj = x @ w_in
    q, k, v, g = jnp.split(proj, [RET_HK, 2 * RET_HK, 2 * RET_HK + RET_HV], axis=-1)
    q = rotary_2(q.reshape(B, S, RET_HEADS, RET_DK), positions)
    k = rotary_2(k.reshape(B, S, RET_HEADS, RET_DK), positions) * (RET_DK ** -0.5)
    v = v.reshape(B, S, RET_HEADS, RET_DV)
    log_gamma = jnp.log1p(-jnp.exp(log1m_decay.astype(jnp.float32)))
    fwd = retention_scan(q, k, v, log_gamma[0], strict=False)
    bwd = jnp.flip(retention_scan(jnp.flip(q, 1), jnp.flip(k, 1), jnp.flip(v, 1), log_gamma[1], strict=True), 1)
    y = (fwd + bwd).astype(jnp.float32)
    mu = jnp.mean(y, axis=-1, keepdims=True)
    var = jnp.mean(jnp.square(y - mu), axis=-1, keepdims=True)
    yn = ((y - mu) * lax.rsqrt(var + LN_EPS)).reshape(B, S, RET_HV)
    yn = (yn * gn_g.astype(jnp.float32) + gn_b.astype(jnp.float32)).astype(x.dtype)
    return (jax.nn.silu(g) * yn) @ w_out

def mla_mixer(x, positions, w_in, q_norm_g, kv_norm_g, w_uq, w_ukv, w_out):
    B, S, _ = x.shape
    c_q, c_kv, k_rope = jnp.split(x @ w_in, [MLA_Q_RANK, MLA_Q_RANK + MLA_KV_RANK], axis=-1)
    q = (rms_norm_2(c_q, q_norm_g) @ w_uq).reshape(B, S, MLA_HEADS, MLA_NOPE + MLA_ROPE)
    q_nope, q_rope = jnp.split(q, [MLA_NOPE], axis=-1)
    q_rope = rotary_2(q_rope, positions)
    kv = (rms_norm_2(c_kv, kv_norm_g) @ w_ukv).reshape(B, S, MLA_HEADS, MLA_NOPE + MLA_VDIM)
    k_nope, v = jnp.split(kv, [MLA_NOPE], axis=-1)
    k_rope = rotary_2(k_rope[:, :, None, :], positions)[:, :, 0, :]
    scale = (MLA_NOPE + MLA_ROPE) ** -0.5
    nb = S // MLA_QBLOCK

    def blocks(t):
        return t.reshape(B, nb, MLA_QBLOCK, MLA_HEADS, t.shape[-1]).transpose(1, 0, 2, 3, 4)

    def attend(blk):
        qn, qr = blk
        s = jnp.einsum('bqhd,bkhd->bhqk', qn, k_nope) + jnp.einsum('bqhd,bkd->bhqk', qr, k_rope)
        p = jax.nn.softmax(s.astype(jnp.float32) * scale, axis=-1).astype(v.dtype)
        return jnp.einsum('bhqk,bkhd->bqhd', p, v)

    o = lax.map(attend, (blocks(q_nope), blocks(q_rope)))
    o = o.transpose(1, 0, 2, 3, 4).reshape(B, S, MLA_HEADS * MLA_VDIM)
    return o @ w_out

def peer_ffn(x, w_q, sub_keys, u, v):
    B, S, D = x.shape
    T = B * S
    xt = x.reshape(T // PEER_TOKEN_BLOCK, PEER_TOKEN_BLOCK, D)

    def block(xb):
        q = (xb @ w_q).reshape(PEER_TOKEN_BLOCK, PEER_HEADS, 2, PEER_HALF)
        s = jnp.einsum('thcd,hckd->thck', q, sub_keys).astype(jnp.float32)
        s1, i1 = lax.top_k(s[:, :, 0], PEER_TOPK)
        s2, i2 = lax.top_k(s[:, :, 1], PEER_TOPK)
        cand_s = (s1[..., :, None] + s2[..., None, :]).reshape(PEER_TOKEN_BLOCK, PEER_HEADS, PEER_TOPK * PEER_TOPK)
        cand_i = (i1[..., :, None] * PEER_NKEYS + i2[..., None, :]).reshape(PEER_TOKEN_BLOCK, PEER_HEADS, PEER_TOPK * PEER_TOPK)
        top_s, pos = lax.top_k(cand_s, PEER_TOPK)
        eidx = jnp.take_along_axis(cand_i, pos, axis=-1)
        gate = jax.nn.softmax(top_s, axis=-1).astype(xb.dtype)
        h = jax.nn.gelu(jnp.einsum('thkd,td->thk', u[eidx], xb), approximate=False)
        return jnp.einsum('thk,thkd->td', gate * h, v[eidx])

    return lax.map(block, xt).reshape(B, S, D)

def second_inputs(seed: int = 0) -> dict:
    key = jax.random.key(seed)
    ks = jax.random.split(key, 24)
    f32 = jnp.float32
    nrm = lambda k, shape, s: jax.random.normal(k, shape, f32) * s
    x = jax.random.normal(ks[0], (BATCH, SEQ, D_MODEL), f32)
    offsets = jax.random.randint(ks[1], (BATCH, 1), 0, 512, dtype=jnp.int32)
    positions = (offsets + jnp.arange(SEQ, dtype=jnp.int32)[None, :]).astype(jnp.int32)
    ret_w_in = nrm(ks[2], (N_RET_LAYERS, D_MODEL, RET_IN), D_MODEL ** -0.5)
    base = (-5.0 - jnp.arange(RET_HEADS, dtype=f32)) * math.log(2.0)
    ret_log1m_decay = base[None, None, :] + nrm(ks[3], (N_RET_LAYERS, 2, RET_HEADS), 0.05)
    ret_gn_g = 1.0 + nrm(ks[4], (N_RET_LAYERS, RET_HV), 0.02)
    ret_gn_b = nrm(ks[5], (N_RET_LAYERS, RET_HV), 0.02)
    ret_w_out = nrm(ks[6], (N_RET_LAYERS, RET_HV, D_MODEL), DN_BETA * RET_HV ** -0.5)
    mla_w_in = nrm(ks[7], (N_MLA_LAYERS, D_MODEL, MLA_IN), D_MODEL ** -0.5)
    mla_q_norm = 1.0 + nrm(ks[8], (N_MLA_LAYERS, MLA_Q_RANK), 0.02)
    mla_kv_norm = 1.0 + nrm(ks[9], (N_MLA_LAYERS, MLA_KV_RANK), 0.02)
    mla_w_uq = nrm(ks[10], (N_MLA_LAYERS, MLA_Q_RANK, MLA_HEADS * (MLA_NOPE + MLA_ROPE)), MLA_Q_RANK ** -0.5)
    mla_w_ukv = nrm(ks[11], (N_MLA_LAYERS, MLA_KV_RANK, MLA_HEADS * (MLA_NOPE + MLA_VDIM)), MLA_KV_RANK ** -0.5)
    mla_w_out = nrm(ks[12], (N_MLA_LAYERS, MLA_HEADS * MLA_VDIM, D_MODEL), DN_BETA * (MLA_HEADS * MLA_VDIM) ** -0.5)
    peer_w_q = nrm(ks[13], (DEPTH, D_MODEL, PEER_HEADS * PEER_DKEY), D_MODEL ** -0.5)
    peer_sub_keys = nrm(ks[14], (DEPTH, PEER_HEADS, 2, PEER_NKEYS, PEER_HALF), PEER_HALF ** -0.5)
    peer_u = nrm(ks[15], (DEPTH, PEER_EXPERTS, D_MODEL), D_MODEL ** -0.5)
    peer_v = nrm(ks[16], (DEPTH, PEER_EXPERTS, D_MODEL), DN_BETA * (PEER_HEADS * PEER_TOPK) ** -0.5)
    ln_mix_g = 1.0 + nrm(ks[17], (DEPTH, D_MODEL), 0.02)
    ln_mix_b = nrm(ks[18], (DEPTH, D_MODEL), 0.02)
    ln_ffn_g = 1.0 + nrm(ks[19], (DEPTH, D_MODEL), 0.02)
    ln_ffn_b = nrm(ks[20], (DEPTH, D_MODEL), 0.02)
    return {'x': x, 'positions': positions,
            'ret_w_in': ret_w_in, 'ret_log1m_decay': ret_log1m_decay, 'ret_gn_g': ret_gn_g, 'ret_gn_b': ret_gn_b, 'ret_w_out': ret_w_out,
            'mla_w_in': mla_w_in, 'mla_q_norm': mla_q_norm, 'mla_kv_norm': mla_kv_norm, 'mla_w_uq': mla_w_uq, 'mla_w_ukv': mla_w_ukv, 'mla_w_out': mla_w_out,
            'peer_w_q': peer_w_q, 'peer_sub_keys': peer_sub_keys, 'peer_u': peer_u, 'peer_v': peer_v,
            'ln_mix_g': ln_mix_g, 'ln_mix_b': ln_mix_b, 'ln_ffn_g': ln_ffn_g, 'ln_ffn_b': ln_ffn_b}

def second_block(x, positions,
              ret_w_in, ret_log1m_decay, ret_gn_g, ret_gn_b, ret_w_out,
              mla_w_in, mla_q_norm, mla_kv_norm, mla_w_uq, mla_w_ukv, mla_w_out,
              peer_w_q, peer_sub_keys, peer_u, peer_v,
              ln_mix_g, ln_mix_b, ln_ffn_g, ln_ffn_b):
    h = x
    for i in range(DEPTH):
        j = i // N_MIXERS
        if i % N_MIXERS == 0:
            mix = retention_mixer(h, positions, ret_w_in[j], ret_log1m_decay[j], ret_gn_g[j], ret_gn_b[j], ret_w_out[j])
        else:
            mix = mla_mixer(h, positions, mla_w_in[j], mla_q_norm[j], mla_kv_norm[j], mla_w_uq[j], mla_w_ukv[j], mla_w_out[j])
        h = layer_norm_2(DN_ALPHA * h + mix, ln_mix_g[i], ln_mix_b[i])
        ffn = peer_ffn(h, peer_w_q[i], peer_sub_keys[i], peer_u[i], peer_v[i])
        h = layer_norm_2(DN_ALPHA * h + ffn, ln_ffn_g[i], ln_ffn_b[i])
    return h


def setup_inputs(seed=0):
    out = dict(first_inputs(seed))
    for name, value in second_inputs(seed + 1).items():
        if name != "x":
            out[name + "_2"] = value
    return out


def reference(
    x, a_norm_g, a_w_in, a_ln_g, a_ln_b, a_ws, a_bs, a_w_out, kv_norm_g, w_kv, b_kv, b_norm_g,
    b_w_in, b_bq, b_sinks, b_w_out, final_norm_g, positions_2, ret_w_in_2, ret_log1m_decay_2,
    ret_gn_g_2, ret_gn_b_2, ret_w_out_2, mla_w_in_2, mla_q_norm_2, mla_kv_norm_2, mla_w_uq_2,
    mla_w_ukv_2, mla_w_out_2, peer_w_q_2, peer_sub_keys_2, peer_u_2, peer_v_2, ln_mix_g_2,
    ln_mix_b_2, ln_ffn_g_2, ln_ffn_b_2,
):
    x = first_block(
        x, a_norm_g, a_w_in, a_ln_g, a_ln_b, a_ws, a_bs, a_w_out, kv_norm_g, w_kv, b_kv,
        b_norm_g, b_w_in, b_bq, b_sinks, b_w_out, final_norm_g,
    )
    return second_block(
        x, positions_2, ret_w_in_2, ret_log1m_decay_2, ret_gn_g_2, ret_gn_b_2, ret_w_out_2,
        mla_w_in_2, mla_q_norm_2, mla_kv_norm_2, mla_w_uq_2, mla_w_ukv_2, mla_w_out_2,
        peer_w_q_2, peer_sub_keys_2, peer_u_2, peer_v_2, ln_mix_g_2, ln_mix_b_2, ln_ffn_g_2,
        ln_ffn_b_2,
    )


_drawn_inputs = setup_inputs


def setup_inputs(seed=0):
    import zlib

    import numpy as np

    out = dict(_drawn_inputs(seed))
    spreads = {}
    factors = {'a_norm_g': 5.345,
     'a_ln_g': 8.0,
     'a_ln_b': 8.0,
     'a_bs': 8.0,
     'kv_norm_g': 8.0,
     'b_kv': 4.573,
     'b_norm_g': 8.0,
     'b_bq': 8.0,
     'b_sinks': 3.894,
     'ret_gn_g_2': 8.0,
     'ret_gn_b_2': 8.0,
     'mla_q_norm_2': 8.0,
     'mla_kv_norm_2': 8.0,
     'peer_u_2': 2.94}
    for name, (base, spread) in spreads.items():
        noise = np.random.default_rng([zlib.crc32(name.encode()), seed]).standard_normal(out[name].shape)
        drawn = base * np.exp(spread * noise) if base else spread * noise
        out[name] = __import__('jax').numpy.asarray(drawn.astype(out[name].dtype))
    for name, factor in factors.items():
        out[name] = (out[name] * factor).astype(out[name].dtype)
    return out
```

```python
from contextlib import ExitStack

import numpy as np

import concourse.bass as bass
from concourse import mybir

P = 128
T = 256
NB = T // P
D = 1024
DC = D // P
W_A = 2048
RING = 4
EPS = 1e-5
ALPHA = 4.0 ** 0.25
HEADS_B, KVH, DH = 16, 2, 64
RET_H, RET_DK, RET_DV = 4, 256, 512
MLA_H, Q_RANK, KV_RANK, ROPE = 8, 384, 256, 64
PK_H, NKEYS, TOPK = 8, 128, 16
NEG = -1.0e30
LOWEST = -3.0e38

SLAB_STAGES = [
    ("a_v", 8), ("a_u", 8), ("a_g", 8), ("a_out", 8),
    ("b_kv", 1), ("b_q", 4), ("b_g", 4), ("b_out", 4),
    ("r_qk", 8), ("r_v", 8), ("r_g", 8), ("r_out", 8),
    ("pq0", 8), ("u0", 64), ("v0", 64),
    ("m_in", 3), ("m_qn", 4), ("m_qr", 2), ("m_kv", 8), ("m_out", 4),
    ("pq1", 8), ("u1", 64), ("v1", 64),
]
X_STAGES = [
    ("a_tr", 4), ("a_sv", 8), ("b_tr", 4), ("b_ktr", 1), ("b_qtr", 4),
    ("b_s0", 4), ("b_s1", 8), ("b_pt0", 4), ("b_pt1", 8), ("b_pv0", 2), ("b_pv1", 2),
    ("r_tr", 4), ("r_s", 4), ("r_y", 8), ("r_yt", 8),
    ("p_tr0", 4), ("p_s0", 8), ("p_kt0", 2), ("p_w0", 64), ("p_y0", 4), ("p_yr0", 4),
    ("m_tr", 4), ("m_ct", 3), ("m_krt", 1), ("m_qrt", 2), ("m_s", 8), ("m_pt", 8), ("m_pv", 4),
    ("p_tr1", 4), ("p_s1", 8), ("p_kt1", 2), ("p_w1", 64), ("p_y1", 4), ("p_yr1", 4),
]


def first_index(stages):
    at, out = 0, {}
    for name, n in stages:
        out[name] = at
        at += n
    return out, at


SLAB0, N_SLABS = first_index(SLAB_STAGES)
X0, _ = first_index(X_STAGES)
SLABS = dict(SLAB_STAGES)
XTILES = dict(X_STAGES)


def tiles_before(slab):
    n = 0
    for name, count in SLAB_STAGES:
        if name in ("v0", "v1"):
            continue
        n += sum(1 for s in range(SLAB0[name], SLAB0[name] + count) if s < slab and s % 4 == slab % 4)
    return n


COLS = [("a_g", 8), ("kv_g", 8), ("b_g", 8), ("gn_g", 16), ("gn_b", 16), ("m_qg", 3), ("m_kvg", 2), ("invf", 1)]
ROWS = [("ln_g", 2048), ("ln_b", 2048), ("bs", 2048), ("bq", 1024), ("bkv", 256), ("sinks", 16),
        ("decay", 8), ("invf_row", 32), ("fin_g", 1024),
        ("mix0", 2048), ("ffn0", 2048), ("mix1", 2048), ("ffn1", 2048)]
COL0, N_COLS = first_index(COLS)
ROW0, N_ROWS = first_index(ROWS)
ROWN = dict(ROWS)


def build(nc, slabs, x_in, cols_in, rows_in, ws_in, keys_in, pos_row, pos_col, rope_in, diff_in, out):
    f32, u32, i32 = mybir.dt.float32, mybir.dt.uint32, mybir.dt.int32
    ALU, ACT, AX = mybir.AluOpType, mybir.ActivationFunctionType, mybir.AxisListType
    ctx = ExitStack()
    with ctx:
        def sb(name, shape, dt=f32):
            return ctx.enter_context(nc.sbuf_tensor(name, shape, dt))

        made = {}

        def sem(name):
            if name not in made:
                made[name] = ctx.enter_context(nc.semaphore(name))
            return made[name]

        big = sb("big", [P, NKEYS * T])
        ring = [sb(f"ring{i}", [P, 2048]) for i in range(RING)]
        hT = sb("hT", [P, DC, T])
        h = sb("h", [P, NB, D])
        keysT = sb("keysT", [P, 16, NKEYS])
        ident = sb("ident", [P, P])
        iota = sb("iota", [P, P])
        lnw = sb("lnw", [P, 2, D])
        picksT = sb("picksT", [P, 3, T])
        key1 = sb("key1", [P, 2, 4])
        hot = sb("hot", [P, 2, 2, 4, NKEYS])
        cols = sb("cols", [P, N_COLS])
        rope_row = sb("rope_row", [P, NB, 2, 32])
        st = sb("st", [P, 8, 6])
        mv = sb("mv", [P, 8, 2])
        rstd = sb("rstd", [P, 8])
        mx = sb("mx", [P, 16])
        negm = sb("negm", [P, 16])
        rsum = sb("rsum", [P, 16])
        esink = sb("esink", [P, 16])
        rden = sb("rden", [P, 16])
        G = [ctx.enter_context(nc.psum_tensor(f"G{i}", [P, 512], f32)) for i in range(4)]
        X = [ctx.enter_context(nc.psum_tensor(f"X{i}", [P, 512], f32)) for i in range(4)]

        def area(off, *shape):
            n = int(np.prod(shape))
            a = big[:, off:off + n]
            if len(shape) == 1:
                return a
            names = "abcd"[:len(shape)]
            return a.rearrange(f"p ({' '.join(names)}) -> p {' '.join(names)}",
                               **dict(zip(names[1:], shape[1:])))

        def col(name, i):
            return cols[:, COL0[name] + i:COL0[name] + i + 1]

        def bc(ap, axis, n):
            shape = list(ap.shape)
            shape.insert(axis, n)
            return ap.unsqueeze(axis).broadcast_to(shape)

        xs = area(0, NB, D)
        A_v = area(2048, NB, W_A)
        A_u = area(6144, 16, T)
        A_g = area(10240, 16, T)
        A_y = area(14336, 16, T)
        A_lng, A_lnb = area(18432, W_A), area(20480, W_A)
        A_ws = area(22528, 16, P)
        A_bs = area(24576, 16, P)
        hKV = area(26624, DC, T)
        B_mask = area(28672, T)
        B_bq, B_bkv = area(30720, D), area(31744, 256)
        B_sink = area(32000, 16)
        B_rope = area(32128, NB, 2, 32)
        R_decay = area(32256, 8)
        B_q = area(2048, NB, D)
        B_kv = area(4096, NB, 256)
        B_kdup = area(4608, NB, KVH, 2, DH)
        B_vz = area(5120, NB, KVH, 192)
        B_qT = area(5888, DC, T)
        B_kTe, B_kTo = area(7936, KVH, T), area(8448, KVH, T)
        B_s0 = area(8960, 16, P)
        B_s1 = area(11008, 16, T)
        B_pT0 = area(15104, 16, P)
        B_pT1 = area(17152, 16, 2, P)
        B_gT = area(21248, DC, T)
        B_yT = area(23296, DC, T)
        TMP = area(25344, 1280)
        R_qk = area(0, 16, T)
        R_tmp = area(4096, 2, 512)
        R_v = area(5120, NB, 2048)
        R_g = area(9216, 16, T)
        R_D = area(13312, RET_H, 512)
        R_s = area(15360, RET_H, NB, T)
        R_y = area(17408, NB, 2048)
        R_yT = area(21504, 16, T)
        cosT, sinT = area(28928, T), area(29184, T)
        R_diff = area(26624, 2, 512)
        R_lg = area(32264, 6, 8)
        R_invf = area(32320, 32)
        pos_i = area(26624, T).bitcast(i32)
        posc_i = area(26880, NB).bitcast(i32)
        iota_i = area(26944, P).bitcast(i32)
        M_c = area(0, NB, 768)
        M_cn = area(1536, NB, 640)
        M_cT = area(2816, 5, T)
        M_kr = area(4096, NB, 2, ROPE)
        M_krTe, M_krTo = area(4352, T), area(4608, T)
        M_qn = area(4864, MLA_H, T)
        M_qr = area(6912, NB, 512)
        M_qrT = area(7936, 4, T)
        M_kn = area(8960, MLA_H, T)
        M_v = area(11008, NB, MLA_H * P)
        M_s = area(13056, 16, T)
        M_pT = area(17152, MLA_H, 2, T)
        M_oT = area(21248, DC, T)
        M_tmp = area(23296, 1280)
        K_q = area(0, 16, T)
        K_s = area(24576, NB, 16, NKEYS)
        K_cand = area(28672, PK_H, 256)
        K_eq = area(30720, PK_H, TOPK, TOPK)
        K_yT = area(0, DC, T)
        FREE_SLABS = 44
        assert FREE_SLABS * 512 <= 24576
        hf = hot[:, :, :, :, :].rearrange("p a b c d -> p (a b c d)")
        K_top = hf[:, 0:256].rearrange("p (a b) -> p a b", a=16)
        K_iu = hf[:, 256:512].bitcast(u32).rearrange("p (a b) -> p a b", a=16)
        K_if = hf[:, 512:768].rearrange("p (a b) -> p a b", a=16)
        K_ts = hf[:, 768:896].rearrange("p (a b) -> p a b", a=8)
        K_pu = hf[:, 896:1024].bitcast(u32).rearrange("p (a b) -> p a b", a=8)
        K_au = hf[:, 1024:1152].bitcast(u32).rearrange("p (a b) -> p a b", a=8)
        K_af = hf[:, 1152:1280].rearrange("p (a b) -> p a b", a=8)
        K_sum = mx[:, 0:PK_H]
        picks = hf[:, 1280:2048].rearrange("p (b a k) -> p b a k", b=NB, a=3)

        slab_loaded = [sem(f"slab_loaded{i}") for i in range(RING)]
        slab_done = sem("slab_done")
        g_free = [sem(f"g_free{i}") for i in range(4)]
        x_full = sem("x_full")
        x_free = [sem(f"x_free{i}") for i in range(4)]
        dve_step, act_step, pool_step = sem("dve_step"), sem("act_step"), sem("pool_step")

        block = ctx.enter_context(nc.Block())

        def fours(eng, n):
            if n % 4 or n < 8:
                for j in range(n):
                    yield j, j
            else:
                with eng.Fori(0, n // 4) as it:
                    for j in range(4):
                        yield j, it * 4 + j

        def at(n, size):
            return bass.ds(n * size, size) if not isinstance(n, int) else slice(n * size, (n + 1) * size)

        def flat(ap):
            names = "abcd"[:len(ap.shape) - 1]
            return ap.rearrange(f"p {' '.join(names)} -> p ({' '.join(names)})")

        def x_tile(eng, stage, i):
            x = X0[stage] + i
            eng.wait_ge(x_full, x + 1)
            return X[x % 4], x_free[x % 4]

        def x_read(eng, stage, i=None):
            tiles = range(max(0, XTILES[stage] - 4), XTILES[stage]) if i is None else [i]
            for k in tiles:
                x = X0[stage] + k
                eng.wait_ge(x_free[x % 4], x // 4 + 1)

        def g_tile(eng, stage, j, n):
            s = SLAB0[stage] + j
            eng.wait_ge(slab_done, n + (SLAB0[stage] + 1))
            return G[s % 4], g_free[s % 4]

        def g_read(eng, stage):
            for s in range(SLAB0[stage] + max(0, SLABS[stage] - 4), SLAB0[stage] + SLABS[stage]):
                eng.wait_ge(g_free[s % 4], tiles_before(s) + 1)

        R_a = area(29440, 4, 320)

        def take_T4(stage, eng, dst, tiles):
            for i in tiles:
                tile, free = x_tile(eng, stage, i)
                to = flat(dst)[:, 512 * i:512 * (i + 1)]
                if eng is nc.scalar:
                    nc.scalar.activation(to, tile[:, :], ACT.Copy).then_inc(free, 1)
                else:
                    nc.vector.tensor_copy(to, tile[:, :]).then_inc(free, 1)

        @block.sync
        def _(sp):
            for s in range(RING):
                sp.dma_start(ring[s][:, :], slabs[s]).then_inc(slab_loaded[s], 16)
            with sp.Fori(1, N_SLABS // RING) as it:
                for j in range(RING):
                    sp.wait_ge(slab_done, it * RING + (j + 1 - RING))
                    sp.dma_start(ring[j][:, :], slabs[bass.ds(it * RING + j, 1)].rearrange("a p n -> (a p) n")
                                 ).then_inc(slab_loaded[j], 16)
            for s in range(N_SLABS // RING * RING, N_SLABS):
                sp.wait_ge(slab_done, s + 1 - RING)
                sp.dma_start(ring[s % RING][:, :], slabs[s]).then_inc(slab_loaded[s % RING], 16)
            sp.wait_ge(sem("h_ffn1"), 2)
            sp.dma_start(out.rearrange("(b p) d -> p b d", p=P), h[:, :, :]).then_inc(sem("out_stored"), 16)
            sp.wait_ge(sem("out_stored"), 16)

        @block.tensor
        def _(pe):
            def begin(s0, j, n, tile=True):
                slot = (s0 + j) % 4
                loaded = 16 * ((s0 + j) // 4 + 1)
                free = tiles_before(s0 + j)
                if isinstance(n, int):
                    pe.wait_ge(slab_loaded[slot], loaded + 4 * (n - j))
                    if tile and free + (n - j) // 4 > 0:
                        pe.wait_ge(g_free[slot], free + (n - j) // 4)
                else:
                    it = begin.it
                    pe.wait_ge(slab_loaded[slot], it * 16 + loaded)
                    if tile:
                        pe.wait_ge(g_free[slot], it + free)
                return slot

            def steps(n):
                if n % 4 or n < 8:
                    for j in range(n):
                        yield j, j
                else:
                    with pe.Fori(0, n // 4) as it:
                        begin.it = it
                        for j in range(4):
                            yield j, it

            def project_rows(stage, src, k, width, width_k=None):
                s0 = SLAB0[stage]
                first = 0
                if tiles_before(s0) == 0:
                    for j in range(4):
                        rows_slab(begin(s0, j, j), src, k, width)
                    first = 4
                if first:
                    s0 += 4
                for j, n in steps(SLABS[stage] - first):
                    rows_slab(begin(s0, j, n), src, k, width)

            def rows_slab(slot, src, k, width):
                w = ring[slot][:, 0:k * width].rearrange("p (k n) -> p k n", k=k)
                for b in range(NB):
                    for c in range(k):
                        last = nc.tensor.matmul(G[slot][:, b * width:(b + 1) * width], src[:, c, b * P:(b + 1) * P],
                                                w[:, c, :], start=(c == 0), stop=(c == k - 1))
                last.then_inc(slab_done, 1)

            def project_cols(stage, src, k):
                s0 = SLAB0[stage]
                for j, n in steps(SLABS[stage]):
                    slot = begin(s0, j, n)
                    w = ring[slot][:, 0:k * 256].rearrange("p (k n) -> p k n", k=k)
                    for a in range(2):
                        for c in range(k):
                            last = nc.tensor.matmul(G[slot][:, a * T:(a + 1) * T], w[:, c, a * P:(a + 1) * P],
                                                    src[:, c, :], start=(c == 0), stop=(c == k - 1))
                    last.then_inc(slab_done, 1)

            def x_begin(stage, i):
                x = X0[stage] + i
                if x >= 4:
                    pe.wait_ge(x_free[x % 4], x // 4)
                return X[x % 4]

            def transpose_rows(stage, src, chunks=DC):
                for i in range(XTILES[stage]):
                    tile = x_begin(stage, i)
                    for a in range(min(2, chunks - 2 * i)):
                        for b in range(NB):
                            c = 2 * i + a
                            last = nc.tensor.transpose(tile[:, a * T + b * P:a * T + (b + 1) * P],
                                                       src[:, b, c * P:(c + 1) * P], ident[:, :])
                    last.then_inc(x_full, 1)

            pe.wait_ge(sem("ident_ready"), 2)
            pe.wait_ge(sem("xs_a"), 2)
            transpose_rows("a_tr", xs)
            x_read(pe, "a_tr")
            project_rows("a_v", hT, DC, 256)
            project_cols("a_u", hT, DC)
            pe.wait_ge(sem("vn_ready"), 1)
            pe.wait_ge(sem("ws_masked"), 1)
            for i in range(8):
                tile = x_begin("a_sv", i)
                for a in range(2):
                    for b in range(NB):
                        g = 2 * i + a
                        last = nc.tensor.matmul(tile[:, a * T + b * P:a * T + (b + 1) * P],
                                                A_v[:, b, g * P:(g + 1) * P], A_ws[:, g, :], start=True, stop=True)
                last.then_inc(x_full, 1)
            project_cols("a_g", hT, DC)
            pe.wait_ge(sem("a_y_ready"), 8)
            project_rows("a_out", A_y, 16, P)

            pe.wait_ge(sem("xs_b"), 2)
            transpose_rows("b_tr", xs)
            x_read(pe, "b_tr")
            project_rows("b_kv", hKV, DC, 256)
            project_rows("b_q", hT, DC, 256)
            project_cols("b_g", hT, DC)
            pe.wait_ge(sem("k_rotated"), 1)
            tile = x_begin("b_ktr", 0)
            for g in range(KVH):
                for b in range(NB):
                    last = nc.tensor.transpose(tile[:, g * T + b * P:g * T + (b + 1) * P],
                                               B_kdup[:, b, g, :, :].rearrange("p a d -> p (a d)"), ident[:, :])
            last.then_inc(x_full, 1)
            pe.wait_ge(sem("q_rotated"), 4)
            transpose_rows("b_qtr", B_q)
            x_read(pe, "b_ktr")
            pe.wait_ge(sem("pads_zero"), 3)
            x_read(pe, "b_qtr")
            kT = [B_kTe, B_kTo]
            for i in range(4):
                tile = x_begin("b_s0", i)
                for a in range(4):
                    hd = 4 * i + a
                    last = nc.tensor.matmul(tile[:, a * P:(a + 1) * P], B_qT[:, hd // 2, 0:P],
                                            kT[hd % 2][:, hd // 8, 0:P], start=True, stop=True)
                last.then_inc(x_full, 1)
            for i in range(8):
                tile = x_begin("b_s1", i)
                for a in range(2):
                    hd = 2 * i + a
                    last = nc.tensor.matmul(tile[:, a * T:(a + 1) * T], B_qT[:, hd // 2, P:T],
                                            kT[hd % 2][:, hd // 8, :], start=True, stop=True)
                last.then_inc(x_full, 1)
            pe.wait_ge(sem("p_b0"), 1)
            for i in range(4):
                tile = x_begin("b_pt0", i)
                for a in range(4):
                    last = nc.tensor.transpose(tile[:, a * P:(a + 1) * P], B_s0[:, 4 * i + a, :], ident[:, :])
                last.then_inc(x_full, 1)
            pe.wait_ge(sem("p_b1"), 1)
            for i in range(8):
                tile = x_begin("b_pt1", i)
                for a in range(2):
                    for c in range(2):
                        last = nc.tensor.transpose(tile[:, a * T + c * P:a * T + (c + 1) * P],
                                                   B_s1[:, 2 * i + a, c * P:(c + 1) * P], ident[:, :])
                last.then_inc(x_full, 1)
            x_read(pe, "b_pt0")
            pe.wait_ge(sem("vz_ready"), 1)

            def v_of(b, hd):
                return B_vz[:, b, hd // 8, 64:192] if hd % 2 == 0 else B_vz[:, b, hd // 8, 0:128]

            for i in range(2):
                tile = x_begin("b_pv0", i)
                for a in range(4):
                    for e in range(2):
                        hd = 2 * (4 * i + a) + e
                        last = nc.tensor.matmul(tile[:, a * P:(a + 1) * P], v_of(0, hd), B_pT0[:, hd, :],
                                                start=(e == 0), stop=(e == 1))
                last.then_inc(x_full, 1)
            x_read(pe, "b_pt1")
            for i in range(2):
                tile = x_begin("b_pv1", i)
                for a in range(4):
                    for e in range(4):
                        hd, kc = 2 * (4 * i + a) + e // 2, e % 2
                        last = nc.tensor.matmul(tile[:, a * P:(a + 1) * P], v_of(kc, hd), B_pT1[:, hd, kc, :],
                                                start=(e == 0), stop=(e == 3))
                last.then_inc(x_full, 1)
            x_read(pe, "b_pv0")
            x_read(pe, "b_pv1")
            project_rows("b_out", B_yT, DC, 256)

            pe.wait_ge(sem("h_b"), 2)
            transpose_rows("r_tr", h)
            x_read(pe, "r_tr")
            project_cols("r_qk", hT, DC)
            project_rows("r_v", hT, DC, 256)
            pe.wait_ge(sem("r_qk_ready"), 8)
            for hd in range(RET_H):
                tile = x_begin("r_s", hd)
                for m in range(NB):
                    for c in range(2):
                        last = nc.tensor.matmul(tile[:, m * T:(m + 1) * T], R_qk[:, 8 + 2 * hd + c, m * P:(m + 1) * P],
                                                R_qk[:, 2 * hd + c, :], start=(c == 0), stop=(c == 1))
                last.then_inc(x_full, 1)
            g_read(pe, "r_v")
            for i in range(8):
                hd, b = i // 2, i % 2
                if b == 0:
                    x_read(pe, "r_s", hd)
                tile = x_begin("r_y", i)
                for m in range(NB):
                    last = nc.tensor.matmul(tile[:, :], R_s[:, hd, m, b * P:(b + 1) * P],
                                            R_v[:, m, hd * RET_DV:(hd + 1) * RET_DV], start=(m == 0), stop=(m == 1))
                last.then_inc(x_full, 1)
            project_cols("r_g", hT, DC)
            pe.wait_ge(sem("r_yn_ready"), 1)
            transpose_rows("r_yt", R_y, 16)
            pe.wait_ge(sem("r_y_ready"), 8)
            project_rows("r_out", R_yT, 16, P)

            def experts(l):
                pe.wait_ge(sem(f"h_mix{l}"), 2)
                transpose_rows(f"p_tr{l}", h)
                x_read(pe, f"p_tr{l}")
                project_cols(f"pq{l}", hT, DC)
                pe.wait_ge(sem(f"keys_loaded{l}"), 16)
                g_read(pe, f"pq{l}")
                for i in range(8):
                    tile = x_begin(f"p_s{l}", i)
                    for a in range(4):
                        hc = 4 * (i % 4) + a
                        last = nc.tensor.matmul(tile[:, a * P:(a + 1) * P], K_q[:, hc, (i // 4) * P:(i // 4 + 1) * P],
                                                keysT[:, hc, :], start=True, stop=True)
                    last.then_inc(x_full, 1)
                project_cols(f"u{l}", hT, DC)
                for b in range(NB):
                    pe.wait_ge(sem(f"picks{l}"), b + 1)
                    tile = x_begin(f"p_kt{l}", b)
                    for a in range(3):
                        last = nc.tensor.transpose(tile[:, a * P:(a + 1) * P], picks[:, b, a, :], ident[:, :])
                    last.then_inc(x_full, 1)
                w0 = X0[f"p_w{l}"]
                with pe.Fori(0, 16) as it:
                    for j in range(4):
                        x = w0 + j
                        pe.wait_ge(x_free[x % 4], it + x // 4)
                        pe.wait_ge(sem(f"hot1_{l}"), it * 4 + (j + 1))
                        pe.wait_ge(sem(f"hot2_{l}"), it * 4 + (j + 1))
                        for q in range(4):
                            last = nc.tensor.matmul(X[x % 4][:, q * P:(q + 1) * P], hot[:, 1, j % 2, q, :],
                                                    hot[:, 0, j % 2, q, :], start=True, stop=True)
                        last.then_inc(x_full, 1)
                s0, y0 = SLAB0[f"v{l}"], X0[f"p_y{l}"]
                for i in range(4):
                    pe.wait_ge(x_free[(y0 + i) % 4], (y0 + i) // 4)

                def v_slab(slot, g, first, final):
                    for a in range(2):
                        for c in range(DC):
                            last = nc.tensor.matmul(
                                X[(y0 + c // 2) % 4][:, (c % 2) * T:(c % 2 + 1) * T],
                                ring[slot][:, a * D + c * P:a * D + (c + 1) * P],
                                big[:, bass.ds(g * 512 + a * T, T)],
                                start=(first and a == 0 and c % 2 == 0), stop=(final and a == 1),
                                skip_group_check=True)
                            if final and a == 1 and c % 2:
                                last.then_inc(x_full, 1)
                    return last

                for j in range(4):
                    v_slab(begin(s0, j, j, False), j, j == 0, False).then_inc(slab_done, 1)
                with pe.Fori(0, 14) as it:
                    begin.it = it
                    for j in range(4):
                        v_slab(begin(s0 + 4, j, it, False), it * 4 + (j + 4), False, False).then_inc(slab_done, 1)
                for j in range(4):
                    last = v_slab(begin(s0 + 60, j, j, False), 60 + j, False, j == 3)
                    if j < 3:
                        last.then_inc(slab_done, 1)
                pe.wait_ge(x_full, y0 + 4)
                pe.sem_inc(slab_done, 1)
                x_read(pe, f"p_y{l}")
                for i in range(4):
                    tile = x_begin(f"p_yr{l}", i)
                    for a in range(4):
                        c = 4 * (i % 2) + a
                        last = nc.tensor.transpose(tile[:, a * P:(a + 1) * P],
                                                   K_yT[:, c, (i // 2) * P:(i // 2 + 1) * P], ident[:, :])
                    last.then_inc(x_full, 1)

            experts(0)

            pe.wait_ge(sem("h_ffn0"), 2)
            transpose_rows("m_tr", h)
            x_read(pe, "m_tr")
            project_rows("m_in", hT, DC, 256)
            pe.wait_ge(sem("cn_ready"), 1)
            transpose_rows("m_ct", M_cn, 5)
            pe.wait_ge(sem("kr_rotated"), 1)
            tile = x_begin("m_krt", 0)
            for b in range(NB):
                last = nc.tensor.transpose(tile[:, b * P:(b + 1) * P],
                                           M_kr[:, b, :, :].rearrange("p a d -> p (a d)"), ident[:, :])
            last.then_inc(x_full, 1)
            x_read(pe, "m_ct")
            project_cols("m_qn", M_cT, 3)
            project_rows("m_qr", M_cT, 3, 256)
            s0 = SLAB0["m_kv"]
            for j, n in steps(8):
                slot = begin(s0, j, n)
                w = ring[slot][:, 0:512].rearrange("p (k n) -> p k n", k=2)
                for c in range(2):
                    nc.tensor.matmul(G[slot][:, 0:T], w[:, c, 0:P], M_cT[:, 3 + c, :], start=(c == 0), stop=(c == 1))
                for b in range(NB):
                    for c in range(2):
                        last = nc.tensor.matmul(G[slot][:, T + b * P:T + (b + 1) * P],
                                                M_cT[:, 3 + c, b * P:(b + 1) * P], w[:, c, P:2 * P],
                                                start=(c == 0), stop=(c == 1))
                last.then_inc(slab_done, 1)
            pe.wait_ge(sem("mq_rotated"), 2)
            transpose_rows("m_qrt", M_qr, 4)
            x_read(pe, "m_krt")
            pe.wait_ge(sem("pads_zero"), 5)
            g_read(pe, "m_qn")
            g_read(pe, "m_kv")
            x_read(pe, "m_qrt")
            krT = [M_krTe, M_krTo]
            for hd in range(MLA_H):
                tile = x_begin("m_s", hd)
                for b in range(NB):
                    o = tile[:, b * T:(b + 1) * T]
                    nc.tensor.matmul(o, M_qn[:, hd, b * P:(b + 1) * P], M_kn[:, hd, :], start=True, stop=False)
                    last = nc.tensor.matmul(o, M_qrT[:, hd // 2, b * P:(b + 1) * P], krT[hd % 2], start=False, stop=True)
                last.then_inc(x_full, 1)
            pe.wait_ge(sem("p_m"), 1)
            for hd in range(MLA_H):
                tile = x_begin("m_pt", hd)
                for kc in range(2):
                    for b in range(NB):
                        last = nc.tensor.transpose(tile[:, kc * T + b * P:kc * T + (b + 1) * P],
                                                   M_s[:, 2 * hd + b, kc * P:(kc + 1) * P], ident[:, :])
                last.then_inc(x_full, 1)
            x_read(pe, "m_pt")
            for i in range(4):
                tile = x_begin("m_pv", i)
                for a in range(2):
                    hd = 2 * i + a
                    for kc in range(2):
                        last = nc.tensor.matmul(tile[:, a * T:(a + 1) * T], M_v[:, kc, hd * P:(hd + 1) * P],
                                                M_pT[:, hd, kc, :], start=(kc == 0), stop=(kc == 1))
                last.then_inc(x_full, 1)
            x_read(pe, "m_pv")
            project_rows("m_out", M_oT, DC, 256)
            experts(1)

        @block.scalar
        def _(act):
            def row(dst, name):
                a = rows_in[0:1, ROW0[name]:ROW0[name] + ROWN[name]]
                act.dma_start(dst, a.broadcast_to([P, ROWN[name]])).then_inc(sem("rows_loaded"), 16)

            act.dma_start(h[:, :, :], x_in.rearrange("(b p) d -> p b d", p=P)).then_inc(sem("x_loaded"), 16)
            act.dma_start(cols[:, :], cols_in).then_inc(sem("cols_loaded"), 16)
            act.dma_start(pos_i[:, :], pos_row.broadcast_to([P, T])).then_inc(sem("pos_loaded"), 16)
            act.dma_start(posc_i[:, :], pos_col).then_inc(sem("pos_loaded"), 16)
            row(R_decay, "decay")
            row(R_invf, "invf_row")
            row(A_lng, "ln_g")
            row(A_lnb, "ln_b")
            row(flat(A_bs), "bs")
            row(B_bq, "bq")
            row(B_bkv, "bkv")
            row(B_sink, "sinks")
            act.dma_start(flat(A_ws), ws_in).then_inc(sem("ws_loaded"), 16)
            act.dma_start(B_rope, rope_in.rearrange("p (a b c) -> p a b c", a=NB, b=2)).then_inc(sem("rope_loaded"), 16)
            act.dma_start(flat(keysT[:, :, :]), keys_in[0]).then_inc(sem("keys_loaded0"), 16)

            def root(name, n):
                act.wait_ge(sem(f"var_{name}"), 1)
                nc.scalar.activation(rstd[:, 0:n], rstd[:, 0:n], ACT.Sqrt).then_inc(sem(f"std_{name}"), 1)

            def take_T(stage, dst, tiles=(0, 2), scales=None):
                for i in tiles:
                    tile, free = x_tile(act, stage, i)
                    if scales is None:
                        nc.scalar.activation(flat(dst[:, 2 * i:2 * i + 2, :]), tile[:, :], ACT.Copy).then_inc(free, 1)
                        continue
                    for a in range(min(2, dst.shape[1] - 2 * i)):
                        for to, g in scales:
                            last = nc.scalar.activation(to[:, 2 * i + a, :], tile[:, a * T:(a + 1) * T], ACT.Copy,
                                                        scale=col(g, 2 * i + a))
                    last.then_inc(free, 1)

            def take_cols(stage, dst, func=ACT.Copy, every=1):
                for j, n in fours(act, SLABS[stage]):
                    if j % every == 0:
                        tile, free = g_tile(act, stage, j, n)
                        nc.scalar.activation(flat(dst)[:, at(n, 512)], tile[:, :], func).then_inc(free, 1)

            def take_rows(stage, dst, every=1):
                for j, n in fours(act, SLABS[stage]):
                    if j % every == 0:
                        tile, free = g_tile(act, stage, j, n)
                        nc.scalar.activation(dst[:, :, at(n, 256)], tile[:, :].rearrange("p (b n) -> p b n", b=NB),
                                             ACT.Copy).then_inc(free, 1)

            def exps(name, s, sinks):
                act.wait_ge(sem(f"max_{name}"), 1)
                if sinks:
                    nc.scalar.activation(esink[:, :], esink[:, :], ACT.Exp)
                for u in range(16):
                    last = nc.scalar.activation(s[:, u, :], s[:, u, :], ACT.Exp, bias=negm[:, u:u + 1],
                                                accum_out=rsum[:, u:u + 1])
                last.then_inc(sem(f"exp_{name}"), 1)

            root("a", 2)
            act.wait_ge(sem("cols_loaded"), 16)
            take_T("a_tr", hT, scales=[(hT, "a_g")])
            act.wait_ge(sem("angles"), 1)
            nc.scalar.activation(sinT, R_a[:, 2, 0:T], ACT.Sin)
            nc.scalar.activation(cosT, R_a[:, 3, 0:T], ACT.Sin)
            nc.scalar.activation(rope_row[:, :, 1, :], R_a[:, 2, T:].rearrange("p (b f) -> p b f", b=NB), ACT.Sin)
            nc.scalar.activation(rope_row[:, :, 0, :], R_a[:, 3, T:].rearrange("p (b f) -> p b f", b=NB),
                                 ACT.Sin).then_inc(sem("rotary_ready"), 1)
            act.wait_ge(sem("rows_loaded"), 16 * 8)
            nc.scalar.activation(R_lg[:, 0, :], R_decay, ACT.Exp).then_inc(sem("decay_exp"), 1)
            act.wait_ge(sem("one_minus"), 1)
            nc.scalar.activation(R_lg[:, 2, :], R_lg[:, 1, :], ACT.Ln).then_inc(sem("decay_ln"), 1)
            take_rows("a_v", A_v, 2)
            root("vn", 2)
            take_cols("a_u", A_u, every=2)
            take_cols("a_g", A_g, ACT.Silu)

            root("b", 2)
            take_T("b_tr", hT, scales=[(hT, "b_g"), (hKV, "kv_g")])
            take_cols("b_g", B_gT, ACT.Silu)
            tile, free = x_tile(act, "b_ktr", 0)
            act.wait_ge(sem("pads_zero"), 2)
            nc.scalar.activation(flat(B_kTe)[0:64, :], tile[0:64, :], ACT.Copy)
            nc.scalar.activation(flat(B_kTo)[64:128, :], tile[64:128, :], ACT.Copy).then_inc(free, 1)
            take_T("b_qtr", B_qT)
            exps("b0", B_s0, True)
            take_T4("b_pt0", act, B_pT0, (0, 2))
            exps("b1", B_s1, True)
            take_T4("b_pt1", act, B_pT1, (0, 2, 4, 6))
            root("fin", 2)

            take_T("r_tr", hT)
            for i in range(RET_H):
                act.wait_ge(sem("decay_arg"), i + 1)
                nc.scalar.activation(R_D[:, i, :], R_D[:, i, :], ACT.Exp).then_inc(sem("decay_ready"), 1)
            take_rows("r_v", R_v)
            for i in range(8):
                tile, free = x_tile(act, "r_y", i)
                nc.scalar.activation(R_y[:, i % 2, (i // 2) * RET_DV:(i // 2 + 1) * RET_DV], tile[:, :],
                                     ACT.Copy).then_inc(free, 1)
            root("gn", 8)
            take_cols("r_g", R_g, ACT.Silu)
            root("mix0", 2)

            def experts(l):
                take_T(f"p_tr{l}", hT)
                take_cols(f"pq{l}", K_q)
                for i in range(8):
                    tile, free = x_tile(act, f"p_s{l}", i)
                    nc.scalar.activation(flat(K_s[:, i // 4, 4 * (i % 4):4 * (i % 4) + 4, :]), tile[:, :],
                                         ACT.Copy).then_inc(free, 1)

                def gelus(first, n):
                    with act.Fori(first // 4, (first + n) // 4) as it:
                        for j in range(4):
                            tile, free = g_tile(act, f"u{l}", j, it * 4 + j)
                            nc.scalar.activation(big[:, bass.ds(it * 2048 + j * 512, 512)], tile[:, :],
                                                 ACT.Gelu).then_inc(free, 1)

                gelus(0, FREE_SLABS)
                for b in range(NB):
                    act.wait_ge(sem(f"top{l}"), b + 1)
                    nc.scalar.activation(picks[:, b, 2, :], picks[:, b, 2, :], ACT.Exp).then_inc(sem(f"gates{l}"), 1)
                gelus(FREE_SLABS, 64 - FREE_SLABS)
                take_T(f"p_y{l}", K_yT)
                root(f"ffn{l}", 2)

            experts(0)

            take_T("m_tr", hT)
            take_rows("m_in", M_c)
            root("cn", 4)
            take_T("m_ct", M_cT, (0, 1, 2), [(M_cT, "m_qg")])
            tile, free = x_tile(act, "m_krt", 0)
            act.wait_ge(sem("pads_zero"), 5)
            nc.scalar.activation(M_krTe[0:64, :], tile[0:64, 0:T], ACT.Copy)
            nc.scalar.activation(M_krTo[64:128, :], tile[64:128, 0:T], ACT.Copy).then_inc(free, 1)
            take_cols("m_qn", M_qn)
            for j, n in fours(act, 8):
                tile, free = g_tile(act, "m_kv", j, n)
                nc.scalar.activation(flat(M_kn)[:, at(n, T)], tile[:, 0:T], ACT.Copy)
                nc.scalar.activation(M_v[:, :, at(n, P)], tile[:, T:].rearrange("p (b n) -> p b n", b=NB),
                                     ACT.Copy).then_inc(free, 1)
            for i in range(8):
                tile, free = x_tile(act, "m_s", i)
                nc.scalar.activation(flat(M_s[:, 2 * i:2 * i + 2, :]), tile[:, :], ACT.Copy,
                                     scale=float(P + ROPE) ** -0.5).then_inc(free, 1)
            exps("m", M_s, False)
            take_T4("m_pt", act, M_pT, (0, 2, 4, 6))
            take_T("m_pv", M_oT)
            root("mix1", 2)
            experts(1)

        @block.vector
        def _(dve):
            taken = [0]

            def link(ins):
                taken[0] += 1
                ins.then_inc(dve_step, 1)
                dve.wait_ge(dve_step, taken[0])

            V = nc.vector

            def stats(name, rows, centered):
                k = 0
                parts = []
                for r in rows:
                    n = r.shape[1]
                    m = -(-n // 512)
                    for q in range(m):
                        last = V.bn_stats(st[:, k + q, :], r[:, q * (n // m):(q + 1) * (n // m)])
                    parts.append((k, m))
                    k += m
                link(last)
                for i, (k, m) in enumerate(parts):
                    last = V.bn_aggr(mv[:, i, :], st[:, k:k + m, :].rearrange("p a b -> p (a b)"))
                link(last)
                n = len(rows)
                if centered:
                    V.tensor_scalar(rstd[:, 0:n], mv[:, 0:n, 1], EPS, None, ALU.add).then_inc(sem(f"var_{name}"), 1)
                else:
                    link(V.tensor_tensor(rstd[:, 0:n], mv[:, 0:n, 0], mv[:, 0:n, 0], ALU.mult))
                    V.scalar_tensor_tensor(rstd[:, 0:n], rstd[:, 0:n], EPS, mv[:, 0:n, 1], ALU.add,
                                           ALU.add).then_inc(sem(f"var_{name}"), 1)
                dve.wait_ge(sem(f"std_{name}"), 1)
                link(V.reciprocal(rstd[:, 0:n], rstd[:, 0:n]))

            def layer_norm(name, count):
                stats(name, [h[:, b, :] for b in range(NB)], True)
                for b in range(NB):
                    last = V.tensor_scalar(h[:, b, :], h[:, b, :], mv[:, b, 0:1], rstd[:, b:b + 1], ALU.subtract, ALU.mult)
                link(last)
                dve.wait_ge(sem("lnw_loaded"), 16 * count)
                for b in range(NB):
                    last = V.tensor_tensor(h[:, b, :], h[:, b, :], lnw[:, 0, :], ALU.mult)
                link(last)
                for b in range(NB):
                    V.tensor_tensor(h[:, b, :], h[:, b, :], lnw[:, 1, :], ALU.add).then_inc(sem(f"h_{name}"), 1)
                dve.wait_ge(sem(f"h_{name}"), NB)
                dve.sem_inc(sem("lnw_used"), 1)

            def normed(name, dst, src):
                for b in range(NB):
                    V.tensor_scalar(dst[:, b, :], src[:, b, :], rstd[:, b:b + 1], None, ALU.mult).then_inc(sem(name), 1)

            def take_T(stage, dst, tiles=(1, 3), scales=None):
                for i in tiles:
                    tile, free = x_tile(dve, stage, i)
                    if scales is None:
                        V.tensor_copy(flat(dst[:, 2 * i:2 * i + 2, :]), tile[:, :]).then_inc(free, 1)
                        continue
                    for a in range(2):
                        for to, g in scales:
                            last = V.tensor_scalar(to[:, 2 * i + a, :], tile[:, a * T:(a + 1) * T], col(g, 2 * i + a),
                                                   None, ALU.mult)
                    last.then_inc(free, 1)

            def rotate(x, n, table, tmp, done):
                t = [tmp[:, q * (NB * n * 32):(q + 1) * (NB * n * 32)].rearrange("p (b n f) -> p b n f", b=NB, n=n)
                     for q in range(4)]
                x1, x2 = x[:, :, :, 0:32], x[:, :, :, 32:64]
                cos, sin = bc(table[:, :, 0, :], 2, n), bc(table[:, :, 1, :], 2, n)
                V.tensor_tensor(t[0], x1, cos, ALU.mult)
                V.tensor_tensor(t[1], x2, sin, ALU.mult)
                V.tensor_tensor(t[2], x2, cos, ALU.mult)
                link(V.tensor_tensor(t[3], x1, sin, ALU.mult))
                V.tensor_tensor(x1, t[0], t[1], ALU.subtract)
                V.tensor_tensor(x2, t[2], t[3], ALU.add).then_inc(done, 1)

            def softmax(name, s, sinks):
                link(V.tensor_reduce(mx[:, :], s, AX.X, ALU.max))
                if sinks:
                    link(V.tensor_tensor(mx[:, :], mx[:, :], B_sink, ALU.max))
                    V.tensor_tensor(esink[:, :], B_sink, mx[:, :], ALU.subtract)
                V.tensor_scalar(negm[:, :], mx[:, :], -1.0, None, ALU.mult).then_inc(sem(f"max_{name}"), 1)
                dve.wait_ge(sem(f"exp_{name}"), 1)
                if sinks:
                    link(V.tensor_tensor(rsum[:, :], rsum[:, :], esink[:, :], ALU.add))
                link(V.reciprocal(rden[:, :], rsum[:, :]))
                for u in range(16):
                    last = V.tensor_scalar(s[:, u, :], s[:, u, :], rden[:, u:u + 1], None, ALU.mult)
                last.then_inc(sem(f"p_{name}"), 1)

            dve.wait_ge(sem("x_loaded"), 16)
            stats("a", [h[:, b, :] for b in range(NB)], False)
            normed("xs_a", xs, h)
            dve.wait_ge(sem("cols_loaded"), 16)
            take_T("a_tr", hT, scales=[(hT, "a_g")])
            dve.wait_ge(sem("pos_loaded"), 32)
            dve.wait_ge(sem("rows_loaded"), 16 * 8)
            V.tensor_copy(R_a[:, 1, 0:T], pos_i[:, :])
            link(V.tensor_copy(mx[:, 0:NB], posc_i[:, :]))
            V.tensor_scalar(R_a[:, 0, 0:T], R_a[:, 1, 0:T], col("invf", 0), None, ALU.mult)
            for b in range(NB):
                last = V.tensor_scalar(R_a[:, 0, T + 32 * b:T + 32 * b + 32], R_invf, mx[:, b:b + 1], None, ALU.mult)
            link(last)
            link(V.tensor_scalar(R_a[:, 1, :], R_a[:, 0, :], 1.0 / (2 * np.pi), 12582912.0, ALU.mult, ALU.add))
            link(V.tensor_scalar(R_a[:, 1, :], R_a[:, 1, :], 12582912.0, None, ALU.subtract))
            src = 0
            for part in (6.28125, 0.0019350051879882812, 3.019916050561733e-07):
                link(V.scalar_tensor_tensor(R_a[:, 2, :], R_a[:, 1, :], -part, R_a[:, src, :], ALU.mult, ALU.add))
                src = 2
            link(V.tensor_scalar(R_a[:, 3, :], R_a[:, 2, :], np.pi / 2, None, ALU.add))
            link(V.tensor_scalar(R_a[:, 1, :], R_a[:, 3, :], np.pi, -2 * np.pi, ALU.is_gt, ALU.mult))
            link(V.tensor_tensor(R_a[:, 3, :], R_a[:, 3, :], R_a[:, 1, :], ALU.add))
            V.tensor_scalar(R_a[:, 2:4, :], R_a[:, 2:4, :], 3.1415925, -3.1415925, ALU.min, ALU.max
                            ).then_inc(sem("angles"), 1)
            dve.wait_ge(sem("decay_exp"), 1)
            V.tensor_scalar(R_lg[:, 1, :], R_lg[:, 0, :], -1.0, 1.0, ALU.mult, ALU.add).then_inc(sem("one_minus"), 1)
            dve.wait_ge(sem("one_minus"), 1)
            link(V.tensor_scalar(R_lg[:, 3, :], R_lg[:, 1, :], -1.0, None, ALU.add))
            link(V.tensor_scalar(R_lg[:, 4, :], R_lg[:, 3, :], 0.0, None, ALU.is_equal))
            link(V.tensor_tensor(R_lg[:, 3, :], R_lg[:, 3, :], R_lg[:, 4, :], ALU.add))
            link(V.reciprocal(R_lg[:, 5, :], R_lg[:, 3, :]))
            dve.wait_ge(sem("decay_ln"), 1)
            link(V.tensor_tensor(R_lg[:, 5, :], R_lg[:, 5, :], R_lg[:, 2, :], ALU.mult))
            link(V.tensor_tensor(R_lg[:, 5, :], R_lg[:, 5, :], R_lg[:, 4, :], ALU.add))
            link(V.scalar_tensor_tensor(R_lg[:, 5, :], R_lg[:, 0, :], -1.0, R_lg[:, 5, :], ALU.mult, ALU.mult))

            for j, n in fours(dve, 8):
                if j % 2:
                    tile, free = g_tile(dve, "a_v", j, n)
                    V.tensor_copy(A_v[:, :, at(n, 256)], tile[:, :].rearrange("p (b n) -> p b n", b=NB)).then_inc(free, 1)
            g_read(dve, "a_v")
            stats("vn", [A_v[:, b, :] for b in range(NB)], True)
            for b in range(NB):
                last = V.tensor_scalar(A_v[:, b, :], A_v[:, b, :], mv[:, b, 0:1], rstd[:, b:b + 1], ALU.subtract, ALU.mult)
            link(last)
            for b in range(NB):
                last = V.tensor_tensor(A_v[:, b, :], A_v[:, b, :], A_lng, ALU.mult)
            link(last)
            for b in range(NB):
                last = V.tensor_tensor(A_v[:, b, :], A_v[:, b, :], A_lnb, ALU.add)
            last.then_inc(sem("vn_ready"), 1)
            for j, n in fours(dve, 8):
                if j % 2:
                    tile, free = g_tile(dve, "a_u", j, n)
                    V.tensor_copy(flat(A_u)[:, at(n, 512)], tile[:, :]).then_inc(free, 1)
            g_read(dve, "a_u")
            for i in range(8):
                tile, free = x_tile(dve, "a_sv", i)
                y = A_y[:, 2 * i:2 * i + 2, :].rearrange("p a (b t) -> p a b t", b=NB)
                V.tensor_tensor(y, tile[:, :].rearrange("p (a b t) -> p a b t", a=2, b=NB),
                                bc(A_bs[:, 2 * i:2 * i + 2, :], 2, NB), ALU.add).then_inc(free, 1)
                x_read(dve, "a_sv", i)
                last = V.tensor_tensor(flat(A_y[:, 2 * i:2 * i + 2, :]), flat(A_y[:, 2 * i:2 * i + 2, :]),
                                       flat(A_u[:, 2 * i:2 * i + 2, :]), ALU.mult)
            link(last)
            for i in range(8):
                s = SLAB0["a_g"] + i
                dve.wait_ge(g_free[s % 4], tiles_before(s) + 1)
                V.tensor_tensor(flat(A_y[:, 2 * i:2 * i + 2, :]), flat(A_y[:, 2 * i:2 * i + 2, :]),
                                flat(A_g[:, 2 * i:2 * i + 2, :]), ALU.mult).then_inc(sem("a_y_ready"), 1)

            def add_out(stage, width, alpha):
                for j, n in fours(dve, SLABS[stage]):
                    tile, free = g_tile(dve, stage, j, n)
                    V.scalar_tensor_tensor(h[:, :, at(n, width)], h[:, :, at(n, width)], alpha,
                                           tile[:, 0:NB * width].rearrange("p (b n) -> p b n", b=NB),
                                           ALU.mult, ALU.add).then_inc(free, 1)
                g_read(dve, stage)

            add_out("a_out", P, 1.0)

            stats("b", [h[:, b, :] for b in range(NB)], False)
            normed("xs_b", xs, h)
            take_T("b_tr", hT, scales=[(hT, "b_g"), (hKV, "kv_g")])
            tile, free = g_tile(dve, "b_kv", 0, 0)
            V.tensor_tensor(B_kv, tile[:, :].rearrange("p (b n) -> p b n", b=NB), bc(B_bkv, 1, NB),
                            ALU.add).then_inc(free, 1)
            g_read(dve, "b_kv")
            dve.wait_ge(sem("rope_loaded"), 16)
            k4 = B_kv[:, :, 0:P].rearrange("p b (g d) -> p b g d", g=KVH)
            rotate(k4, KVH, B_rope, TMP, sem("k_rot"))
            dve.wait_ge(sem("k_rot"), 1)
            for a in range(2):
                last = V.tensor_copy(B_kdup[:, :, :, a, :], k4)
            last.then_inc(sem("k_rotated"), 1)
            dve.wait_ge(sem("pads_zero"), 3)
            V.tensor_copy(B_vz[:, :, :, 64:128], B_kv[:, :, P:2 * P].rearrange("p b (g d) -> p b g d", g=KVH)
                          ).then_inc(sem("vz_ready"), 1)
            for i in range(4):
                tile, free = g_tile(dve, "b_q", i, i)
                link(V.tensor_tensor(B_q[:, :, i * 256:(i + 1) * 256], tile[:, :].rearrange("p (b n) -> p b n", b=NB),
                                     bc(B_bq[:, i * 256:(i + 1) * 256], 1, NB), ALU.add))
                dve.sem_inc(free, 1)
                rotate(B_q[:, :, i * 256:(i + 1) * 256].rearrange("p b (n d) -> p b n d", n=4), 4, B_rope, TMP,
                       sem("q_rotated"))
                dve.wait_ge(sem("q_rotated"), i + 1)
            take_T("b_qtr", B_qT)
            dve.wait_ge(sem("b_mask_ready"), 1)
            for i in range(4):
                tile, free = x_tile(dve, "b_s0", i)
                V.scalar_tensor_tensor(B_s0[:, 4 * i:4 * i + 4, :], tile[:, :].rearrange("p (a k) -> p a k", a=4),
                                       DH ** -0.5, bc(B_mask[:, P:], 1, 4), ALU.mult, ALU.add).then_inc(free, 1)
            for i in range(8):
                tile, free = x_tile(dve, "b_s1", i)
                V.scalar_tensor_tensor(B_s1[:, 2 * i:2 * i + 2, :], tile[:, :].rearrange("p (a k) -> p a k", a=2),
                                       DH ** -0.5, bc(B_mask, 1, 2), ALU.mult, ALU.add).then_inc(free, 1)
            x_read(dve, "b_s1")
            softmax("b0", B_s0, True)
            take_T4("b_pt0", dve, B_pT0, (1, 3))
            softmax("b1", B_s1, True)
            take_T4("b_pt1", dve, B_pT1, (1, 3, 5, 7))
            g_read(dve, "b_g")
            for b in range(NB):
                for i in range(2):
                    tile, free = x_tile(dve, f"b_pv{b}", i)
                    V.tensor_tensor(B_yT[:, 4 * i:4 * i + 4, b * P:(b + 1) * P],
                                    tile[:, :].rearrange("p (a t) -> p a t", a=4),
                                    B_gT[:, 4 * i:4 * i + 4, b * P:(b + 1) * P], ALU.mult).then_inc(free, 1)
            add_out("b_out", 256, 1.0)
            stats("fin", [h[:, b, :] for b in range(NB)], False)
            dve.wait_ge(sem("lnw_loaded"), 16)
            for b in range(NB):
                V.scalar_tensor_tensor(h[:, b, :], h[:, b, :], rstd[:, b:b + 1], lnw[:, 0, :], ALU.mult,
                                       ALU.mult).then_inc(sem("h_b"), 1)
            dve.wait_ge(sem("h_b"), 2)
            dve.sem_inc(sem("lnw_used"), 1)

            take_T("r_tr", hT)
            dve.wait_ge(sem("diff_loaded"), 16)
            for i in range(RET_H):
                link(V.tensor_scalar(R_D[:, i, :], R_diff[:, 0, :], R_lg[:, 5, i:i + 1], None, ALU.mult))
                V.scalar_tensor_tensor(R_D[:, i, :], R_diff[:, 1, :], R_lg[:, 5, 4 + i:5 + i], R_D[:, i, :], ALU.mult,
                                       ALU.add).then_inc(sem("decay_arg"), 1)
            dve.wait_ge(sem("rotary_ready"), 1)
            for i in range(8):
                tile, free = g_tile(dve, "r_qk", i, i)
                halves = tile[:, :].rearrange("p (a t) -> p a t", a=2)
                V.tensor_tensor(R_tmp[:, 0, :].rearrange("p (a t) -> p a t", a=2), halves, bc(cosT, 1, 2), ALU.mult)
                V.tensor_tensor(R_tmp[:, 1, :].rearrange("p (a t) -> p a t", a=2), halves, bc(sinT, 1, 2),
                                ALU.mult).then_inc(free, 1)
                s = SLAB0["r_qk"] + i
                dve.wait_ge(free, tiles_before(s) + 1)
                V.tensor_tensor(R_qk[:, 2 * i, :], R_tmp[:, 0, 0:T], R_tmp[:, 1, T:], ALU.subtract)
                link(V.tensor_tensor(R_qk[:, 2 * i + 1, :], R_tmp[:, 0, T:], R_tmp[:, 1, 0:T], ALU.add))
            dve.sem_inc(sem("r_qk_ready"), 8)
            for i in range(RET_H):
                tile, free = x_tile(dve, "r_s", i)
                dve.wait_ge(sem("decay_ready"), i + 1)
                V.scalar_tensor_tensor(flat(R_s[:, i, :, :]), tile[:, :], RET_DK ** -0.5, R_D[:, i, :], ALU.mult,
                                       ALU.mult).then_inc(free, 1)
            x_read(dve, "r_y")
            groups = [R_y[:, i % 2, (i // 2) * RET_DV:(i // 2 + 1) * RET_DV] for i in range(8)]
            stats("gn", groups, True)
            for i, g in enumerate(groups):
                last = V.tensor_scalar(g, g, mv[:, i, 0:1], rstd[:, i:i + 1], ALU.subtract, ALU.mult)
            last.then_inc(sem("r_yn_ready"), 1)
            g_read(dve, "r_g")
            for i in range(8):
                tile, free = x_tile(dve, "r_yt", i)
                for a in range(2):
                    c = 2 * i + a
                    last = V.tensor_scalar(R_yT[:, c, :], tile[:, a * T:(a + 1) * T], col("gn_g", c), col("gn_b", c),
                                           ALU.mult, ALU.add)
                last.then_inc(free, 1)
                x_read(dve, "r_yt", i)
                V.tensor_tensor(flat(R_yT[:, 2 * i:2 * i + 2, :]), flat(R_yT[:, 2 * i:2 * i + 2, :]),
                                flat(R_g[:, 2 * i:2 * i + 2, :]), ALU.mult).then_inc(sem("r_y_ready"), 1)
            add_out("r_out", P, ALPHA)
            layer_norm("mix0", 3)

            def top16(src, best, index):
                n = len(src)
                for k in range(2):
                    for i in range(n):
                        last = V.max(best[:, i, 8 * k:8 * k + 8], src[i])
                    link(last)
                    for i in range(n):
                        last = V.max_index(index[:, i, 8 * k:8 * k + 8], best[:, i, 8 * k:8 * k + 8], src[i])
                    link(last)
                    if k == 0:
                        for i in range(n):
                            last = V.match_replace(src[i], best[:, i, 0:8], src[i], LOWEST)
                        link(last)

            def experts(l):
                take_T(f"p_tr{l}", hT)
                for b in range(NB):
                    for i in range(4):
                        x_read(dve, f"p_s{l}", 4 * b + i)
                    top16([K_s[:, b, i, :] for i in range(16)], K_top, K_iu)
                    V.tensor_copy(K_if, K_iu)
                    tops = K_top.rearrange("p (n c) k -> p n c k", c=2)
                    link(V.tensor_tensor(K_cand.rearrange("p n (a b) -> p n a b", a=16), bc(tops[:, :, 0, :], 3, 16),
                                         bc(tops[:, :, 1, :], 2, 16), ALU.add))
                    top16([K_cand[:, i, :] for i in range(PK_H)], K_ts, K_pu)
                    index = K_if.rearrange("p (n c) k -> p n c k", c=2)
                    for c, (op, amount) in enumerate([(ALU.logical_shift_right, 4), (ALU.bitwise_and, 15)]):
                        link(V.tensor_scalar(K_au, K_pu, amount, None, op))
                        link(V.tensor_copy(K_af, K_au))
                        link(V.tensor_tensor(K_eq, bc(K_af, 3, 16), bc(bc(iota[:, 0:16], 1, 16), 1, PK_H), ALU.is_equal))
                        link(V.tensor_tensor(K_eq, K_eq, bc(index[:, :, c, :], 2, 16), ALU.mult))
                        link(V.tensor_reduce(picks[:, b, c, :].rearrange("p (n k) -> p n k", k=TOPK), K_eq, AX.X, ALU.add))
                    gate = picks[:, b, 2, :].rearrange("p (n k) -> p n k", k=TOPK)
                    V.tensor_tensor(gate, K_ts, K_ts[:, :, 0:1].broadcast_to([P, PK_H, TOPK]), ALU.subtract
                                    ).then_inc(sem(f"top{l}"), 1)
                    dve.wait_ge(sem(f"top{l}"), b + 1)
                for b in range(NB):
                    gate = picks[:, b, 2, :].rearrange("p (n k) -> p n k", k=TOPK)
                    dve.wait_ge(sem(f"gates{l}"), b + 1)
                    link(V.tensor_reduce(K_sum, gate, AX.X, ALU.add))
                    link(V.reciprocal(K_sum, K_sum))
                    V.tensor_tensor(gate, gate, bc(K_sum, 2, TOPK), ALU.mult).then_inc(sem(f"picks{l}"), 1)
                    dve.wait_ge(sem(f"picks{l}"), b + 1)
                for b in range(NB):
                    tile, free = x_tile(dve, f"p_kt{l}", b)
                    V.tensor_copy(picksT[:, :, b * P:(b + 1) * P], tile[:, 0:3 * P].rearrange("p (a t) -> p a t", a=3)
                                  ).then_inc(free, 1)
                x_read(dve, f"p_kt{l}")
                g_read(dve, f"u{l}")
                w0 = X0[f"p_w{l}"]
                experts_by_token = big[:, :].rearrange("p (i t) -> p i t", t=T)

                def hot2(buf, token):
                    for q in range(4):
                        t = bass.ds(token + q, 1) if not isinstance(token, int) else slice(token + q, token + q + 1)
                        last = V.tensor_scalar(hot[:, 1, buf, q, :], iota[:, :], picksT[:, 1, t], picksT[:, 2, t],
                                               ALU.is_equal, ALU.mult)
                    last.then_inc(sem(f"hot2_{l}"), 1)

                def gate_group(x, token, rounds):
                    t = bass.ds(token, 4) if not isinstance(token, int) else slice(token, token + 4)
                    dve.wait_ge(x_full, rounds + (x + 1))
                    V.tensor_tensor(experts_by_token[:, :, t], X[x % 4][:, :].rearrange("p (q i) -> p i q", q=4),
                                    experts_by_token[:, :, t], ALU.mult).then_inc(x_free[x % 4], 1)

                hot2(0, 0)
                hot2(1, 4)
                with dve.Fori(0, 15) as it:
                    for j in range(4):
                        gate_group(w0 + j, it * 16 + 4 * j, it * 4)
                        hot2(j % 2, it * 16 + (4 * j + 8))
                for j in range(4):
                    gate_group(w0 + 60 + j, 240 + 4 * j, 0)
                    if j < 2:
                        hot2(j % 2, 240 + 4 * j + 8)
                take_T(f"p_y{l}", K_yT)
                for i in range(4):
                    tile, free = x_tile(dve, f"p_yr{l}", i)
                    part = h[:, i // 2, (i % 2) * 512:(i % 2 + 1) * 512]
                    V.scalar_tensor_tensor(part, part, ALPHA, tile[:, :], ALU.mult, ALU.add).then_inc(free, 1)
                x_read(dve, f"p_yr{l}")
                layer_norm(f"ffn{l}", 5 if l == 0 else 9)

            experts(0)

            take_T("m_tr", hT)
            g_read(dve, "m_in")
            latents = [M_c[:, b, a:z] for a, z in ((0, Q_RANK), (Q_RANK, Q_RANK + KV_RANK)) for b in range(NB)]
            stats("cn", latents, False)
            for i, (a, z) in enumerate(((0, Q_RANK), (Q_RANK, Q_RANK + KV_RANK))):
                for b in range(NB):
                    last = V.tensor_scalar(M_cn[:, b, a:z], M_c[:, b, a:z], rstd[:, 2 * i + b:2 * i + b + 1], None,
                                           ALU.mult)
            last.then_inc(sem("cn_ready"), 1)
            kr = M_c[:, :, 640:704].unsqueeze(2)
            rotate(kr, 1, rope_row, M_tmp, sem("kr_rot"))
            dve.wait_ge(sem("kr_rot"), 1)
            for a in range(2):
                last = V.tensor_copy(M_kr[:, :, a, :], M_c[:, :, 640:704])
            last.then_inc(sem("kr_rotated"), 1)
            for i in range(2):
                tile, free = g_tile(dve, "m_qr", i, i)
                link(V.tensor_copy(M_qr[:, :, i * 256:(i + 1) * 256], tile[:, :].rearrange("p (b n) -> p b n", b=NB)))
                dve.sem_inc(free, 1)
                rotate(M_qr[:, :, i * 256:(i + 1) * 256].rearrange("p b (n d) -> p b n d", n=4), 4, rope_row, M_tmp,
                       sem("mq_rotated"))
                dve.wait_ge(sem("mq_rotated"), i + 1)
            take_T("m_qrt", M_qrT, (0, 1))
            x_read(dve, "m_s")
            softmax("m", M_s, False)
            take_T4("m_pt", dve, M_pT, (1, 3, 5, 7))
            take_T("m_pv", M_oT)
            add_out("m_out", 256, ALPHA)
            layer_norm("mix1", 7)
            experts(1)

        @block.gpsimd
        def _(pool):
            taken = [0]

            def link(ins):
                taken[0] += 1
                ins.then_inc(pool_step, 1)
                pool.wait_ge(pool_step, taken[0])

            Q = nc.gpsimd

            def row(dst, name, a=0, n=None):
                n = ROWN[name] if n is None else n
                src = rows_in[0:1, ROW0[name] + a:ROW0[name] + a + n]
                pool.dma_start(dst, src.broadcast_to([P, n])).then_inc(sem("lnw_loaded"), 16)

            def norm_weights(name, used):
                pool.wait_ge(sem("lnw_used"), used)
                row(lnw[:, 0, :], name, 0, D)
                row(lnw[:, 1, :], name, D, D)

            row(lnw[:, 0, :], "fin_g")
            link(Q.memset(ident[:, :], 0.0))
            Q.affine_select(out=ident[:, :], in_=ident[:, :], compare_op=ALU.not_equal, fill=1.0, base=0,
                            pattern=[[-1, P]], channel_multiplier=1).then_inc(sem("ident_ready"), 1)
            link(Q.iota(iota_i[:, :], pattern=[[1, P]], base=0, channel_multiplier=0))
            Q.tensor_copy(iota[:, :], iota_i[:, :]).then_inc(sem("ident_ready"), 1)
            pool.wait_ge(sem("ws_loaded"), 16)
            Q.affine_select(out=A_ws, in_=A_ws, compare_op=ALU.is_ge, fill=0.0, base=0,
                            pattern=[[0, 16], [1, P]], channel_multiplier=-1).then_inc(sem("ws_masked"), 1)
            link(Q.memset(B_mask, 0.0))
            link(Q.affine_select(out=B_mask, in_=B_mask, compare_op=ALU.is_ge, fill=NEG, base=-1,
                                 pattern=[[1, T]], channel_multiplier=-1))
            Q.affine_select(out=B_mask, in_=B_mask, compare_op=ALU.is_ge, fill=NEG, base=P,
                            pattern=[[-1, T]], channel_multiplier=1).then_inc(sem("b_mask_ready"), 1)
            pool.wait_ge(slab_done, SLAB0["a_out"] + 8)
            pool.wait_ge(sem("b_mask_ready"), 1)
            for i, (a, part) in enumerate(((B_kTe, slice(64, P)), (B_kTo, slice(0, 64)), (B_vz, slice(0, P)))):
                Q.memset(flat(a)[part, :], 0.0).then_inc(sem("pads_zero"), 1)
                pool.wait_ge(sem("pads_zero"), i + 1)
            pool.wait_ge(slab_done, SLAB0["b_kv"] + 1)
            pool.dma_start(flat(R_diff), diff_in).then_inc(sem("diff_loaded"), 16)
            norm_weights("mix0", 1)

            def experts(l):
                norm_weights(f"ffn{l}", 2 * l + 2)
                if l == 0:
                    pool.wait_ge(slab_done, SLAB0["u0"] + 1)
                    pool.dma_start(flat(keysT[:, :, :]), keys_in[1]).then_inc(sem("keys_loaded1"), 16)
                x_read(pool, f"p_kt{l}")
                w0 = X0[f"p_w{l}"]

                def hot1(buf, group):
                    t = bass.ds(group * 4, 4) if not isinstance(group, int) else slice(group * 4, group * 4 + 4)
                    Q.tensor_copy(key1[:, buf, :], picksT[:, 0, t]).then_inc(sem(f"key1_{l}"), 1)
                    pool.wait_ge(sem(f"key1_{l}"), group + 1)
                    pool.sem_inc(sem(f"key1_seen{l}"), 1)
                    for q in range(4):
                        last = Q.tensor_scalar(hot[:, 0, buf, q, :], iota[:, :], key1[:, buf, q:q + 1], None,
                                               ALU.is_equal)
                    last.then_inc(sem(f"hot1_{l}"), 1)

                hot1(0, 0)
                hot1(1, 1)
                for j in range(2, 4):
                    pool.wait_ge(x_full, w0 + j - 1)
                    hot1(j % 2, j)
                with pool.Fori(1, 16) as it:
                    for j in range(4):
                        pool.wait_ge(x_full, it * 4 + (w0 + j - 1))
                        hot1(j % 2, it * 4 + j)

            experts(0)
            pool.wait_ge(slab_done, SLAB0["m_in"])
            pool.wait_ge(sem("hot1_0"), 64)
            for i, (a, part) in enumerate(((M_krTe, slice(64, P)), (M_krTo, slice(0, 64)))):
                Q.memset(a[part, :], 0.0).then_inc(sem("pads_zero"), 1)
                pool.wait_ge(sem("pads_zero"), i + 4)
            norm_weights("mix1", 3)
            experts(1)


def kernel(**inputs):
    import concourse.bacc as bacc
    from concourse.bass_utils import run_bass_kernel_spmd

    a = {k: np.asarray(v) for k, v in inputs.items()}
    f32 = np.float32

    def slabs_of(w, width):
        k, n = w.shape
        s = w.reshape(k // P, P, n // width, width).transpose(2, 1, 0, 3).reshape(n // width, P, -1)
        return np.pad(s, ((0, 0), (0, 0), (0, 2048 - s.shape[2])))

    w_in = a["a_w_in"][0]
    b_in = a["b_w_in"][0]
    ret = a["ret_w_in_2"][0]
    uq = a["mla_w_uq_2"][0].reshape(Q_RANK, MLA_H, P + ROPE)
    mla_in = np.pad(a["mla_w_in_2"][0], ((0, 0), (0, 64)))

    def u_slabs(l):
        return slabs_of(a["peer_u_2"][l].T, 256)

    def v_slabs(l):
        return a["peer_v_2"][l].reshape(64, 2, P, D).transpose(0, 2, 1, 3).reshape(64, P, 2048)

    stages = {
        "a_v": slabs_of(w_in[:, W_A:2 * W_A], 256), "a_u": slabs_of(w_in[:, :W_A], 256),
        "a_g": slabs_of(w_in[:, 2 * W_A:], 256), "a_out": slabs_of(a["a_w_out"][0], P),
        "b_kv": slabs_of(a["w_kv"], 256), "b_q": slabs_of(b_in[:, :D], 256), "b_g": slabs_of(b_in[:, D:], 256),
        "b_out": slabs_of(a["b_w_out"][0], 256),
        "r_qk": slabs_of(ret[:, :2048], 256), "r_v": slabs_of(ret[:, 2048:4096], 256),
        "r_g": slabs_of(ret[:, 4096:], 256), "r_out": slabs_of(a["ret_w_out_2"][0], P),
        "m_in": slabs_of(mla_in, 256), "m_qn": slabs_of(uq[:, :, :P].reshape(Q_RANK, -1), 256),
        "m_qr": slabs_of(uq[:, :, P:].reshape(Q_RANK, -1), 256), "m_kv": slabs_of(a["mla_w_ukv_2"][0], 256),
        "m_out": slabs_of(a["mla_w_out_2"][0], 256),
    }
    slabs = np.empty((N_SLABS, P, 2048), f32)
    for name, n in SLAB_STAGES:
        if name[0] in "uv" and name[1] in "01":
            part = (u_slabs if name[0] == "u" else v_slabs)(int(name[1]))
        elif name.startswith("pq"):
            part = slabs_of(a["peer_w_q_2"][int(name[2])], 256)
        else:
            part = stages[name]
        assert part.shape[0] == n, name
        slabs[SLAB0[name]:SLAB0[name] + n] = part

    def inv_freq(dh):
        return (np.float32(10000.0) ** (-np.arange(0, dh, 2, dtype=f32) / np.float32(dh))).astype(f32)

    angle = np.arange(T, dtype=f32)[:, None] * inv_freq(DH)[None, :]
    rope = np.stack([np.cos(angle), np.sin(angle)], 1).astype(f32).reshape(NB, P, 64).transpose(1, 0, 2).reshape(P, P)
    m, n = np.arange(T)[:, None], np.arange(T)[None, :]
    diff = np.stack([np.maximum(n - m, 0), np.maximum(m - n, 0)]).astype(f32)
    diff = diff.reshape(2, NB, P, T).transpose(2, 0, 1, 3).reshape(P, 1024)

    def columns(v):
        return v.reshape(-1, P).T

    cols = np.concatenate([columns(a["a_norm_g"]), columns(a["kv_norm_g"]), columns(a["b_norm_g"]),
                           columns(a["ret_gn_g_2"]), columns(a["ret_gn_b_2"]), columns(a["mla_q_norm_2"]),
                           columns(a["mla_kv_norm_2"]), inv_freq(RET_DK)[:, None]], 1)

    def pair(w, b, l):
        return np.concatenate([a[w][l], a[b][l]])

    row_parts = {
        "ln_g": a["a_ln_g"], "ln_b": a["a_ln_b"], "bs": a["a_bs"], "bq": a["b_bq"], "bkv": a["b_kv"],
        "sinks": a["b_sinks"], "decay": a["ret_log1m_decay_2"], "invf_row": inv_freq(ROPE), "fin_g": a["final_norm_g"],
        "mix0": pair("ln_mix_g_2", "ln_mix_b_2", 0), "ffn0": pair("ln_ffn_g_2", "ln_ffn_b_2", 0),
        "mix1": pair("ln_mix_g_2", "ln_mix_b_2", 1), "ffn1": pair("ln_ffn_g_2", "ln_ffn_b_2", 1),
    }
    rows = np.concatenate([row_parts[name].ravel() for name, _ in ROWS])[None, :]
    pos = a["positions_2"].reshape(T)
    arrays = {
        "slabs": slabs,
        "x": a["x"].reshape(T, D),
        "cols": cols,
        "rows": rows,
        "ws": a["a_ws"][0].transpose(2, 0, 1).reshape(P, 16 * P),
        "keys": a["peer_sub_keys_2"].reshape(2, 16, NKEYS, P).transpose(0, 3, 1, 2).reshape(2, P, 16 * NKEYS),
        "pos_row": pos.reshape(1, T),
        "pos_col": pos.reshape(NB, P).T,
        "rope": rope,
        "diff": diff,
    }
    arrays = {f"{k}_in": np.ascontiguousarray(v) for k, v in arrays.items()}
    nc = bacc.Bacc("TRN2", target_bir_lowering=False, num_devices=1)
    args = [nc.dram_tensor(k, v.shape, mybir.dt.from_np(v.dtype), kind="ExternalInput").ap() for k, v in arrays.items()]
    out = nc.dram_tensor("out", (T, D), mybir.dt.float32, kind="ExternalOutput").ap()
    build(nc, *args, out)
    r = run_bass_kernel_spmd(nc, [arrays], core_ids=[0])
    return r.results[0]["out"].reshape(1, T, D)
```

```python
from contextlib import ExitStack

import numpy as np

import concourse.bass as bass
from concourse import mybir

P = 128
T = 256
NB = T // P
D = 1024
DC = D // P
W_A = 2048
RING = 2
SPLIT = 4
HOT = 4
EPS = 1e-5
ALPHA = 4.0 ** 0.25
HEADS_B, KVH, DH = 16, 2, 64
RET_H, RET_DK, RET_DV = 4, 256, 512
MLA_H, Q_RANK, KV_RANK, ROPE = 8, 384, 256, 64
PK_H, NKEYS, TOPK = 8, 128, 16
NEG = -1.0e30
LOWEST = -3.0e38

SLAB_STAGES = [
    ("a_v", 8), ("a_u", 8), ("a_g", 8), ("a_out", 8),
    ("b_kv", 1), ("b_q", 4), ("b_g", 4), ("b_out", 4),
    ("r_qk", 8), ("r_v", 8), ("r_g", 8), ("r_out", 8),
    ("pq0", 8), ("u0", 64), ("v0", 64),
    ("m_in", 3), ("m_qn", 4), ("m_qr", 2), ("m_kv", 8), ("m_out", 4),
    ("pq1", 8), ("u1", 64), ("v1", 64),
]
X_STAGES = [
    ("a_tr", 4), ("a_sv", 8), ("b_tr", 4), ("b_ktr", 1), ("b_qtr", 4),
    ("b_s0", 4), ("b_s1", 8), ("b_pt0", 4), ("b_pt1", 8), ("b_pv0", 2), ("b_pv1", 2),
    ("r_tr", 4), ("r_s", 4), ("r_y", 8), ("r_yt", 8),
    ("p_tr0", 4), ("p_s0", 8), ("p_kt0", 2), ("p_w0", 64), ("p_y0", 4), ("p_yr0", 4),
    ("m_tr", 4), ("m_ct", 3), ("m_krt", 1), ("m_qrt", 2), ("m_s", 8), ("m_pt", 8), ("m_pv", 4),
    ("p_tr1", 4), ("p_s1", 8), ("p_kt1", 2), ("p_w1", 64), ("p_y1", 4), ("p_yr1", 4),
]


def first_index(stages):
    at, out = 0, {}
    for name, n in stages:
        out[name] = at
        at += n
    return out, at


SLAB0, N_SLABS = first_index(SLAB_STAGES)
X0, _ = first_index(X_STAGES)
SLABS = dict(SLAB_STAGES)
XTILES = dict(X_STAGES)


def gives_tile(name, n):
    return name not in ("v0", "v1") and (name not in ("a_out", "r_out") or n % 2 == 1)


def tiles_before(slab):
    return sum(1 for name, count in SLAB_STAGES for n in range(count)
               if gives_tile(name, n) and SLAB0[name] + n < slab and (SLAB0[name] + n) % 4 == slab % 4)


COLS = [("a_g", 8), ("kv_g", 8), ("b_g", 8), ("gn_g", 16), ("gn_b", 16), ("m_qg", 3), ("m_kvg", 2), ("invf", 1)]
ROWS = [("ln_g", 2048), ("ln_b", 2048), ("bs", 2048), ("bq", 1024), ("bkv", 256), ("sinks", 16),
        ("decay", 8), ("invf_row", 32), ("fin_g", 1024),
        ("mix0", 2048), ("ffn0", 2048), ("mix1", 2048), ("ffn1", 2048)]
COL0, N_COLS = first_index(COLS)
ROW0, N_ROWS = first_index(ROWS)
ROWN = dict(ROWS)


def build(nc, slabs, x_in, cols_in, rows_in, ws_in, keys_in, pos_row, pos_col, rope_in, diff_in, out):
    f32, u32, i32 = mybir.dt.float32, mybir.dt.uint32, mybir.dt.int32
    f32r = mybir.dt.float32r
    ALU, ACT, AX = mybir.AluOpType, mybir.ActivationFunctionType, mybir.AxisListType
    ctx = ExitStack()
    with ctx:
        def sb(name, shape, dt=f32):
            return ctx.enter_context(nc.sbuf_tensor(name, shape, dt))

        made = {}

        def sem(name):
            if name not in made:
                made[name] = ctx.enter_context(nc.semaphore(name))
            return made[name]

        def twin(name, shape, dt, other):
            return nc.alloc_sbuf_tensor_at(name, shape, dt, offset=other)

        def here():
            return (nc.sbuf_base + 31) // 32 * 32

        big_at = here()
        big = sb("big", [P, NKEYS * T])
        ring = [sb(f"ring{i}", [P, 2048]) for i in range(RING)]
        w_hi = sb("w_hi", [P, SPLIT, 1024], f32r)
        w_lo = sb("w_lo", [P, SPLIT, 1024], f32r)
        hT_at = here()
        hT_hi = sb("hT_hi", [P, DC, T], f32r)
        hT_lo = sb("hT_lo", [P, DC, T], f32r)
        hot = twin("hot", [P, 2, HOT, 4, NKEYS], f32, hT_at)
        h = sb("h", [P, NB, D])
        ident = sb("ident", [P, P])
        iota = sb("iota", [P, P])
        picksT = sb("picksT", [P, 3, T])
        key1 = sb("key1", [P, 2, 4])
        cols = sb("cols", [P, N_COLS])
        rope_row = sb("rope_row", [P, NB, 2, 32])
        st = sb("st", [P, 8, 6])
        mv = sb("mv", [P, 8, 2])
        rstd = sb("rstd", [P, 8])
        mx = sb("mx", [P, 16])
        negm = sb("negm", [P, 16])
        rsum = sb("rsum", [P, 16])
        esink = sb("esink", [P, 16])
        rden = sb("rden", [P, 16])
        G = [ctx.enter_context(nc.psum_tensor(f"G{i}", [P, 512], f32)) for i in range(4)]
        X = [ctx.enter_context(nc.psum_tensor(f"X{i}", [P, 512], f32)) for i in range(4)]

        def shaped(a, shape):
            if len(shape) == 1:
                return a
            names = "abcd"[:len(shape)]
            return a.rearrange(f"p ({' '.join(names)}) -> p {' '.join(names)}",
                               **dict(zip(names[1:], shape[1:])))

        def area(off, *shape):
            return shaped(big[:, off:off + int(np.prod(shape))], shape)

        def area_r(name, off, *shape):
            return shaped(twin(name, [P, int(np.prod(shape))], f32r, big_at + 4 * off)[:, :], shape)

        def col(name, i):
            return cols[:, COL0[name] + i:COL0[name] + i + 1]

        def bc(ap, axis, n):
            shape = list(ap.shape)
            shape.insert(axis, n)
            return ap.unsqueeze(axis).broadcast_to(shape)

        xs = area(0, NB, D)
        A_v = area(2048, NB, W_A)
        A_u = area(6144, 16, T)
        A_g = area(10240, 16, T)
        A_y = area(14336, 16, T)
        A_lng, A_lnb = area(18432, W_A), area(20480, W_A)
        A_ws = area(22528, 16, P)
        A_bs = area(24576, 16, P)
        A_yh = area_r("A_yh", 6144, 16, T)
        A_yl = area_r("A_yl", 2048, 16, T)
        hKV_hi = area_r("hKV_hi", 26624, DC, T)
        hKV_lo = area_r("hKV_lo", 17152, DC, T)
        fin_g = area(27648, D)
        lnw = area(30720, 2, D)
        B_mask = area(28672, T)
        B_bq, B_bkv = area(30720, D), area(31744, 256)
        B_sink = area(32000, 16)
        B_rope = area(32128, NB, 2, 32)
        R_decay = area(32256, 8)
        B_q = area(2048, NB, D)
        B_kv = area(4096, NB, 256)
        B_kdup = area(4608, NB, KVH, 2, DH)
        B_vz = area(5120, NB, KVH, 192)
        B_qT = area(5888, DC, T)
        B_kTe, B_kTo = area(7936, KVH, T), area(8448, KVH, T)
        B_s0 = area(8960, 16, P)
        B_s1 = area(11008, 16, T)
        B_pT0 = area(15104, 16, P)
        B_pT1 = area(17152, 16, 2, P)
        B_gT = area(21248, DC, T)
        B_yT = area(23296, DC, T)
        B_yh = area_r("B_yh", 8960, DC, T)
        B_yl = area_r("B_yl", 11008, DC, T)
        TMP = area(25344, 1280)
        R_qk = area(0, 16, T)
        R_tmp = area(4096, 2, 512)
        R_v = area(5120, NB, 2048)
        R_g = area(9216, 16, T)
        R_D = area(13312, RET_H, 512)
        R_s = area(15360, RET_H, NB, T)
        R_y = area(17408, NB, 2048)
        R_yT = area(21504, 16, T)
        R_yh = area_r("R_yh", 0, 16, T)
        R_yl = area_r("R_yl", 5120, 16, T)
        cosT, sinT = area(28928, T), area(29184, T)
        R_diff = area(26624, 2, 512)
        R_lg = area(32264, 6, 8)
        R_invf = area(32320, 32)
        pos_i = area(26624, T).bitcast(i32)
        posc_i = area(26880, NB).bitcast(i32)
        iota_i = area(26944, P).bitcast(i32)
        M_c = area(0, NB, 768)
        M_cn = area(1536, NB, 640)
        M_cTh = area_r("M_cTh", 2816, 5, T)
        M_cTl = area_r("M_cTl", 24576, 5, T)
        M_kr = area(4096, NB, 2, ROPE)
        M_krTe, M_krTo = area(4352, T), area(4608, T)
        M_qn = area(4864, MLA_H, T)
        M_qr = area(6912, NB, 512)
        M_qrT = area(7936, 4, T)
        M_kn = area(8960, MLA_H, T)
        M_v = area(11008, NB, MLA_H * P)
        M_s = area(13056, 16, T)
        M_pT = area(17152, MLA_H, 2, T)
        M_oTh = area_r("M_oTh", 21248, DC, T)
        M_oTl = area_r("M_oTl", 25856, DC, T)
        M_tmp = area(23296, 1280)
        K_q = area(0, 16, T)
        K_s = area(22528, NB, 16, NKEYS)
        K_cand = area(26624, PK_H, 256)
        K_eq = area(28672, PK_H, TOPK, TOPK)
        keysT = area(28672, 16, NKEYS)
        K_top = area(30720, 16, TOPK)
        K_iu = area(30976, 16, TOPK).bitcast(u32)
        K_if = area(31232, 16, TOPK)
        K_ts = area(31488, PK_H, TOPK)
        K_pu = area(31616, PK_H, TOPK).bitcast(u32)
        K_au = area(31744, PK_H, TOPK).bitcast(u32)
        K_af = area(31872, PK_H, TOPK)
        K_sum = mx[:, 0:PK_H]
        K_yT = area(0, DC, T)
        FREE_SLABS = 44
        assert FREE_SLABS * 512 <= 22528
        picks = picksT[:, :, :].rearrange("p a t -> p (a t)").rearrange("p (b a k) -> p b a k", b=NB, a=3)

        slab_loaded = [sem(f"slab_loaded{i}") for i in range(RING)]
        hi_ready = sem("hi_ready")
        split_ready = sem("split_ready")
        half_done = sem("half_done")
        g_free = [sem(f"g_free{i}") for i in range(4)]
        x_full = sem("x_full")
        x_free = [sem(f"x_free{i}") for i in range(4)]
        dve_step, act_step, pool_step = sem("dve_step"), sem("act_step"), sem("pool_step")

        block = ctx.enter_context(nc.Block())

        def fours(eng, n):
            if n % 4 or n < 8:
                for j in range(n):
                    yield j, j
            else:
                with eng.Fori(0, n // 4) as it:
                    for j in range(4):
                        yield j, it * 4 + j

        def at(n, size):
            return bass.ds(n * size, size) if not isinstance(n, int) else slice(n * size, (n + 1) * size)

        def flat(ap):
            names = "abcd"[:len(ap.shape) - 1]
            return ap.rearrange(f"p {' '.join(names)} -> p ({' '.join(names)})")

        def x_tile(eng, stage, i):
            x = X0[stage] + i
            eng.wait_ge(x_full, x + 1)
            return X[x % 4], x_free[x % 4]

        def x_read(eng, stage, i=None):
            tiles = range(max(0, XTILES[stage] - 4), XTILES[stage]) if i is None else [i]
            for k in tiles:
                x = X0[stage] + k
                eng.wait_ge(x_free[x % 4], x // 4 + 1)

        def g_tile(eng, stage, j, n):
            s = SLAB0[stage] + j
            eng.wait_ge(half_done, n * 2 + 2 * (SLAB0[stage] + 1))
            return G[s % 4], g_free[s % 4]

        def g_read(eng, stage):
            for n in range(max(0, SLABS[stage] - 4), SLABS[stage]):
                if gives_tile(stage, n):
                    s = SLAB0[stage] + n
                    eng.wait_ge(g_free[s % 4], tiles_before(s) + 1)

        R_a = area(29440, 4, 320)

        def take_T4(stage, eng, dst, tiles):
            for i in tiles:
                tile, free = x_tile(eng, stage, i)
                to = flat(dst)[:, 512 * i:512 * (i + 1)]
                if eng is nc.scalar:
                    nc.scalar.activation(to, tile[:, :], ACT.Copy).then_inc(free, 1)
                else:
                    nc.vector.tensor_copy(to, tile[:, :]).then_inc(free, 1)

        @block.sync
        def _(sp):
            for s in range(RING):
                sp.dma_start(ring[s][:, :], slabs[s]).then_inc(slab_loaded[s], 16)
            assert N_SLABS % RING == 0
            with sp.Fori(1, N_SLABS // RING) as it:
                for j in range(RING):
                    sp.wait_ge(split_ready, it * (2 * RING) + 2 * (j + 1 - RING))
                    sp.dma_start(ring[j][:, :], slabs[bass.ds(it * RING + j, 1)].rearrange("a p n -> (a p) n")
                                 ).then_inc(slab_loaded[j], 16)
            sp.wait_ge(sem("h_ffn1"), 2)
            sp.dma_start(out.rearrange("(b p) d -> p b d", p=P), h[:, :, :]).then_inc(sem("out_stored"), 16)
            sp.wait_ge(sem("out_stored"), 16)

        @block.tensor
        def _(pe):
            def rounds(n):
                if n % 4 or n < 8:
                    for j in range(n):
                        yield j % 4, j // 4
                else:
                    with pe.Fori(0, n // 4) as it:
                        for j in range(4):
                            yield j, it

            def half_ready(s, r, half):
                pe.wait_ge(split_ready, r * 8 + (2 * s + half + 1))
                return 2 * (s % 2) + half

            def bank_free(s, r):
                before = tiles_before(s)
                if before or not isinstance(r, int) or r:
                    pe.wait_ge(g_free[s % 4], r + before)

            def triple(out, stationary, moving, start, stop):
                (a_hi, a_lo), (b_hi, b_lo) = stationary, moving
                nc.tensor.matmul(out, a_hi, b_hi, start=start, stop=False, skip_group_check=True)
                nc.tensor.matmul(out, a_hi, b_lo, start=False, stop=False, skip_group_check=True)
                return nc.tensor.matmul(out, a_lo, b_hi, start=False, stop=stop, skip_group_check=True)

            def project_slab(s, r, src, k, rows, pair):
                hi, lo = src
                k0 = 0 if pair is None else 8 * pair
                if pair != 1:
                    bank_free(s + (pair is not None), r)
                bank = G[(s + (pair == 0)) % 4]
                for half in range(2):
                    q = half_ready(s, r, half)
                    kh = (k + 1) // 2
                    for i in range(kh if half == 0 else k - kh):
                        c = k0 + half * kh + i
                        for a in range(2):
                            act = [x[:, c, a * P:(a + 1) * P] if rows else x[:, c, :] for x in src]
                            w = [x[:, q, i * 256:(i + 1) * 256] if rows else x[:, q, i * 256 + a * P:i * 256 + (a + 1) * P]
                                 for x in (w_hi, w_lo)]
                            last = triple(bank[:, a * T:(a + 1) * T], act if rows else w, w if rows else act,
                                          c == 0 and a == 0, c == k0 + k - 1 and pair != 0)
                    last.then_inc(half_done, 1)

            def project(stage, src, k, rows, pairs=False):
                s0, n = SLAB0[stage], SLABS[stage]
                if tiles_before(s0 + 3) == 0:
                    for j in range(4):
                        project_slab(s0 + j, 0, src, k, rows, None)
                    s0, n = s0 + 4, n - 4
                for j, r in rounds(n):
                    project_slab(s0 + j, r, src, k, rows, j % 2 if pairs else None)

            def project_rows(stage, src, k):
                project(stage, src, k, True)

            def project_cols(stage, src, k):
                project(stage, src, k, False)

            def x_begin(stage, i):
                x = X0[stage] + i
                if x >= 4:
                    pe.wait_ge(x_free[x % 4], x // 4)
                return X[x % 4]

            def transpose_rows(stage, src, chunks=DC):
                for i in range(XTILES[stage]):
                    tile = x_begin(stage, i)
                    for a in range(min(2, chunks - 2 * i)):
                        for b in range(NB):
                            c = 2 * i + a
                            last = nc.tensor.transpose(tile[:, a * T + b * P:a * T + (b + 1) * P],
                                                       src[:, b, c * P:(c + 1) * P], ident[:, :])
                    last.then_inc(x_full, 1)

            hT = (hT_hi, hT_lo)
            cT = (M_cTh, M_cTl)

            pe.wait_ge(sem("ident_ready"), 2)
            pe.wait_ge(sem("xs_a"), 2)
            transpose_rows("a_tr", xs)
            x_read(pe, "a_tr")
            project_rows("a_v", hT, DC)
            project_cols("a_u", hT, DC)
            pe.wait_ge(sem("vn_ready"), 1)
            pe.wait_ge(sem("ws_masked"), 1)
            for i in range(8):
                tile = x_begin("a_sv", i)
                for a in range(2):
                    for b in range(NB):
                        g = 2 * i + a
                        last = nc.tensor.matmul(tile[:, a * T + b * P:a * T + (b + 1) * P],
                                                A_v[:, b, g * P:(g + 1) * P], A_ws[:, g, :], start=True, stop=True)
                last.then_inc(x_full, 1)
            project_cols("a_g", hT, DC)
            pe.wait_ge(sem("a_y_ready"), 8)
            project("a_out", (A_yh, A_yl), DC, True, pairs=True)

            pe.wait_ge(sem("xs_b"), 2)
            transpose_rows("b_tr", xs)
            x_read(pe, "b_tr")
            project_rows("b_kv", (hKV_hi, hKV_lo), DC)
            project_rows("b_q", hT, DC)
            project_cols("b_g", hT, DC)
            pe.wait_ge(sem("k_rotated"), 1)
            tile = x_begin("b_ktr", 0)
            for g in range(KVH):
                for b in range(NB):
                    last = nc.tensor.transpose(tile[:, g * T + b * P:g * T + (b + 1) * P],
                                               B_kdup[:, b, g, :, :].rearrange("p a d -> p (a d)"), ident[:, :])
            last.then_inc(x_full, 1)
            pe.wait_ge(sem("q_rotated"), 4)
            transpose_rows("b_qtr", B_q)
            x_read(pe, "b_ktr")
            pe.wait_ge(sem("pads_zero"), 3)
            x_read(pe, "b_qtr")
            kT = [B_kTe, B_kTo]
            for i in range(4):
                tile = x_begin("b_s0", i)
                for a in range(4):
                    hd = 4 * i + a
                    last = nc.tensor.matmul(tile[:, a * P:(a + 1) * P], B_qT[:, hd // 2, 0:P],
                                            kT[hd % 2][:, hd // 8, 0:P], start=True, stop=True)
                last.then_inc(x_full, 1)
            for i in range(8):
                tile = x_begin("b_s1", i)
                for a in range(2):
                    hd = 2 * i + a
                    last = nc.tensor.matmul(tile[:, a * T:(a + 1) * T], B_qT[:, hd // 2, P:T],
                                            kT[hd % 2][:, hd // 8, :], start=True, stop=True)
                last.then_inc(x_full, 1)
            pe.wait_ge(sem("p_b0"), 1)
            for i in range(4):
                tile = x_begin("b_pt0", i)
                for a in range(4):
                    last = nc.tensor.transpose(tile[:, a * P:(a + 1) * P], B_s0[:, 4 * i + a, :], ident[:, :])
                last.then_inc(x_full, 1)
            pe.wait_ge(sem("p_b1"), 1)
            for i in range(8):
                tile = x_begin("b_pt1", i)
                for a in range(2):
                    for c in range(2):
                        last = nc.tensor.transpose(tile[:, a * T + c * P:a * T + (c + 1) * P],
                                                   B_s1[:, 2 * i + a, c * P:(c + 1) * P], ident[:, :])
                last.then_inc(x_full, 1)
            x_read(pe, "b_pt0")
            pe.wait_ge(sem("vz_ready"), 1)

            def v_of(b, hd):
                return B_vz[:, b, hd // 8, 64:192] if hd % 2 == 0 else B_vz[:, b, hd // 8, 0:128]

            for i in range(2):
                tile = x_begin("b_pv0", i)
                for a in range(4):
                    for e in range(2):
                        hd = 2 * (4 * i + a) + e
                        last = nc.tensor.matmul(tile[:, a * P:(a + 1) * P], v_of(0, hd), B_pT0[:, hd, :],
                                                start=(e == 0), stop=(e == 1))
                last.then_inc(x_full, 1)
            x_read(pe, "b_pt1")
            for i in range(2):
                tile = x_begin("b_pv1", i)
                for a in range(4):
                    for e in range(4):
                        hd, kc = 2 * (4 * i + a) + e // 2, e % 2
                        last = nc.tensor.matmul(tile[:, a * P:(a + 1) * P], v_of(kc, hd), B_pT1[:, hd, kc, :],
                                                start=(e == 0), stop=(e == 3))
                last.then_inc(x_full, 1)
            pe.wait_ge(sem("b_y_ready"), 1)
            project_rows("b_out", (B_yh, B_yl), DC)

            pe.wait_ge(sem("h_b"), 2)
            transpose_rows("r_tr", h)
            x_read(pe, "r_tr")
            project_cols("r_qk", hT, DC)
            project_rows("r_v", hT, DC)
            pe.wait_ge(sem("r_qk_ready"), 8)
            for hd in range(RET_H):
                tile = x_begin("r_s", hd)
                for m in range(NB):
                    for c in range(2):
                        last = nc.tensor.matmul(tile[:, m * T:(m + 1) * T], R_qk[:, 8 + 2 * hd + c, m * P:(m + 1) * P],
                                                R_qk[:, 2 * hd + c, :], start=(c == 0), stop=(c == 1))
                last.then_inc(x_full, 1)
            g_read(pe, "r_v")
            for i in range(8):
                hd, b = i // 2, i % 2
                if b == 0:
                    x_read(pe, "r_s", hd)
                tile = x_begin("r_y", i)
                for m in range(NB):
                    last = nc.tensor.matmul(tile[:, :], R_s[:, hd, m, b * P:(b + 1) * P],
                                            R_v[:, m, hd * RET_DV:(hd + 1) * RET_DV], start=(m == 0), stop=(m == 1))
                last.then_inc(x_full, 1)
            project_cols("r_g", hT, DC)
            pe.wait_ge(sem("r_yn_ready"), 1)
            transpose_rows("r_yt", R_y, 16)
            pe.wait_ge(sem("r_y_ready"), 8)
            project("r_out", (R_yh, R_yl), DC, True, pairs=True)

            def experts(l):
                pe.wait_ge(sem(f"h_mix{l}"), 2)
                transpose_rows(f"p_tr{l}", h)
                x_read(pe, f"p_tr{l}")
                project_cols(f"pq{l}", hT, DC)
                pe.wait_ge(sem(f"keys_loaded{l}"), 16)
                g_read(pe, f"pq{l}")
                for i in range(8):
                    tile = x_begin(f"p_s{l}", i)
                    for a in range(4):
                        hc = 4 * (i % 4) + a
                        last = nc.tensor.matmul(tile[:, a * P:(a + 1) * P], K_q[:, hc, (i // 4) * P:(i // 4 + 1) * P],
                                                keysT[:, hc, :], start=True, stop=True)
                    last.then_inc(x_full, 1)
                project_cols(f"u{l}", hT, DC)
                for b in range(NB):
                    pe.wait_ge(sem(f"picks{l}"), b + 1)
                    tile = x_begin(f"p_kt{l}", b)
                    for a in range(3):
                        last = nc.tensor.transpose(tile[:, a * P:(a + 1) * P], picks[:, b, a, :], ident[:, :])
                    last.then_inc(x_full, 1)
                w0 = X0[f"p_w{l}"]
                with pe.Fori(0, 16) as it:
                    for j in range(4):
                        x = w0 + j
                        pe.wait_ge(x_free[x % 4], it + x // 4)
                        pe.wait_ge(sem(f"hot1a_{l}"), it * 4 + (j + 1))
                        pe.wait_ge(sem(f"hot1b_{l}"), it * 4 + (j + 1))
                        pe.wait_ge(sem(f"hot2_{l}"), it * 4 + (j + 1))
                        for q in range(4):
                            last = nc.tensor.matmul(X[x % 4][:, q * P:(q + 1) * P], hot[:, 1, j, q, :],
                                                    hot[:, 0, j, q, :], start=True, stop=True)
                        last.then_inc(x_full, 1)
                s0, y0 = SLAB0[f"v{l}"], X0[f"p_y{l}"]
                for i in range(4):
                    pe.wait_ge(x_free[(y0 + i) % 4], (y0 + i) // 4)

                def v_slab(j, r, first, final):
                    for a in range(2):
                        q = half_ready(s0 + j, r, a)
                        pe.wait_ge(sem(f"gated_split{l}"), r * 8 + (2 * j + a + 1))
                        act = [x[:, (2 * j + a) % 4, :] for x in hT]
                        for c in range(DC):
                            w = [x[:, q, c * P:(c + 1) * P] for x in (w_hi, w_lo)]
                            last = triple(X[(y0 + c // 2) % 4][:, (c % 2) * T:(c % 2 + 1) * T], w, act,
                                          first and a == 0 and c % 2 == 0, final and a == 1)
                            if final and a == 1 and c % 2:
                                last.then_inc(x_full, 1)
                        if not (final and a == 1):
                            last.then_inc(half_done, 1)

                for j in range(4):
                    v_slab(j, 0, j == 0, False)
                with pe.Fori(1, 15) as it:
                    for j in range(4):
                        v_slab(j, it, False, False)
                for j in range(4):
                    v_slab(j, 15, False, j == 3)
                pe.wait_ge(x_full, y0 + 4)
                pe.sem_inc(half_done, 1)
                x_read(pe, f"p_y{l}")
                for i in range(4):
                    tile = x_begin(f"p_yr{l}", i)
                    for a in range(4):
                        c = 4 * (i % 2) + a
                        last = nc.tensor.transpose(tile[:, a * P:(a + 1) * P],
                                                   K_yT[:, c, (i // 2) * P:(i // 2 + 1) * P], ident[:, :])
                    last.then_inc(x_full, 1)

            experts(0)

            pe.wait_ge(sem("h_ffn0"), 2)
            transpose_rows("m_tr", h)
            x_read(pe, "m_tr")
            project_rows("m_in", hT, DC)
            pe.wait_ge(sem("cn_ready"), 1)
            transpose_rows("m_ct", M_cn, 5)
            pe.wait_ge(sem("kr_rotated"), 1)
            tile = x_begin("m_krt", 0)
            for b in range(NB):
                last = nc.tensor.transpose(tile[:, b * P:(b + 1) * P],
                                           M_kr[:, b, :, :].rearrange("p a d -> p (a d)"), ident[:, :])
            last.then_inc(x_full, 1)
            x_read(pe, "m_ct")
            project_cols("m_qn", cT, 3)
            project_rows("m_qr", cT, 3)
            for j, r in rounds(8):
                s = SLAB0["m_kv"] + j
                bank_free(s, r)
                bank = G[s % 4]
                for c in range(2):
                    q = half_ready(s, r, c)
                    k_w = [x[:, q, 0:P] for x in (w_hi, w_lo)]
                    v_w = [x[:, q, P:2 * P] for x in (w_hi, w_lo)]
                    triple(bank[:, 0:T], k_w, [x[:, 3 + c, :] for x in cT], c == 0, c == 1)
                    for b in range(NB):
                        last = triple(bank[:, T + b * P:T + (b + 1) * P], [x[:, 3 + c, b * P:(b + 1) * P] for x in cT],
                                      v_w, False, c == 1)
                    last.then_inc(half_done, 1)
            pe.wait_ge(sem("mq_rotated"), 2)
            transpose_rows("m_qrt", M_qr, 4)
            x_read(pe, "m_krt")
            pe.wait_ge(sem("pads_zero"), 5)
            g_read(pe, "m_qn")
            g_read(pe, "m_kv")
            x_read(pe, "m_qrt")
            krT = [M_krTe, M_krTo]
            for hd in range(MLA_H):
                tile = x_begin("m_s", hd)
                for b in range(NB):
                    o = tile[:, b * T:(b + 1) * T]
                    nc.tensor.matmul(o, M_qn[:, hd, b * P:(b + 1) * P], M_kn[:, hd, :], start=True, stop=False)
                    last = nc.tensor.matmul(o, M_qrT[:, hd // 2, b * P:(b + 1) * P], krT[hd % 2], start=False, stop=True)
                last.then_inc(x_full, 1)
            pe.wait_ge(sem("p_m"), 1)
            for hd in range(MLA_H):
                tile = x_begin("m_pt", hd)
                for kc in range(2):
                    for b in range(NB):
                        last = nc.tensor.transpose(tile[:, kc * T + b * P:kc * T + (b + 1) * P],
                                                   M_s[:, 2 * hd + b, kc * P:(kc + 1) * P], ident[:, :])
                last.then_inc(x_full, 1)
            x_read(pe, "m_pt")
            for i in range(4):
                tile = x_begin("m_pv", i)
                for a in range(2):
                    hd = 2 * i + a
                    for kc in range(2):
                        last = nc.tensor.matmul(tile[:, a * T:(a + 1) * T], M_v[:, kc, hd * P:(hd + 1) * P],
                                                M_pT[:, hd, kc, :], start=(kc == 0), stop=(kc == 1))
                last.then_inc(x_full, 1)
            x_read(pe, "m_pv")
            project_rows("m_out", (M_oTh, M_oTl), DC)
            experts(1)

        @block.scalar
        def _(act):
            def row(dst, name, loaded="rows_loaded", a=0, n=None):
                n = ROWN[name] if n is None else n
                src = rows_in[0:1, ROW0[name] + a:ROW0[name] + a + n]
                act.dma_start(dst, src.broadcast_to([P, n])).then_inc(sem(loaded), 16)

            def norm_weights(name):
                row(lnw[:, 0, :], name, "lnw_loaded", 0, D)
                row(lnw[:, 1, :], name, "lnw_loaded", D, D)

            act.dma_start(h[:, :, :], x_in.rearrange("(b p) d -> p b d", p=P)).then_inc(sem("x_loaded"), 16)
            act.dma_start(cols[:, :], cols_in).then_inc(sem("cols_loaded"), 16)
            act.dma_start(pos_i, pos_row.broadcast_to([P, T])).then_inc(sem("pos_loaded"), 16)
            act.dma_start(posc_i, pos_col).then_inc(sem("pos_loaded"), 16)
            row(R_decay, "decay")
            row(R_invf, "invf_row")
            row(A_lng, "ln_g")
            row(A_lnb, "ln_b")
            row(flat(A_bs), "bs")
            row(B_bq, "bq")
            row(B_bkv, "bkv")
            row(B_sink, "sinks")
            act.dma_start(flat(A_ws), ws_in).then_inc(sem("ws_loaded"), 16)
            act.dma_start(B_rope, rope_in.rearrange("p (a b c) -> p a b c", a=NB, b=2)).then_inc(sem("rope_loaded"), 16)

            def split(s, r=0):
                j = s % 2
                act.wait_ge(slab_loaded[j], r * 32 + 16 * (s // 2 + 1))
                for half in range(2):
                    n = 2 * s + half - SPLIT
                    if n >= 0:
                        act.wait_ge(half_done, r * 8 + (n + 1))
                    nc.scalar.activation(w_hi[:, 2 * j + half, :], ring[j][:, half * 1024:(half + 1) * 1024],
                                         ACT.Copy).then_inc(hi_ready, 1)

            def slabs_of(stage, first=0, count=None):
                count = SLABS[stage] if count is None else count
                s0 = SLAB0[stage] + first
                if count % 4 or count < 8:
                    for j in range(count):
                        yield j, first + j
                        if s0 + j + RING < N_SLABS:
                            split(s0 + j + RING)
                else:
                    with act.Fori(0, count // 4) as it:
                        for j in range(4):
                            yield j, it * 4 + (first + j)
                            split(s0 + j + RING, it)

            def only_split(stage, first=0, count=None):
                for _ in slabs_of(stage, first, count):
                    pass

            def root(name, n):
                act.wait_ge(sem(f"var_{name}"), 1)
                nc.scalar.activation(rstd[:, 0:n], rstd[:, 0:n], ACT.Sqrt).then_inc(sem(f"std_{name}"), 1)

            def round_T(stage, to, scale=None, tiles=4):
                for i in range(tiles):
                    tile, _ = x_tile(act, stage, i)
                    for dst, g in zip(to, scale or [None]):
                        if g is None:
                            last = nc.scalar.activation(flat(dst[:, 2 * i:2 * i + 2, :]), tile[:, :], ACT.Copy)
                            continue
                        for a in range(min(2, dst.shape[1] - 2 * i)):
                            last = nc.scalar.activation(dst[:, 2 * i + a, :], tile[:, a * T:(a + 1) * T], ACT.Copy,
                                                        scale=col(g, 2 * i + a))
                    last.then_inc(sem(f"rounded_{stage}"), 1)

            def take_T(stage, dst, tiles=(0, 2)):
                for i in tiles:
                    tile, free = x_tile(act, stage, i)
                    nc.scalar.activation(flat(dst[:, 2 * i:2 * i + 2, :]), tile[:, :], ACT.Copy).then_inc(free, 1)

            def take_cols(stage, dst, func=ACT.Copy, every=1, first=0, count=None):
                for j, n in slabs_of(stage, first, count):
                    if j % every == 0:
                        tile, free = g_tile(act, stage, (first + j) % 4, n)
                        nc.scalar.activation(flat(dst)[:, at(n, 512)], tile[:, :], func).then_inc(free, 1)

            def take_rows(stage, dst, every=1):
                for j, n in slabs_of(stage):
                    if j % every == 0:
                        tile, free = g_tile(act, stage, j, n)
                        nc.scalar.activation(dst[:, :, at(n, 256)], tile[:, :].rearrange("p (b n) -> p b n", b=NB),
                                             ACT.Copy).then_inc(free, 1)

            def exps(name, s, sinks):
                act.wait_ge(sem(f"max_{name}"), 1)
                if sinks:
                    nc.scalar.activation(esink[:, :], esink[:, :], ACT.Exp)
                for u in range(16):
                    last = nc.scalar.activation(s[:, u, :], s[:, u, :], ACT.Exp, bias=negm[:, u:u + 1],
                                                accum_out=rsum[:, u:u + 1])
                last.then_inc(sem(f"exp_{name}"), 1)

            for s in range(RING):
                split(s)
            root("a", 2)
            act.wait_ge(sem("cols_loaded"), 16)
            round_T("a_tr", [hT_hi], ["a_g"])
            act.wait_ge(sem("angles"), 1)
            nc.scalar.activation(sinT, R_a[:, 2, 0:T], ACT.Sin)
            nc.scalar.activation(cosT, R_a[:, 3, 0:T], ACT.Sin)
            nc.scalar.activation(rope_row[:, :, 1, :], R_a[:, 2, T:].rearrange("p (b f) -> p b f", b=NB), ACT.Sin)
            nc.scalar.activation(rope_row[:, :, 0, :], R_a[:, 3, T:].rearrange("p (b f) -> p b f", b=NB),
                                 ACT.Sin).then_inc(sem("rotary_ready"), 1)
            act.wait_ge(sem("rows_loaded"), 16 * 8)
            nc.scalar.activation(R_lg[:, 0, :], R_decay, ACT.Exp).then_inc(sem("decay_exp"), 1)
            act.wait_ge(sem("one_minus"), 1)
            nc.scalar.activation(R_lg[:, 2, :], R_lg[:, 1, :], ACT.Ln).then_inc(sem("decay_ln"), 1)
            take_rows("a_v", A_v, 2)
            take_cols("a_u", A_u, every=2, count=2)
            root("vn", 2)
            take_cols("a_u", A_u, every=2, first=2, count=6)
            take_cols("a_g", A_g, ACT.Silu)
            only_split("a_out")

            root("b", 2)
            round_T("b_tr", [hT_hi, hKV_hi], ["b_g", "kv_g"])
            only_split("b_kv")
            only_split("b_q")
            take_cols("b_g", B_gT, ACT.Silu)
            tile, free = x_tile(act, "b_ktr", 0)
            act.wait_ge(sem("pads_zero"), 2)
            nc.scalar.activation(flat(B_kTe)[0:64, :], tile[0:64, :], ACT.Copy)
            nc.scalar.activation(flat(B_kTo)[64:128, :], tile[64:128, :], ACT.Copy).then_inc(free, 1)
            act.dma_start(flat(R_diff), diff_in).then_inc(sem("diff_loaded"), 16)
            row(fin_g, "fin_g", "lnw_loaded")
            take_T("b_qtr", B_qT)
            exps("b0", B_s0, True)
            take_T4("b_pt0", act, B_pT0, (0, 2))
            exps("b1", B_s1, True)
            take_T4("b_pt1", act, B_pT1, (0, 2, 4, 6))
            only_split("b_out")
            root("fin", 2)

            round_T("r_tr", [hT_hi])
            for i in range(RET_H):
                act.wait_ge(sem("decay_arg"), i + 1)
                nc.scalar.activation(R_D[:, i, :], R_D[:, i, :], ACT.Exp).then_inc(sem("decay_ready"), 1)
            norm_weights("mix0")
            only_split("r_qk")
            take_rows("r_v", R_v)
            for i in range(8):
                tile, free = x_tile(act, "r_y", i)
                nc.scalar.activation(R_y[:, i % 2, (i // 2) * RET_DV:(i // 2 + 1) * RET_DV], tile[:, :],
                                     ACT.Copy).then_inc(free, 1)
            take_cols("r_g", R_g, ACT.Silu, count=2)
            root("gn", 8)
            take_cols("r_g", R_g, ACT.Silu, first=2, count=6)
            only_split("r_out")
            root("mix0", 2)

            def experts(l):
                act.wait_ge(sem(f"h_mix{l}"), NB)
                act.dma_start(flat(keysT), keys_in[l]).then_inc(sem(f"keys_loaded{l}"), 16)
                round_T(f"p_tr{l}", [hT_hi])
                take_cols(f"pq{l}", K_q)
                for i in range(8):
                    tile, free = x_tile(act, f"p_s{l}", i)
                    nc.scalar.activation(flat(K_s[:, i // 4, 4 * (i % 4):4 * (i % 4) + 4, :]), tile[:, :],
                                         ACT.Copy).then_inc(free, 1)

                def gelus(first, count):
                    for j, n in slabs_of(f"u{l}", first, count):
                        tile, free = g_tile(act, f"u{l}", j, n)
                        nc.scalar.activation(big[:, at(n, 512)], tile[:, :], ACT.Gelu).then_inc(free, 1)

                gelus(0, FREE_SLABS)
                for b in range(NB):
                    act.wait_ge(sem(f"top{l}"), b + 1)
                    nc.scalar.activation(picks[:, b, 2, :], picks[:, b, 2, :], ACT.Exp).then_inc(sem(f"gates{l}"), 1)
                gelus(FREE_SLABS, 64 - FREE_SLABS)
                x_read(act, f"p_kt{l}")
                w0 = X0[f"p_w{l}"]

                def hot1(j, group):
                    for q in range(2):
                        t = bass.ds(group * 4 + q, 1) if not isinstance(group, int) else slice(group * 4 + q,
                                                                                               group * 4 + q + 1)
                        last = nc.scalar.activation(hot[:, 0, j, q, :], iota[:, :], ACT.Abs, bias=picksT[:, 0, t],
                                                    scale=-1.0)
                    last.then_inc(sem(f"distance{l}"), 1)
                    act.wait_ge(sem(f"distance{l}"), group + 1)
                    nc.scalar.activation(hot[:, 0, j, 0:2, :], hot[:, 0, j, 0:2, :], ACT.Relu, bias=1.0,
                                         scale=-1.0).then_inc(sem(f"hot1a_{l}"), 1)

                for j in range(HOT):
                    hot1(j, j)
                with act.Fori(1, T // 16) as it:
                    for j in range(4):
                        act.wait_ge(x_full, it * 4 + (w0 + j - 3))
                        hot1(j, it * 4 + j)
                only_split(f"v{l}", 0, 60)
                only_split(f"v{l}", 60, 4)
                take_T(f"p_y{l}", K_yT)
                norm_weights(f"ffn{l}")
                root(f"ffn{l}", 2)

            experts(0)

            round_T("m_tr", [hT_hi])
            norm_weights("mix1")
            take_rows("m_in", M_c)
            root("cn", 4)
            round_T("m_ct", [M_cTh], ["m_qg"], 3)
            tile, free = x_tile(act, "m_krt", 0)
            act.wait_ge(sem("pads_zero"), 5)
            nc.scalar.activation(M_krTe[0:64, :], tile[0:64, 0:T], ACT.Copy)
            nc.scalar.activation(M_krTo[64:128, :], tile[64:128, 0:T], ACT.Copy).then_inc(free, 1)
            take_cols("m_qn", M_qn)
            only_split("m_qr")
            for j, n in slabs_of("m_kv"):
                tile, free = g_tile(act, "m_kv", j, n)
                nc.scalar.activation(flat(M_kn)[:, at(n, T)], tile[:, 0:T], ACT.Copy)
                nc.scalar.activation(M_v[:, :, at(n, P)], tile[:, T:].rearrange("p (b n) -> p b n", b=NB),
                                     ACT.Copy).then_inc(free, 1)
            for i in range(8):
                tile, free = x_tile(act, "m_s", i)
                nc.scalar.activation(flat(M_s[:, 2 * i:2 * i + 2, :]), tile[:, :], ACT.Copy,
                                     scale=float(P + ROPE) ** -0.5).then_inc(free, 1)
            exps("m", M_s, False)
            take_T4("m_pt", act, M_pT, (0, 2, 4, 6))
            round_T("m_pv", [M_oTh])
            only_split("m_out")
            root("mix1", 2)
            experts(1)

        @block.vector
        def _(dve):
            taken = [0]

            def link(ins):
                taken[0] += 1
                ins.then_inc(dve_step, 1)
                dve.wait_ge(dve_step, taken[0])

            V = nc.vector

            def stats(name, rows, centered):
                k = 0
                parts = []
                for r in rows:
                    n = r.shape[1]
                    m = -(-n // 512)
                    for q in range(m):
                        last = V.bn_stats(st[:, k + q, :], r[:, q * (n // m):(q + 1) * (n // m)])
                    parts.append((k, m))
                    k += m
                link(last)
                for i, (k, m) in enumerate(parts):
                    last = V.bn_aggr(mv[:, i, :], st[:, k:k + m, :].rearrange("p a b -> p (a b)"))
                link(last)
                n = len(rows)
                if centered:
                    V.tensor_scalar(rstd[:, 0:n], mv[:, 0:n, 1], EPS, None, ALU.add).then_inc(sem(f"var_{name}"), 1)
                else:
                    link(V.tensor_tensor(rstd[:, 0:n], mv[:, 0:n, 0], mv[:, 0:n, 0], ALU.mult))
                    V.scalar_tensor_tensor(rstd[:, 0:n], rstd[:, 0:n], EPS, mv[:, 0:n, 1], ALU.add,
                                           ALU.add).then_inc(sem(f"var_{name}"), 1)
                dve.wait_ge(sem(f"std_{name}"), 1)
                link(V.reciprocal(rstd[:, 0:n], rstd[:, 0:n]))

            def layer_norm(name, count):
                stats(name, [h[:, b, :] for b in range(NB)], True)
                for b in range(NB):
                    last = V.tensor_scalar(h[:, b, :], h[:, b, :], mv[:, b, 0:1], rstd[:, b:b + 1], ALU.subtract, ALU.mult)
                link(last)
                dve.wait_ge(sem("lnw_loaded"), 16 * count)
                for b in range(NB):
                    last = V.tensor_tensor(h[:, b, :], h[:, b, :], lnw[:, 0, :], ALU.mult)
                link(last)
                for b in range(NB):
                    V.tensor_tensor(h[:, b, :], h[:, b, :], lnw[:, 1, :], ALU.add).then_inc(sem(f"h_{name}"), 1)
                dve.wait_ge(sem(f"h_{name}"), NB)

            def normed(name, dst, src):
                for b in range(NB):
                    V.tensor_scalar(dst[:, b, :], src[:, b, :], rstd[:, b:b + 1], None, ALU.mult).then_inc(sem(name), 1)

            def rest_T(stage, to, scale=None, tiles=4):
                for i in range(tiles):
                    tile, free = x_tile(dve, stage, i)
                    dve.wait_ge(sem(f"rounded_{stage}"), i + 1)
                    for (hi, lo), g in zip(to, scale or [None]):
                        if g is None:
                            last = V.tensor_tensor(flat(lo[:, 2 * i:2 * i + 2, :]), tile[:, :],
                                                   flat(hi[:, 2 * i:2 * i + 2, :]), ALU.subtract)
                            continue
                        for a in range(min(2, lo.shape[1] - 2 * i)):
                            last = V.scalar_tensor_tensor(lo[:, 2 * i + a, :], tile[:, a * T:(a + 1) * T],
                                                          col(g, 2 * i + a), hi[:, 2 * i + a, :], ALU.mult, ALU.subtract)
                    last.then_inc(free, 1)

            def split(hi, lo, x):
                link(V.tensor_copy(hi, x))
                return V.tensor_tensor(lo, x, hi, ALU.subtract)

            def take_T(stage, dst, tiles=(1, 3)):
                for i in tiles:
                    tile, free = x_tile(dve, stage, i)
                    V.tensor_copy(flat(dst[:, 2 * i:2 * i + 2, :]), tile[:, :]).then_inc(free, 1)

            def rotate(x, n, table, tmp, done):
                t = [tmp[:, q * (NB * n * 32):(q + 1) * (NB * n * 32)].rearrange("p (b n f) -> p b n f", b=NB, n=n)
                     for q in range(4)]
                x1, x2 = x[:, :, :, 0:32], x[:, :, :, 32:64]
                cos, sin = bc(table[:, :, 0, :], 2, n), bc(table[:, :, 1, :], 2, n)
                V.tensor_tensor(t[0], x1, cos, ALU.mult)
                V.tensor_tensor(t[1], x2, sin, ALU.mult)
                V.tensor_tensor(t[2], x2, cos, ALU.mult)
                link(V.tensor_tensor(t[3], x1, sin, ALU.mult))
                V.tensor_tensor(x1, t[0], t[1], ALU.subtract)
                V.tensor_tensor(x2, t[2], t[3], ALU.add).then_inc(done, 1)

            def softmax(name, s, sinks):
                link(V.tensor_reduce(mx[:, :], s, AX.X, ALU.max))
                if sinks:
                    link(V.tensor_tensor(mx[:, :], mx[:, :], B_sink, ALU.max))
                    V.tensor_tensor(esink[:, :], B_sink, mx[:, :], ALU.subtract)
                V.tensor_scalar(negm[:, :], mx[:, :], -1.0, None, ALU.mult).then_inc(sem(f"max_{name}"), 1)
                dve.wait_ge(sem(f"exp_{name}"), 1)
                if sinks:
                    link(V.tensor_tensor(rsum[:, :], rsum[:, :], esink[:, :], ALU.add))
                link(V.reciprocal(rden[:, :], rsum[:, :]))
                for u in range(16):
                    last = V.tensor_scalar(s[:, u, :], s[:, u, :], rden[:, u:u + 1], None, ALU.mult)
                last.then_inc(sem(f"p_{name}"), 1)

            hT = (hT_hi, hT_lo)

            dve.wait_ge(sem("x_loaded"), 16)
            stats("a", [h[:, b, :] for b in range(NB)], False)
            normed("xs_a", xs, h)
            dve.wait_ge(sem("cols_loaded"), 16)
            rest_T("a_tr", [hT], ["a_g"])
            dve.wait_ge(sem("pos_loaded"), 32)
            dve.wait_ge(sem("rows_loaded"), 16 * 8)
            V.tensor_copy(R_a[:, 1, 0:T], pos_i[:, :])
            link(V.tensor_copy(mx[:, 0:NB], posc_i[:, :]))
            V.tensor_scalar(R_a[:, 0, 0:T], R_a[:, 1, 0:T], col("invf", 0), None, ALU.mult)
            for b in range(NB):
                last = V.tensor_scalar(R_a[:, 0, T + 32 * b:T + 32 * b + 32], R_invf, mx[:, b:b + 1], None, ALU.mult)
            link(last)
            link(V.tensor_scalar(R_a[:, 1, :], R_a[:, 0, :], 1.0 / (2 * np.pi), 12582912.0, ALU.mult, ALU.add))
            link(V.tensor_scalar(R_a[:, 1, :], R_a[:, 1, :], 12582912.0, None, ALU.subtract))
            src = 0
            for part in (6.28125, 0.0019350051879882812, 3.019916050561733e-07):
                link(V.scalar_tensor_tensor(R_a[:, 2, :], R_a[:, 1, :], -part, R_a[:, src, :], ALU.mult, ALU.add))
                src = 2
            link(V.tensor_scalar(R_a[:, 3, :], R_a[:, 2, :], np.pi / 2, None, ALU.add))
            link(V.tensor_scalar(R_a[:, 1, :], R_a[:, 3, :], np.pi, -2 * np.pi, ALU.is_gt, ALU.mult))
            link(V.tensor_tensor(R_a[:, 3, :], R_a[:, 3, :], R_a[:, 1, :], ALU.add))
            V.tensor_scalar(R_a[:, 2:4, :], R_a[:, 2:4, :], 3.1415925, -3.1415925, ALU.min, ALU.max
                            ).then_inc(sem("angles"), 1)
            dve.wait_ge(sem("decay_exp"), 1)
            V.tensor_scalar(R_lg[:, 1, :], R_lg[:, 0, :], -1.0, 1.0, ALU.mult, ALU.add).then_inc(sem("one_minus"), 1)
            dve.wait_ge(sem("one_minus"), 1)
            link(V.tensor_scalar(R_lg[:, 3, :], R_lg[:, 1, :], -1.0, None, ALU.add))
            link(V.tensor_scalar(R_lg[:, 4, :], R_lg[:, 3, :], 0.0, None, ALU.is_equal))
            link(V.tensor_tensor(R_lg[:, 3, :], R_lg[:, 3, :], R_lg[:, 4, :], ALU.add))
            link(V.reciprocal(R_lg[:, 5, :], R_lg[:, 3, :]))
            dve.wait_ge(sem("decay_ln"), 1)
            link(V.tensor_tensor(R_lg[:, 5, :], R_lg[:, 5, :], R_lg[:, 2, :], ALU.mult))
            link(V.tensor_tensor(R_lg[:, 5, :], R_lg[:, 5, :], R_lg[:, 4, :], ALU.add))
            link(V.scalar_tensor_tensor(R_lg[:, 5, :], R_lg[:, 0, :], -1.0, R_lg[:, 5, :], ALU.mult, ALU.mult))

            for j, n in fours(dve, 8):
                if j % 2:
                    tile, free = g_tile(dve, "a_v", j, n)
                    V.tensor_copy(A_v[:, :, at(n, 256)], tile[:, :].rearrange("p (b n) -> p b n", b=NB)).then_inc(free, 1)
            g_read(dve, "a_v")
            stats("vn", [A_v[:, b, :] for b in range(NB)], True)
            for b in range(NB):
                last = V.tensor_scalar(A_v[:, b, :], A_v[:, b, :], mv[:, b, 0:1], rstd[:, b:b + 1], ALU.subtract, ALU.mult)
            link(last)
            for b in range(NB):
                last = V.tensor_tensor(A_v[:, b, :], A_v[:, b, :], A_lng, ALU.mult)
            link(last)
            for b in range(NB):
                last = V.tensor_tensor(A_v[:, b, :], A_v[:, b, :], A_lnb, ALU.add)
            last.then_inc(sem("vn_ready"), 1)
            for j, n in fours(dve, 8):
                if j % 2:
                    tile, free = g_tile(dve, "a_u", j, n)
                    V.tensor_copy(flat(A_u)[:, at(n, 512)], tile[:, :]).then_inc(free, 1)
            g_read(dve, "a_u")
            for i in range(8):
                tile, free = x_tile(dve, "a_sv", i)
                y = A_y[:, 2 * i:2 * i + 2, :].rearrange("p a (b t) -> p a b t", b=NB)
                V.tensor_tensor(y, tile[:, :].rearrange("p (a b t) -> p a b t", a=2, b=NB),
                                bc(A_bs[:, 2 * i:2 * i + 2, :], 2, NB), ALU.add).then_inc(free, 1)
                x_read(dve, "a_sv", i)
                last = V.tensor_tensor(flat(A_y[:, 2 * i:2 * i + 2, :]), flat(A_y[:, 2 * i:2 * i + 2, :]),
                                       flat(A_u[:, 2 * i:2 * i + 2, :]), ALU.mult)
            link(last)
            for i in range(8):
                s = SLAB0["a_g"] + i
                dve.wait_ge(g_free[s % 4], tiles_before(s) + 1)
                two = slice(2 * i, 2 * i + 2)
                link(V.tensor_tensor(flat(A_y[:, two, :]), flat(A_y[:, two, :]), flat(A_g[:, two, :]), ALU.mult))
                split(flat(A_yh[:, two, :]), flat(A_yl[:, two, :]), flat(A_y[:, two, :])).then_inc(sem("a_y_ready"), 1)

            def add_out(stage, alpha, pairs=False):
                for j, n in fours(dve, SLABS[stage]):
                    if pairs and j % 2 == 0:
                        continue
                    tile, free = g_tile(dve, stage, j, n)
                    if pairs:
                        cols256 = (slice(n // 2 * 256, (n // 2 + 1) * 256) if isinstance(n, int)
                                   else bass.ds((n - 1) * 128, 256))
                    else:
                        cols256 = at(n, 256)
                    V.scalar_tensor_tensor(h[:, :, cols256], h[:, :, cols256], alpha,
                                           tile[:, :].rearrange("p (b n) -> p b n", b=NB),
                                           ALU.mult, ALU.add).then_inc(free, 1)
                g_read(dve, stage)

            add_out("a_out", 1.0, pairs=True)

            stats("b", [h[:, b, :] for b in range(NB)], False)
            normed("xs_b", xs, h)
            rest_T("b_tr", [hT, (hKV_hi, hKV_lo)], ["b_g", "kv_g"])
            tile, free = g_tile(dve, "b_kv", 0, 0)
            V.tensor_tensor(B_kv, tile[:, :].rearrange("p (b n) -> p b n", b=NB), bc(B_bkv, 1, NB),
                            ALU.add).then_inc(free, 1)
            g_read(dve, "b_kv")
            dve.wait_ge(sem("rope_loaded"), 16)
            k4 = B_kv[:, :, 0:P].rearrange("p b (g d) -> p b g d", g=KVH)
            rotate(k4, KVH, B_rope, TMP, sem("k_rot"))
            dve.wait_ge(sem("k_rot"), 1)
            for a in range(2):
                last = V.tensor_copy(B_kdup[:, :, :, a, :], k4)
            last.then_inc(sem("k_rotated"), 1)
            dve.wait_ge(sem("pads_zero"), 3)
            V.tensor_copy(B_vz[:, :, :, 64:128], B_kv[:, :, P:2 * P].rearrange("p b (g d) -> p b g d", g=KVH)
                          ).then_inc(sem("vz_ready"), 1)
            for i in range(4):
                tile, free = g_tile(dve, "b_q", i, i)
                link(V.tensor_tensor(B_q[:, :, i * 256:(i + 1) * 256], tile[:, :].rearrange("p (b n) -> p b n", b=NB),
                                     bc(B_bq[:, i * 256:(i + 1) * 256], 1, NB), ALU.add))
                dve.sem_inc(free, 1)
                rotate(B_q[:, :, i * 256:(i + 1) * 256].rearrange("p b (n d) -> p b n d", n=4), 4, B_rope, TMP,
                       sem("q_rotated"))
                dve.wait_ge(sem("q_rotated"), i + 1)
            take_T("b_qtr", B_qT)
            dve.wait_ge(sem("b_mask_ready"), 1)
            for i in range(4):
                tile, free = x_tile(dve, "b_s0", i)
                V.scalar_tensor_tensor(B_s0[:, 4 * i:4 * i + 4, :], tile[:, :].rearrange("p (a k) -> p a k", a=4),
                                       DH ** -0.5, bc(B_mask[:, P:], 1, 4), ALU.mult, ALU.add).then_inc(free, 1)
            for i in range(8):
                tile, free = x_tile(dve, "b_s1", i)
                V.scalar_tensor_tensor(B_s1[:, 2 * i:2 * i + 2, :], tile[:, :].rearrange("p (a k) -> p a k", a=2),
                                       DH ** -0.5, bc(B_mask, 1, 2), ALU.mult, ALU.add).then_inc(free, 1)
            x_read(dve, "b_s1")
            softmax("b0", B_s0, True)
            take_T4("b_pt0", dve, B_pT0, (1, 3))
            softmax("b1", B_s1, True)
            take_T4("b_pt1", dve, B_pT1, (1, 3, 5, 7))
            g_read(dve, "b_g")
            for b in range(NB):
                for i in range(2):
                    tile, free = x_tile(dve, f"b_pv{b}", i)
                    V.tensor_tensor(B_yT[:, 4 * i:4 * i + 4, b * P:(b + 1) * P],
                                    tile[:, :].rearrange("p (a t) -> p a t", a=4),
                                    B_gT[:, 4 * i:4 * i + 4, b * P:(b + 1) * P], ALU.mult).then_inc(free, 1)
            x_read(dve, "b_pv0")
            x_read(dve, "b_pv1")
            split(flat(B_yh), flat(B_yl), flat(B_yT)).then_inc(sem("b_y_ready"), 1)
            add_out("b_out", 1.0)
            stats("fin", [h[:, b, :] for b in range(NB)], False)
            dve.wait_ge(sem("lnw_loaded"), 16)
            for b in range(NB):
                V.scalar_tensor_tensor(h[:, b, :], h[:, b, :], rstd[:, b:b + 1], fin_g, ALU.mult,
                                       ALU.mult).then_inc(sem("h_b"), 1)
            dve.wait_ge(sem("h_b"), 2)

            rest_T("r_tr", [hT])
            dve.wait_ge(sem("diff_loaded"), 16)
            for i in range(RET_H):
                link(V.tensor_scalar(R_D[:, i, :], R_diff[:, 0, :], R_lg[:, 5, i:i + 1], None, ALU.mult))
                V.scalar_tensor_tensor(R_D[:, i, :], R_diff[:, 1, :], R_lg[:, 5, 4 + i:5 + i], R_D[:, i, :], ALU.mult,
                                       ALU.add).then_inc(sem("decay_arg"), 1)
            dve.wait_ge(sem("rotary_ready"), 1)
            for i in range(8):
                tile, free = g_tile(dve, "r_qk", i, i)
                halves = tile[:, :].rearrange("p (a t) -> p a t", a=2)
                V.tensor_tensor(R_tmp[:, 0, :].rearrange("p (a t) -> p a t", a=2), halves, bc(cosT, 1, 2), ALU.mult)
                V.tensor_tensor(R_tmp[:, 1, :].rearrange("p (a t) -> p a t", a=2), halves, bc(sinT, 1, 2),
                                ALU.mult).then_inc(free, 1)
                s = SLAB0["r_qk"] + i
                dve.wait_ge(free, tiles_before(s) + 1)
                V.tensor_tensor(R_qk[:, 2 * i, :], R_tmp[:, 0, 0:T], R_tmp[:, 1, T:], ALU.subtract)
                link(V.tensor_tensor(R_qk[:, 2 * i + 1, :], R_tmp[:, 0, T:], R_tmp[:, 1, 0:T], ALU.add))
            dve.sem_inc(sem("r_qk_ready"), 8)
            for i in range(RET_H):
                tile, free = x_tile(dve, "r_s", i)
                dve.wait_ge(sem("decay_ready"), i + 1)
                V.scalar_tensor_tensor(flat(R_s[:, i, :, :]), tile[:, :], RET_DK ** -0.5, R_D[:, i, :], ALU.mult,
                                       ALU.mult).then_inc(free, 1)
            x_read(dve, "r_y")
            groups = [R_y[:, i % 2, (i // 2) * RET_DV:(i // 2 + 1) * RET_DV] for i in range(8)]
            stats("gn", groups, True)
            for i, g in enumerate(groups):
                last = V.tensor_scalar(g, g, mv[:, i, 0:1], rstd[:, i:i + 1], ALU.subtract, ALU.mult)
            last.then_inc(sem("r_yn_ready"), 1)
            g_read(dve, "r_g")
            for i in range(8):
                tile, free = x_tile(dve, "r_yt", i)
                for a in range(2):
                    c = 2 * i + a
                    last = V.tensor_scalar(R_yT[:, c, :], tile[:, a * T:(a + 1) * T], col("gn_g", c), col("gn_b", c),
                                           ALU.mult, ALU.add)
                last.then_inc(free, 1)
                x_read(dve, "r_yt", i)
                two = slice(2 * i, 2 * i + 2)
                link(V.tensor_tensor(flat(R_yT[:, two, :]), flat(R_yT[:, two, :]), flat(R_g[:, two, :]), ALU.mult))
                split(flat(R_yh[:, two, :]), flat(R_yl[:, two, :]), flat(R_yT[:, two, :])).then_inc(sem("r_y_ready"), 1)
            add_out("r_out", ALPHA, pairs=True)
            layer_norm("mix0", 3)

            def top16(src, best, index):
                n = len(src)
                for k in range(2):
                    for i in range(n):
                        last = V.max(best[:, i, 8 * k:8 * k + 8], src[i])
                    link(last)
                    for i in range(n):
                        last = V.max_index(index[:, i, 8 * k:8 * k + 8], best[:, i, 8 * k:8 * k + 8], src[i])
                    link(last)
                    if k == 0:
                        for i in range(n):
                            last = V.match_replace(src[i], best[:, i, 0:8], src[i], LOWEST)
                        link(last)

            def experts(l):
                rest_T(f"p_tr{l}", [hT])
                for b in range(NB):
                    for i in range(4):
                        x_read(dve, f"p_s{l}", 4 * b + i)
                    top16([K_s[:, b, i, :] for i in range(16)], K_top, K_iu)
                    V.tensor_copy(K_if, K_iu)
                    tops = K_top.rearrange("p (n c) k -> p n c k", c=2)
                    link(V.tensor_tensor(K_cand.rearrange("p n (a b) -> p n a b", a=16), bc(tops[:, :, 0, :], 3, 16),
                                         bc(tops[:, :, 1, :], 2, 16), ALU.add))
                    top16([K_cand[:, i, :] for i in range(PK_H)], K_ts, K_pu)
                    index = K_if.rearrange("p (n c) k -> p n c k", c=2)
                    x_tile(dve, f"p_s{l}", 7)
                    for c, (op, amount) in enumerate([(ALU.logical_shift_right, 4), (ALU.bitwise_and, 15)]):
                        link(V.tensor_scalar(K_au, K_pu, amount, None, op))
                        link(V.tensor_copy(K_af, K_au))
                        link(V.tensor_tensor(K_eq, bc(K_af, 3, 16), bc(bc(iota[:, 0:16], 1, 16), 1, PK_H), ALU.is_equal))
                        link(V.tensor_tensor(K_eq, K_eq, bc(index[:, :, c, :], 2, 16), ALU.mult))
                        link(V.tensor_reduce(picks[:, b, c, :].rearrange("p (n k) -> p n k", k=TOPK), K_eq, AX.X, ALU.add))
                    gate = picks[:, b, 2, :].rearrange("p (n k) -> p n k", k=TOPK)
                    V.tensor_tensor(gate, K_ts, K_ts[:, :, 0:1].broadcast_to([P, PK_H, TOPK]), ALU.subtract
                                    ).then_inc(sem(f"top{l}"), 1)
                    dve.wait_ge(sem(f"top{l}"), b + 1)
                for b in range(NB):
                    gate = picks[:, b, 2, :].rearrange("p (n k) -> p n k", k=TOPK)
                    dve.wait_ge(sem(f"gates{l}"), b + 1)
                    link(V.tensor_reduce(K_sum, gate, AX.X, ALU.add))
                    link(V.reciprocal(K_sum, K_sum))
                    V.tensor_tensor(gate, gate, bc(K_sum, 2, TOPK), ALU.mult).then_inc(sem(f"picks{l}"), 1)
                    dve.wait_ge(sem(f"picks{l}"), b + 1)
                x_tile(dve, f"p_kt{l}", 1)
                for b in range(NB):
                    tile, free = x_tile(dve, f"p_kt{l}", b)
                    V.tensor_copy(picksT[:, :, b * P:(b + 1) * P], tile[:, 0:3 * P].rearrange("p (a t) -> p a t", a=3)
                                  ).then_inc(free, 1)
                x_read(dve, f"p_kt{l}")
                g_read(dve, f"u{l}")
                w0 = X0[f"p_w{l}"]
                experts_by_token = big[:, :].rearrange("p (i t) -> p i t", t=T)

                def hot2(j, token):
                    for q in range(4):
                        t = bass.ds(token + q, 1) if not isinstance(token, int) else slice(token + q, token + q + 1)
                        last = V.tensor_scalar(hot[:, 1, j, q, :], iota[:, :], picksT[:, 1, t], picksT[:, 2, t],
                                               ALU.is_equal, ALU.mult)
                    last.then_inc(sem(f"hot2_{l}"), 1)

                def gate_group(x, token, rounds):
                    t = bass.ds(token, 4) if not isinstance(token, int) else slice(token, token + 4)
                    dve.wait_ge(x_full, rounds + (x + 1))
                    V.tensor_tensor(experts_by_token[:, :, t], X[x % 4][:, :].rearrange("p (q i) -> p i q", q=4),
                                    experts_by_token[:, :, t], ALU.mult).then_inc(x_free[x % 4], 1)

                for j in range(HOT):
                    hot2(j, 4 * j)
                with dve.Fori(0, T // 16 - 1) as it:
                    for j in range(4):
                        gate_group(w0 + j, it * 16 + 4 * j, it * 4)
                        hot2(j, it * 16 + (4 * j + 16))
                for j in range(4):
                    gate_group(w0 + T // 4 - 4 + j, T - 16 + 4 * j, 0)
                s0 = SLAB0[f"v{l}"]

                def gated(j, key):
                    x = big[:, at(key, T)]
                    V.tensor_copy(hT_hi[:, j, :], x).then_inc(sem(f"gated_hi{l}"), 1)
                    dve.wait_ge(sem(f"gated_hi{l}"), key + 1)
                    V.tensor_tensor(hT_lo[:, j, :], x, hT_hi[:, j, :], ALU.subtract).then_inc(sem(f"gated_split{l}"), 1)

                x_read(dve, f"p_w{l}")
                for j in range(4):
                    gated(j, j)
                with dve.Fori(1, 32) as it:
                    for j in range(4):
                        dve.wait_ge(half_done, it * 4 + (2 * s0 + j - 3))
                        gated(j, it * 4 + j)
                take_T(f"p_y{l}", K_yT)
                for i in range(4):
                    tile, free = x_tile(dve, f"p_yr{l}", i)
                    part = h[:, i // 2, (i % 2) * 512:(i % 2 + 1) * 512]
                    V.scalar_tensor_tensor(part, part, ALPHA, tile[:, :], ALU.mult, ALU.add).then_inc(free, 1)
                x_read(dve, f"p_yr{l}")
                layer_norm(f"ffn{l}", 5 if l == 0 else 9)

            experts(0)

            rest_T("m_tr", [hT])
            g_read(dve, "m_in")
            latents = [M_c[:, b, a:z] for a, z in ((0, Q_RANK), (Q_RANK, Q_RANK + KV_RANK)) for b in range(NB)]
            stats("cn", latents, False)
            for i, (a, z) in enumerate(((0, Q_RANK), (Q_RANK, Q_RANK + KV_RANK))):
                for b in range(NB):
                    last = V.tensor_scalar(M_cn[:, b, a:z], M_c[:, b, a:z], rstd[:, 2 * i + b:2 * i + b + 1], None,
                                           ALU.mult)
            last.then_inc(sem("cn_ready"), 1)
            kr = M_c[:, :, 640:704].unsqueeze(2)
            rotate(kr, 1, rope_row, M_tmp, sem("kr_rot"))
            dve.wait_ge(sem("kr_rot"), 1)
            for a in range(2):
                last = V.tensor_copy(M_kr[:, :, a, :], M_c[:, :, 640:704])
            last.then_inc(sem("kr_rotated"), 1)
            rest_T("m_ct", [(M_cTh, M_cTl)], ["m_qg"], 3)
            for i in range(2):
                tile, free = g_tile(dve, "m_qr", i, i)
                link(V.tensor_copy(M_qr[:, :, i * 256:(i + 1) * 256], tile[:, :].rearrange("p (b n) -> p b n", b=NB)))
                dve.sem_inc(free, 1)
                rotate(M_qr[:, :, i * 256:(i + 1) * 256].rearrange("p b (n d) -> p b n d", n=4), 4, rope_row, M_tmp,
                       sem("mq_rotated"))
                dve.wait_ge(sem("mq_rotated"), i + 1)
            take_T("m_qrt", M_qrT, (0, 1))
            x_read(dve, "m_s")
            softmax("m", M_s, False)
            take_T4("m_pt", dve, M_pT, (1, 3, 5, 7))
            rest_T("m_pv", [(M_oTh, M_oTl)])
            add_out("m_out", ALPHA)
            layer_norm("mix1", 7)
            experts(1)

        @block.gpsimd
        def _(pool):
            taken = [0]

            def link(ins):
                taken[0] += 1
                ins.then_inc(pool_step, 1)
                pool.wait_ge(pool_step, taken[0])

            Q = nc.gpsimd

            link(Q.memset(ident[:, :], 0.0))
            Q.affine_select(out=ident[:, :], in_=ident[:, :], compare_op=ALU.not_equal, fill=1.0, base=0,
                            pattern=[[-1, P]], channel_multiplier=1).then_inc(sem("ident_ready"), 1)
            link(Q.iota(iota_i[:, :], pattern=[[1, P]], base=0, channel_multiplier=0))
            Q.tensor_copy(iota[:, :], iota_i[:, :]).then_inc(sem("ident_ready"), 1)

            def split(first, last):
                def one(s, r):
                    j = s % 2
                    for half in range(2):
                        pool.wait_ge(hi_ready, r * 8 + (2 * s + half + 1))
                        Q.tensor_tensor(w_lo[:, 2 * j + half, :], ring[j][:, half * 1024:(half + 1) * 1024],
                                        w_hi[:, 2 * j + half, :], ALU.subtract).then_inc(split_ready, 1)

                n = (last - first) // 4
                if n > 1:
                    with pool.Fori(0, n) as it:
                        for j in range(4):
                            one(first + j, it)
                    first += 4 * n
                for s in range(first, last):
                    one(s, 0)

            pool.wait_ge(sem("ws_loaded"), 16)
            Q.affine_select(out=A_ws, in_=A_ws, compare_op=ALU.is_ge, fill=0.0, base=0,
                            pattern=[[0, 16], [1, P]], channel_multiplier=-1).then_inc(sem("ws_masked"), 1)
            link(Q.memset(B_mask, 0.0))
            link(Q.affine_select(out=B_mask, in_=B_mask, compare_op=ALU.is_ge, fill=NEG, base=-1,
                                 pattern=[[1, T]], channel_multiplier=-1))
            Q.affine_select(out=B_mask, in_=B_mask, compare_op=ALU.is_ge, fill=NEG, base=P,
                            pattern=[[-1, T]], channel_multiplier=1).then_inc(sem("b_mask_ready"), 1)
            pool.wait_ge(sem("b_mask_ready"), 1)
            split(0, SLAB0["b_kv"] + RING)
            pool.wait_ge(half_done, 2 * SLAB0["b_kv"])
            pool.wait_ge(split_ready, 2 * (SLAB0["b_kv"] + RING))
            for i, (a, part) in enumerate(((B_kTe, slice(64, P)), (B_kTo, slice(0, 64)), (B_vz, slice(0, P)))):
                Q.memset(flat(a)[part, :], 0.0).then_inc(sem("pads_zero"), 1)
                pool.wait_ge(sem("pads_zero"), i + 1)
            split(SLAB0["b_kv"] + RING, SLAB0["v0"] + RING)

            def experts(l):
                x_read(pool, f"p_kt{l}")
                w0 = X0[f"p_w{l}"]

                def hot1(j, group):
                    t = bass.ds(group * 4 + 2, 2) if not isinstance(group, int) else slice(group * 4 + 2, group * 4 + 4)
                    Q.tensor_copy(key1[:, j % 2, 2:4], picksT[:, 0, t]).then_inc(sem(f"key1_{l}"), 1)
                    pool.wait_ge(sem(f"key1_{l}"), group + 1)
                    pool.sem_inc(sem(f"key1_seen{l}"), 1)
                    for q in (2, 3):
                        last = Q.tensor_scalar(hot[:, 0, j, q, :], iota[:, :], key1[:, j % 2, q:q + 1], None,
                                               ALU.is_equal)
                    last.then_inc(sem(f"hot1b_{l}"), 1)

                for j in range(HOT):
                    hot1(j, j)
                with pool.Fori(1, T // 16) as it:
                    for j in range(4):
                        pool.wait_ge(x_full, it * 4 + (w0 + j - 3))
                        hot1(j, it * 4 + j)

            experts(0)
            split(SLAB0["v0"] + RING, SLAB0["m_in"] + RING)
            pool.wait_ge(half_done, 2 * SLAB0["m_in"])
            pool.wait_ge(split_ready, 2 * (SLAB0["m_in"] + RING))
            for i, (a, part) in enumerate(((M_krTe, slice(64, P)), (M_krTo, slice(0, 64)))):
                Q.memset(a[part, :], 0.0).then_inc(sem("pads_zero"), 1)
                pool.wait_ge(sem("pads_zero"), i + 4)
            split(SLAB0["m_in"] + RING, SLAB0["v1"] + RING)
            experts(1)
            split(SLAB0["v1"] + RING, N_SLABS)


def kernel(**inputs):
    import concourse.bacc as bacc
    from concourse.bass_utils import run_bass_kernel_spmd

    a = {k: np.asarray(v) for k, v in inputs.items()}
    f32 = np.float32

    def halves(s):
        n, _, k, width = s.shape
        out = np.zeros((n, P, 2, 1024), f32)
        kh = (k + 1) // 2
        out[:, :, 0, :kh * width] = s[:, :, :kh].reshape(n, P, -1)
        out[:, :, 1, :(k - kh) * width] = s[:, :, kh:].reshape(n, P, -1)
        return out.reshape(n, P, 2048)

    def slabs_of(w):
        k, n = w.shape
        chunks = min(DC, k // P)
        s = w.reshape(k // (P * chunks), chunks, P, n // 256, 256).transpose(3, 0, 2, 1, 4)
        return halves(s.reshape(-1, P, chunks, 256))

    w_in = a["a_w_in"][0]
    b_in = a["b_w_in"][0]
    ret = a["ret_w_in_2"][0]
    uq = a["mla_w_uq_2"][0].reshape(Q_RANK, MLA_H, P + ROPE)
    mla_in = np.pad(a["mla_w_in_2"][0], ((0, 0), (0, 64)))

    def u_slabs(l):
        return slabs_of(a["peer_u_2"][l].T)

    def v_slabs(l):
        return a["peer_v_2"][l].reshape(64, 2, P, D).transpose(0, 2, 1, 3).reshape(64, P, 2048)

    stages = {
        "a_v": slabs_of(w_in[:, W_A:2 * W_A]), "a_u": slabs_of(w_in[:, :W_A]),
        "a_g": slabs_of(w_in[:, 2 * W_A:]), "a_out": slabs_of(a["a_w_out"][0]),
        "b_kv": slabs_of(a["w_kv"]), "b_q": slabs_of(b_in[:, :D]), "b_g": slabs_of(b_in[:, D:]),
        "b_out": slabs_of(a["b_w_out"][0]),
        "r_qk": slabs_of(ret[:, :2048]), "r_v": slabs_of(ret[:, 2048:4096]),
        "r_g": slabs_of(ret[:, 4096:]), "r_out": slabs_of(a["ret_w_out_2"][0]),
        "m_in": slabs_of(mla_in), "m_qn": slabs_of(uq[:, :, :P].reshape(Q_RANK, -1)),
        "m_qr": slabs_of(uq[:, :, P:].reshape(Q_RANK, -1)), "m_kv": slabs_of(a["mla_w_ukv_2"][0]),
        "m_out": slabs_of(a["mla_w_out_2"][0]),
    }
    slabs = np.empty((N_SLABS, P, 2048), f32)
    for name, n in SLAB_STAGES:
        if name[0] in "uv" and name[1] in "01":
            part = (u_slabs if name[0] == "u" else v_slabs)(int(name[1]))
        elif name.startswith("pq"):
            part = slabs_of(a["peer_w_q_2"][int(name[2])])
        else:
            part = stages[name]
        assert part.shape[0] == n, name
        slabs[SLAB0[name]:SLAB0[name] + n] = part

    def inv_freq(dh):
        return (np.float32(10000.0) ** (-np.arange(0, dh, 2, dtype=f32) / np.float32(dh))).astype(f32)

    angle = np.arange(T, dtype=f32)[:, None] * inv_freq(DH)[None, :]
    rope = np.stack([np.cos(angle), np.sin(angle)], 1).astype(f32).reshape(NB, P, 64).transpose(1, 0, 2).reshape(P, P)
    m, n = np.arange(T)[:, None], np.arange(T)[None, :]
    diff = np.stack([np.maximum(n - m, 0), np.maximum(m - n, 0)]).astype(f32)
    diff = diff.reshape(2, NB, P, T).transpose(2, 0, 1, 3).reshape(P, 1024)

    def columns(v):
        return v.reshape(-1, P).T

    cols = np.concatenate([columns(a["a_norm_g"]), columns(a["kv_norm_g"]), columns(a["b_norm_g"]),
                           columns(a["ret_gn_g_2"]), columns(a["ret_gn_b_2"]), columns(a["mla_q_norm_2"]),
                           columns(a["mla_kv_norm_2"]), inv_freq(RET_DK)[:, None]], 1)

    def pair(w, b, l):
        return np.concatenate([a[w][l], a[b][l]])

    row_parts = {
        "ln_g": a["a_ln_g"], "ln_b": a["a_ln_b"], "bs": a["a_bs"], "bq": a["b_bq"], "bkv": a["b_kv"],
        "sinks": a["b_sinks"], "decay": a["ret_log1m_decay_2"], "invf_row": inv_freq(ROPE), "fin_g": a["final_norm_g"],
        "mix0": pair("ln_mix_g_2", "ln_mix_b_2", 0), "ffn0": pair("ln_ffn_g_2", "ln_ffn_b_2", 0),
        "mix1": pair("ln_mix_g_2", "ln_mix_b_2", 1), "ffn1": pair("ln_ffn_g_2", "ln_ffn_b_2", 1),
    }
    rows = np.concatenate([row_parts[name].ravel() for name, _ in ROWS])[None, :]
    pos = a["positions_2"].reshape(T)
    arrays = {
        "slabs": slabs,
        "x": a["x"].reshape(T, D),
        "cols": cols,
        "rows": rows,
        "ws": a["a_ws"][0].transpose(2, 0, 1).reshape(P, 16 * P),
        "keys": a["peer_sub_keys_2"].reshape(2, 16, NKEYS, P).transpose(0, 3, 1, 2).reshape(2, P, 16 * NKEYS),
        "pos_row": pos.reshape(1, T),
        "pos_col": pos.reshape(NB, P).T,
        "rope": rope,
        "diff": diff,
    }
    arrays = {f"{k}_in": np.ascontiguousarray(v) for k, v in arrays.items()}
    nc = bacc.Bacc("TRN2", target_bir_lowering=False, num_devices=1)
    args = [nc.dram_tensor(k, v.shape, mybir.dt.from_np(v.dtype), kind="ExternalInput").ap() for k, v in arrays.items()]
    out = nc.dram_tensor("out", (T, D), mybir.dt.float32, kind="ExternalOutput").ap()
    build(nc, *args, out)
    r = run_bass_kernel_spmd(nc, [arrays], core_ids=[0])
    return r.results[0]["out"].reshape(1, T, D)
```

```python
from contextlib import ExitStack

import numpy as np

import concourse.bass as bass
from concourse import mybir

P = 128
T = 256
NB = T // P
D = 1024
DC = D // P
W_A = 2048
RING = 2
SPLIT = 4
GATED = 28
GROUPS = T // 4
EPS = 1e-5
ALPHA = 4.0 ** 0.25
HEADS_B, KVH, DH = 16, 2, 64
RET_H, RET_DK, RET_DV = 4, 256, 512
MLA_H, Q_RANK, KV_RANK, ROPE = 8, 384, 256, 64
PK_H, NKEYS, TOPK = 8, 128, 16
NEG = -1.0e30
LOWEST = -3.0e38

SLAB_STAGES = [
    ("a_v", 8), ("a_u", 8), ("a_g", 8), ("a_out", 8),
    ("b_kv", 1), ("b_q", 4), ("b_g", 4), ("b_out", 4),
    ("r_qk", 8), ("r_v", 8), ("r_g", 8), ("r_out", 8),
    ("pq0", 8), ("u0", 64), ("v0", 64),
    ("m_in", 3), ("m_q", 3), ("m_kv", 2), ("m_out", 4),
    ("pq1", 8), ("u1", 64), ("v1", 64),
]
UNITS = {"b": 12, "m": 8}
PV_AFTER = {"b": [1, 3, 7, 11], "m": [1, 3, 5, 7]}
AHEAD = 3


def attention_order(name):
    n, out, values = UNITS[name], [], 0
    for k in range(min(AHEAD, n)):
        out.append(("s", k))
    for k in range(n):
        out.append(("t", k))
        while values < len(PV_AFTER[name]) and (PV_AFTER[name][values] < k or k == n - 1):
            out.append(("v", values))
            values += 1
        if k + AHEAD < n:
            out.append(("s", k + AHEAD))
    return out


def attention_stages(name):
    return [(f"{name}_{kind}{k}", 1) for kind, k in attention_order(name)]


X_STAGES = [
    ("a_tr", 4), ("a_sv", 8), ("b_tr", 4), ("b_ktr", 1), ("b_qtr", 4),
    *attention_stages("b"),
    ("r_tr", 4), ("r_s", 4), ("r_y", 8), ("r_yt", 8),
    ("p_tr0", 4), ("p_s0", 8), ("p_kt0", 2), ("p_w0", 64), ("p_y0", 4), ("p_yr0", 4),
    ("m_tr", 4), ("m_ct", 3), ("m_krt", 1), ("m_qr", 2), ("m_qn", 4), ("m_kv", 8), ("m_qrt", 2),
    *attention_stages("m"),
    ("p_tr1", 4), ("p_s1", 8), ("p_kt1", 2), ("p_w1", 64), ("p_y1", 4), ("p_yr1", 4),
]


def first_index(stages):
    at, out = 0, {}
    for name, n in stages:
        out[name] = at
        at += n
    return out, at


SLAB0, N_SLABS = first_index(SLAB_STAGES)
X0, _ = first_index(X_STAGES)
SLABS = dict(SLAB_STAGES)
XTILES = dict(X_STAGES)


def gives_tile(name, n):
    return name not in ("v0", "v1", "m_q", "m_kv") and (name not in ("a_out", "r_out") or n % 2 == 1)


def tiles_before(slab):
    return sum(1 for name, count in SLAB_STAGES for n in range(count)
               if gives_tile(name, n) and SLAB0[name] + n < slab and (SLAB0[name] + n) % 4 == slab % 4)


COLS = [("a_g", 8), ("kv_g", 8), ("b_g", 8), ("gn_g", 16), ("gn_b", 16), ("m_qg", 3), ("m_kvg", 2), ("invf", 1)]
ROWS = [("ln_g", 2048), ("ln_b", 2048), ("bs", 2048), ("bq", 1024), ("bkv", 256), ("sinks", 16),
        ("decay", 8), ("invf_row", 32), ("fin_g", 1024),
        ("mix0", 2048), ("ffn0", 2048), ("mix1", 2048), ("ffn1", 2048)]
COL0, N_COLS = first_index(COLS)
ROW0, N_ROWS = first_index(ROWS)
ROWN = dict(ROWS)


def build(nc, h_kept, slabs, x_in, cols_in, rows_in, ws_in, keys_in, pos_row, pos_col, rope_in, diff_in, out):
    f32, u32, i32 = mybir.dt.float32, mybir.dt.uint32, mybir.dt.int32
    f32r = mybir.dt.float32r
    ALU, ACT, AX = mybir.AluOpType, mybir.ActivationFunctionType, mybir.AxisListType
    ctx = ExitStack()
    with ctx:
        def sb(name, shape, dt=f32):
            return ctx.enter_context(nc.sbuf_tensor(name, shape, dt))

        made = {}

        def sem(name):
            if name not in made:
                made[name] = ctx.enter_context(nc.semaphore(name))
            return made[name]

        def twin(name, shape, dt, other):
            return nc.alloc_sbuf_tensor_at(name, shape, dt, offset=other)

        def here():
            return (nc.sbuf_base + 31) // 32 * 32

        big_at = here()
        big = sb("big", [P, NKEYS * T])
        ring = [sb(f"ring{i}", [P, 2048]) for i in range(RING)]
        w_hi = sb("w_hi", [P, SPLIT, 1024], f32r)
        w_lo = sb("w_lo", [P, SPLIT, 1024], f32r)
        hT_hi = sb("hT_hi", [P, DC, T], f32r)
        hT_lo = sb("hT_lo", [P, DC, T], f32r)
        h_at = here()
        h = sb("h", [P, NB, D])
        hot = twin("hot", [P, 2, 2, 4, NKEYS], f32, h_at)
        ident = sb("ident", [P, P])
        iota = sb("iota", [P, P])
        picksT = sb("picksT", [P, 3, T])
        cols = sb("cols", [P, N_COLS])
        rope_row = sb("rope_row", [P, NB, 2, 32])
        st = sb("st", [P, 8, 6])
        mv = sb("mv", [P, 8, 2])
        rstd = sb("rstd", [P, 8])
        mx = sb("mx", [P, 32])
        negm = sb("negm", [P, 32])
        rsum = sb("rsum", [P, 32])
        esink = sb("esink", [P, 32])
        rden = sb("rden", [P, 32])
        G = [ctx.enter_context(nc.psum_tensor(f"G{i}", [P, 512], f32)) for i in range(4)]
        X = [ctx.enter_context(nc.psum_tensor(f"X{i}", [P, 512], f32)) for i in range(4)]

        def shaped(a, shape):
            if len(shape) == 1:
                return a
            names = "abcd"[:len(shape)]
            return a.rearrange(f"p ({' '.join(names)}) -> p {' '.join(names)}",
                               **dict(zip(names[1:], shape[1:])))

        def area(off, *shape):
            return shaped(big[:, off:off + int(np.prod(shape))], shape)

        def area_r(name, off, *shape):
            return shaped(twin(name, [P, int(np.prod(shape))], f32r, big_at + 4 * off)[:, :], shape)

        def col(name, i):
            return cols[:, COL0[name] + i:COL0[name] + i + 1]

        def bc(ap, axis, n):
            shape = list(ap.shape)
            shape.insert(axis, n)
            return ap.unsqueeze(axis).broadcast_to(shape)

        xs = area(0, NB, D)
        A_v = area(2048, NB, W_A)
        A_u = area(6144, 16, T)
        A_g = area(10240, 16, T)
        A_y = area(14336, 16, T)
        A_lng, A_lnb = area(18432, W_A), area(20480, W_A)
        A_ws = area(22528, 16, P)
        A_bs = area(24576, 16, P)
        A_yh = area_r("A_yh", 6144, 16, T)
        A_yl = area_r("A_yl", 2048, 16, T)
        hKV_hi = area_r("hKV_hi", 26624, DC, T)
        hKV_lo = area_r("hKV_lo", 17152, DC, T)
        fin_g = area(27648, D)
        lnw = area(30720, 2, D)
        B_mask = area(28672, T)
        B_bq, B_bkv = area(30720, D), area(31744, 256)
        B_sink = area(32000, 16)
        B_rope = area(32128, NB, 2, 32)
        R_decay = area(32256, 8)
        B_q = area(2048, NB, D)
        B_kv = area(4096, NB, 256)
        B_kdup = area(4608, NB, KVH, 2, DH)
        B_vz = area(5120, NB, KVH, 192)
        B_qT = area(5888, DC, T)
        B_kTe, B_kTo = area(7936, KVH, T), area(8448, KVH, T)
        B_s0 = area(8960, 16, P)
        B_s1 = area(11008, 16, T)
        B_pT0 = area(15104, 16, P)
        B_pT1 = area(17152, 16, 2, P)
        B_gT = area(21248, DC, T)
        B_yT = area(23296, DC, T)
        B_yh = area_r("B_yh", 0, DC, T)
        B_yl = area_r("B_yl", 2048, DC, T)
        TMP = area(25344, 1280)
        R_qk = area(0, 16, T)
        R_tmp = area(4096, 2, 512)
        R_v = area(5120, NB, 2048)
        R_g = area(9216, 16, T)
        R_D = area(13312, RET_H, 512)
        R_s = area(15360, RET_H, NB, T)
        R_y = area(17408, NB, 2048)
        R_yT = area(21504, 16, T)
        R_yh = area_r("R_yh", 0, 16, T)
        R_yl = area_r("R_yl", 5120, 16, T)
        cosT, sinT = area(28928, T), area(29184, T)
        R_diff = area(26624, 2, 512)
        R_lg = area(32264, 6, 8)
        R_invf = area(32320, 32)
        pos_i = area(26624, T).bitcast(i32)
        posc_i = area(26880, NB).bitcast(i32)
        iota_i = area(26944, P).bitcast(i32)
        M_c = area(0, NB, 768)
        M_cn = area(1536, NB, 640)
        M_cTh = area_r("M_cTh", 2816, 5, T)
        M_cTl = area_r("M_cTl", 24576, 5, T)
        M_kr = area(4096, NB, 2, ROPE)
        M_krTe, M_krTo = area(4352, T), area(4608, T)
        M_qn = area(4864, MLA_H, T)
        M_qr = area(6912, NB, 512)
        M_qrT = area(7936, 4, T)
        M_kn = area(8960, MLA_H, T)
        M_v = area(11008, NB, MLA_H * P)
        M_s = area(13056, 16, T)
        M_pT = area(17152, MLA_H, 2, T)
        M_oTh = area_r("M_oTh", 21248, DC, T)
        M_oTl = area_r("M_oTl", 25856, DC, T)
        M_tmp = area(23296, 1280)
        K_q = area(0, 16, T)
        K_s = area(22528, NB, 16, NKEYS)
        K_cand = area(26624, PK_H, 256)
        K_eq = area(28672, PK_H, TOPK, TOPK)
        keysT = area(28672, 16, NKEYS)
        K_top = area(30720, 16, TOPK)
        K_iu = area(30976, 16, TOPK).bitcast(u32)
        K_if = area(31232, 16, TOPK)
        K_ts = area(31488, PK_H, TOPK)
        K_pu = area(31616, PK_H, TOPK).bitcast(u32)
        K_au = area(31744, PK_H, TOPK).bitcast(u32)
        K_af = area(31872, PK_H, TOPK)
        K_sum = mx[:, 0:PK_H]
        K_yT = area(0, DC, T)
        K_ungated = big[:, GATED * 512:]
        assert GATED * 512 <= 22528 and GROUPS == 2 * 32 and GATED + 32 <= 64
        picks = picksT[:, :, :].rearrange("p a t -> p (a t)").rearrange("p (b a k) -> p b a k", b=NB, a=3)

        units = {"b": [(B_s0[:, 4 * i:4 * i + 4, :], 4 * i) for i in range(4)]
                      + [(B_s1[:, 2 * i:2 * i + 2, :], 16 + 2 * i) for i in range(8)],
                 "m": [(M_s[:, 2 * i:2 * i + 2, :], 2 * i) for i in range(MLA_H)]}

        slab_loaded = [[sem(f"slab_loaded{i}_{half}") for half in range(2)] for i in range(RING)]
        hi_ready = sem("hi_ready")
        split_ready = sem("split_ready")
        half_done = sem("half_done")
        g_free = [sem(f"g_free{i}") for i in range(4)]
        x_full = sem("x_full")
        x_free = [sem(f"x_free{i}") for i in range(4)]
        dve_step, act_step, pool_step = sem("dve_step"), sem("act_step"), sem("pool_step")

        block = ctx.enter_context(nc.Block())

        def fours(eng, n):
            if n % 4 or n < 8:
                for j in range(n):
                    yield j, j
            else:
                with eng.Fori(0, n // 4) as it:
                    for j in range(4):
                        yield j, it * 4 + j

        def at(n, size):
            return bass.ds(n * size, size) if not isinstance(n, int) else slice(n * size, (n + 1) * size)

        def flat(ap):
            names = "abcd"[:len(ap.shape) - 1]
            return ap.rearrange(f"p {' '.join(names)} -> p ({' '.join(names)})")

        def x_tile(eng, stage, i):
            x = X0[stage] + i
            eng.wait_ge(x_full, x + 1)
            return X[x % 4], x_free[x % 4]

        def x_read(eng, stage, i=None):
            tiles = range(max(0, XTILES[stage] - 4), XTILES[stage]) if i is None else [i]
            for k in tiles:
                x = X0[stage] + k
                eng.wait_ge(x_free[x % 4], x // 4 + 1)

        def g_tile(eng, stage, j, n):
            s = SLAB0[stage] + j
            eng.wait_ge(half_done, n * 2 + 2 * (SLAB0[stage] + 1))
            return G[s % 4], g_free[s % 4]

        def g_read(eng, stage):
            for n in range(max(0, SLABS[stage] - 4), SLABS[stage]):
                if gives_tile(stage, n):
                    s = SLAB0[stage] + n
                    eng.wait_ge(g_free[s % 4], tiles_before(s) + 1)

        R_a = area(29440, 4, 320)

        probsT = {"b": [flat(B_pT0)[:, 512 * i:512 * (i + 1)] for i in range(4)]
                       + [flat(B_pT1)[:, 512 * i:512 * (i + 1)] for i in range(8)],
                  "m": [flat(M_pT)[:, 512 * i:512 * (i + 1)] for i in range(MLA_H)]}

        @block.sync
        def _(sp):
            def load(slot, half, slab):
                cols1024 = slice(half * 1024, (half + 1) * 1024)
                sp.dma_start(ring[slot][:, cols1024], slab[:, cols1024]).then_inc(slab_loaded[slot][half], 16)

            for s in range(RING):
                for half in range(2):
                    load(s, half, slabs[s])
            with sp.Fori(1, N_SLABS // RING) as it:
                for j in range(RING):
                    for half in range(2):
                        sp.wait_ge(split_ready, it * (2 * RING) + (2 * (j - RING) + half + 1))
                        load(j, half, slabs[bass.ds(it * RING + j, 1)].rearrange("a p n -> (a p) n"))
            for s in range(N_SLABS // RING * RING, N_SLABS):
                for half in range(2):
                    sp.wait_ge(split_ready, 2 * (s - RING) + half + 1)
                    load(s % RING, half, slabs[s])
            sp.wait_ge(sem("h_ffn1"), 2)
            sp.dma_start(out.rearrange("(b p) d -> p b d", p=P), h[:, :, :]).then_inc(sem("out_stored"), 16)
            sp.wait_ge(sem("out_stored"), 16)

        @block.tensor
        def _(pe):
            def rounds(n):
                if n % 4 or n < 8:
                    for j in range(n):
                        yield j % 4, j // 4
                else:
                    with pe.Fori(0, n // 4) as it:
                        for j in range(4):
                            yield j, it

            def half_ready(s, r, half):
                pe.wait_ge(split_ready, r * 8 + (2 * s + half + 1))
                return 2 * (s % 2) + half

            def bank_free(s, r):
                before = tiles_before(s)
                if before or not isinstance(r, int) or r:
                    pe.wait_ge(g_free[s % 4], r + before)

            def triple(out, stationary, moving, start, stop):
                (a_hi, a_lo), (b_hi, b_lo) = stationary, moving
                nc.tensor.matmul(out, a_hi, b_hi, start=start, stop=False, skip_group_check=True)
                nc.tensor.matmul(out, a_hi, b_lo, start=False, stop=False, skip_group_check=True)
                return nc.tensor.matmul(out, a_lo, b_hi, start=False, stop=stop, skip_group_check=True)

            def project_slab(s, r, src, k, rows, pair, ready=None):
                hi, lo = src
                k0 = 0 if pair is None else 8 * pair
                if pair != 1:
                    bank_free(s + (pair is not None), r)
                bank = G[(s + (pair == 0)) % 4]
                for half in range(2):
                    q = half_ready(s, r, half)
                    kh = (k + 1) // 2
                    if ready is not None:
                        pe.wait_ge(ready, (k0 + half * kh + kh) // 2)
                    for i in range(kh if half == 0 else k - kh):
                        c = k0 + half * kh + i
                        for a in range(2):
                            act = [x[:, c, a * P:(a + 1) * P] if rows else x[:, c, :] for x in src]
                            w = [x[:, q, i * 256:(i + 1) * 256] if rows else x[:, q, i * 256 + a * P:i * 256 + (a + 1) * P]
                                 for x in (w_hi, w_lo)]
                            last = triple(bank[:, a * T:(a + 1) * T], act if rows else w, w if rows else act,
                                          c == 0 and a == 0, c == k0 + k - 1 and pair != 0)
                    last.then_inc(half_done, 1)

            def project(stage, src, k, rows, pairs=False, count=None, ready=None):
                s0, n = SLAB0[stage], SLABS[stage] if count is None else count
                if tiles_before(s0 + 3) == 0:
                    for j in range(4):
                        project_slab(s0 + j, 0, src, k, rows, None)
                    s0, n = s0 + 4, n - 4
                for j, r in rounds(n):
                    project_slab(s0 + j, r, src, k, rows, j % 2 if pairs else None, ready)

            def project_rows(stage, src, k):
                project(stage, src, k, True)

            def project_cols(stage, src, k):
                project(stage, src, k, False)

            def x_begin(stage, i):
                x = X0[stage] + i
                if x >= 4:
                    pe.wait_ge(x_free[x % 4], x // 4)
                return X[x % 4]

            def transpose_rows(stage, src, chunks=DC, tiles=None):
                for i in range(XTILES[stage]) if tiles is None else tiles:
                    tile = x_begin(stage, i)
                    for a in range(min(2, chunks - 2 * i)):
                        for b in range(NB):
                            c = 2 * i + a
                            last = nc.tensor.transpose(tile[:, a * T + b * P:a * T + (b + 1) * P],
                                                       src[:, b, c * P:(c + 1) * P], ident[:, :])
                    last.then_inc(x_full, 1)

            def transpose_blocks(stage, src, ready):
                tiles = [x_begin(stage, i) for i in range(4)]
                for b in range(NB):
                    pe.wait_ge(sem(ready), b + 1)
                    for c in range(DC):
                        o = c % 2 * T + b * P
                        last = nc.tensor.transpose(tiles[c // 2][:, o:o + P], src[:, b, c * P:(c + 1) * P], ident[:, :])
                        if b == NB - 1 and c % 2:
                            last.then_inc(x_full, 1)

            def attention(name, scores, transposes, values):
                for kind, k in attention_order(name):
                    stage = f"{name}_{kind}{k}"
                    if kind == "t":
                        pe.wait_ge(sem(f"p_{name}"), k + 1)
                    if kind == "v":
                        first = PV_AFTER[name][k - 1] + 1 if k else 0
                        for u in range(first, PV_AFTER[name][k] + 1):
                            x_read(pe, f"{name}_t{u}")
                    tile = x_begin(stage, 0)
                    if kind == "s":
                        last = scores(k, tile)
                    elif kind == "v":
                        last = values(k, tile)
                    else:
                        for to, src in transposes(k):
                            last = nc.tensor.transpose(tile[:, to:to + P], src, ident[:, :])
                    last.then_inc(x_full, 1)

            hT = (hT_hi, hT_lo)
            cT = (M_cTh, M_cTl)

            pe.wait_ge(sem("ident_ready"), 2)
            transpose_blocks("a_tr", xs, "xs_a")
            x_read(pe, "a_tr")
            project_rows("a_v", hT, DC)
            project_cols("a_u", hT, DC)
            pe.wait_ge(sem("vn_ready"), 1)
            pe.wait_ge(sem("ws_masked"), 1)
            for i in range(8):
                tile = x_begin("a_sv", i)
                for a in range(2):
                    for b in range(NB):
                        g = 2 * i + a
                        last = nc.tensor.matmul(tile[:, a * T + b * P:a * T + (b + 1) * P],
                                                A_v[:, b, g * P:(g + 1) * P], A_ws[:, g, :], start=True, stop=True)
                last.then_inc(x_full, 1)
            project_cols("a_g", hT, DC)
            project("a_out", (A_yh, A_yl), DC, True, pairs=True, ready=sem("a_y_ready"))

            transpose_blocks("b_tr", xs, "xs_b")
            x_read(pe, "b_tr")
            project_rows("b_kv", (hKV_hi, hKV_lo), DC)
            project_rows("b_q", hT, DC)
            project_cols("b_g", hT, DC)
            pe.wait_ge(sem("k_rotated"), 1)
            tile = x_begin("b_ktr", 0)
            for g in range(KVH):
                for b in range(NB):
                    last = nc.tensor.transpose(tile[:, g * T + b * P:g * T + (b + 1) * P],
                                               B_kdup[:, b, g, :, :].rearrange("p a d -> p (a d)"), ident[:, :])
            last.then_inc(x_full, 1)
            pe.wait_ge(sem("q_rotated"), 4)
            transpose_rows("b_qtr", B_q)
            x_read(pe, "b_ktr")
            pe.wait_ge(sem("pads_zero"), 3)
            x_read(pe, "b_qtr")
            kT = [B_kTe, B_kTo]

            pe.wait_ge(sem("vz_ready"), 1)

            def b_scores(k, tile):
                heads, queries, keys = ((range(4 * k, 4 * k + 4), slice(0, P), P) if k < 4 else
                                        (range(2 * k - 8, 2 * k - 6), slice(P, T), T))
                for a, hd in enumerate(heads):
                    last = nc.tensor.matmul(tile[:, a * keys:(a + 1) * keys], B_qT[:, hd // 2, queries],
                                            kT[hd % 2][:, hd // 8, 0:keys], start=True, stop=True)
                return last

            def b_transposes(k):
                if k < 4:
                    return [(a * P, B_s0[:, 4 * k + a, :]) for a in range(4)]
                return [(a * T + c * P, B_s1[:, 2 * (k - 4) + a, c * P:(c + 1) * P]) for a in range(2) for c in range(2)]

            def v_of(b, hd):
                return B_vz[:, b, hd // 8, 64:192] if hd % 2 == 0 else B_vz[:, b, hd // 8, 0:128]

            def b_values(k, tile):
                b, i = k // 2, k % 2
                for a in range(4):
                    parts = [(2 * (4 * i + a) + e, kc) for e in range(2) for kc in range(b + 1)]
                    for n, (hd, kc) in enumerate(parts):
                        probs = B_pT0[:, hd, :] if b == 0 else B_pT1[:, hd, kc, :]
                        last = nc.tensor.matmul(tile[:, a * P:(a + 1) * P], v_of(kc, hd), probs,
                                                start=(n == 0), stop=(n == len(parts) - 1))
                return last

            attention("b", b_scores, b_transposes, b_values)
            pe.wait_ge(sem("b_y_ready"), 4)
            project_rows("b_out", (B_yh, B_yl), DC)

            transpose_blocks("r_tr", h, "h_b")
            x_read(pe, "r_tr")
            project_cols("r_qk", hT, DC)
            project_rows("r_v", hT, DC)
            pe.wait_ge(sem("r_qk_ready"), 8)
            for hd in range(RET_H):
                tile = x_begin("r_s", hd)
                for m in range(NB):
                    for c in range(2):
                        last = nc.tensor.matmul(tile[:, m * T:(m + 1) * T], R_qk[:, 8 + 2 * hd + c, m * P:(m + 1) * P],
                                                R_qk[:, 2 * hd + c, :], start=(c == 0), stop=(c == 1))
                last.then_inc(x_full, 1)
            g_read(pe, "r_v")
            for i in range(8):
                hd, b = i // 2, i % 2
                if b == 0:
                    x_read(pe, "r_s", hd)
                tile = x_begin("r_y", i)
                for m in range(NB):
                    last = nc.tensor.matmul(tile[:, :], R_s[:, hd, m, b * P:(b + 1) * P],
                                            R_v[:, m, hd * RET_DV:(hd + 1) * RET_DV], start=(m == 0), stop=(m == 1))
                last.then_inc(x_full, 1)
            project("r_g", hT, DC, False, count=4)
            pe.wait_ge(sem("r_yn_ready"), 1)
            for n in range(4, 8):
                project_slab(SLAB0["r_g"] + n, 0, hT, DC, False, None)
                transpose_rows("r_yt", R_y, 16, tiles=(2 * n - 8, 2 * n - 7))
            project("r_out", (R_yh, R_yl), DC, True, pairs=True, ready=sem("r_y_ready"))

            def experts(l):
                transpose_blocks(f"p_tr{l}", h, f"h_mix{l}")
                x_read(pe, f"p_tr{l}")
                project_cols(f"pq{l}", hT, DC)
                pe.wait_ge(sem(f"keys_loaded{l}"), 16)
                g_read(pe, f"pq{l}")
                for i in range(8):
                    tile = x_begin(f"p_s{l}", i)
                    for a in range(4):
                        hc = 4 * (i % 4) + a
                        last = nc.tensor.matmul(tile[:, a * P:(a + 1) * P], K_q[:, hc, (i // 4) * P:(i // 4 + 1) * P],
                                                keysT[:, hc, :], start=True, stop=True)
                    last.then_inc(x_full, 1)
                project(f"u{l}", hT, DC, False, count=GATED)
                for b in range(NB):
                    pe.wait_ge(sem(f"picks{l}"), b + 1)
                    tile = x_begin(f"p_kt{l}", b)
                    for a in range(3):
                        last = nc.tensor.transpose(tile[:, a * P:(a + 1) * P], picks[:, b, a, :], ident[:, :])
                    last.then_inc(x_full, 1)
                s0, w0 = SLAB0[f"u{l}"] + GATED, X0[f"p_w{l}"]
                with pe.Fori(0, 8) as it:
                    for j in range(4):
                        project_slab(s0 + j, it, hT, DC, False, None)
                        for g in range(2):
                            x = w0 + 2 * j + g
                            pe.wait_ge(x_free[x % 4], it * 2 + x // 4)
                            pe.wait_ge(sem(f"hot1_{l}"), it * 8 + (2 * j + g + 1))
                            pe.wait_ge(sem(f"hot2_{l}"), it * 8 + (2 * j + g + 1))
                            for q in range(4):
                                last = nc.tensor.matmul(X[x % 4][:, q * P:(q + 1) * P], hot[:, 1, g, q, :],
                                                        hot[:, 0, g, q, :], start=True, stop=True)
                            last.then_inc(x_full, 1)
                for n in range(GATED + 32, 64):
                    project_slab(SLAB0[f"u{l}"] + n, 0, hT, DC, False, None)
                s0, y0 = SLAB0[f"v{l}"], X0[f"p_y{l}"]
                for i in range(4):
                    pe.wait_ge(x_free[(y0 + i) % 4], (y0 + i) // 4)

                def v_slab(j, r, first, final):
                    for a in range(2):
                        q = half_ready(s0 + j, r, a)
                        pe.wait_ge(sem(f"gated_split{l}"), r * 8 + (2 * j + a + 1))
                        act = [x[:, (2 * j + a) % 4, :] for x in hT]
                        for c in range(DC):
                            w = [x[:, q, c * P:(c + 1) * P] for x in (w_hi, w_lo)]
                            last = triple(X[(y0 + c // 2) % 4][:, (c % 2) * T:(c % 2 + 1) * T], w, act,
                                          first and a == 0 and c % 2 == 0, final and a == 1)
                            if final and a == 1 and c % 2:
                                last.then_inc(x_full, 1)
                        if not (final and a == 1):
                            last.then_inc(half_done, 1)

                for j in range(4):
                    v_slab(j, 0, j == 0, False)
                with pe.Fori(1, 15) as it:
                    for j in range(4):
                        v_slab(j, it, False, False)
                for j in range(4):
                    v_slab(j, 15, False, j == 3)
                pe.wait_ge(x_full, y0 + 4)
                pe.sem_inc(half_done, 1)
                x_read(pe, f"p_y{l}")
                for i in range(4):
                    tile = x_begin(f"p_yr{l}", i)
                    for a in range(4):
                        c = 4 * (i % 2) + a
                        last = nc.tensor.transpose(tile[:, a * P:(a + 1) * P],
                                                   K_yT[:, c, (i // 2) * P:(i // 2 + 1) * P], ident[:, :])
                    last.then_inc(x_full, 1)

            experts(0)

            transpose_blocks("m_tr", h, "h_ffn0")
            x_read(pe, "m_tr")
            project_rows("m_in", hT, DC)
            pe.wait_ge(sem("cn_ready"), 1)
            transpose_rows("m_ct", M_cn, 5)
            pe.wait_ge(sem("kr_rotated"), 1)
            tile = x_begin("m_krt", 0)
            for b in range(NB):
                last = nc.tensor.transpose(tile[:, b * P:(b + 1) * P],
                                           M_kr[:, b, :, :].rearrange("p a d -> p (a d)"), ident[:, :])
            last.then_inc(x_full, 1)
            x_read(pe, "m_ct")

            def half_used(stage, i):
                pe.wait_ge(x_full, X0[stage] + i + 1)
                pe.sem_inc(half_done, 1)

            for j in range(SLABS["m_q"]):
                for half in range(2):
                    q = half_ready(SLAB0["m_q"] + j, 0, half)
                    stage, i = ("m_qr", half) if j == 0 else ("m_qn", 2 * (j - 1) + half)
                    tile = x_begin(stage, i)
                    for c in range(3):
                        for a in range(2):
                            o = tile[:, a * T:(a + 1) * T]
                            if j == 0:
                                last = triple(o, [x[:, c, a * P:(a + 1) * P] for x in cT],
                                              [x[:, q, c * T:(c + 1) * T] for x in (w_hi, w_lo)],
                                              c == 0 and a == 0, c == 2)
                            else:
                                last = triple(o, [x[:, q, c * T + a * P:c * T + (a + 1) * P] for x in (w_hi, w_lo)],
                                              [x[:, c, :] for x in cT], c == 0 and a == 0, c == 2)
                    last.then_inc(x_full, 1)
                    half_used(stage, i)
            for j in range(SLABS["m_kv"]):
                for half in range(2):
                    q = half_ready(SLAB0["m_kv"] + j, 0, half)
                    for a in range(2):
                        i = 4 * j + 2 * half + a
                        tile = x_begin("m_kv", i)
                        for c in range(2):
                            w0 = (2 * a + c) * T
                            k_w = [x[:, q, w0:w0 + P] for x in (w_hi, w_lo)]
                            v_w = [x[:, q, w0 + P:w0 + T] for x in (w_hi, w_lo)]
                            triple(tile[:, 0:T], k_w, [x[:, 3 + c, :] for x in cT], c == 0, c == 1)
                            for b in range(NB):
                                last = triple(tile[:, T + b * P:T + (b + 1) * P],
                                              [x[:, 3 + c, b * P:(b + 1) * P] for x in cT], v_w, False, c == 1)
                        last.then_inc(x_full, 1)
                    half_used("m_kv", i)
            pe.wait_ge(sem("mq_rotated"), 2)
            transpose_rows("m_qrt", M_qr, 4)
            x_read(pe, "m_krt")
            pe.wait_ge(sem("pads_zero"), 5)
            x_read(pe, "m_qn")
            x_read(pe, "m_kv")
            x_read(pe, "m_qrt")
            krT = [M_krTe, M_krTo]

            def m_scores(hd, tile):
                for b in range(NB):
                    o = tile[:, b * T:(b + 1) * T]
                    nc.tensor.matmul(o, M_qn[:, hd, b * P:(b + 1) * P], M_kn[:, hd, :], start=True, stop=False)
                    last = nc.tensor.matmul(o, M_qrT[:, hd // 2, b * P:(b + 1) * P], krT[hd % 2], start=False, stop=True)
                return last

            def m_transposes(hd):
                return [(kc * T + b * P, M_s[:, 2 * hd + b, kc * P:(kc + 1) * P]) for kc in range(2) for b in range(NB)]

            def m_values(i, tile):
                for a in range(2):
                    hd = 2 * i + a
                    for kc in range(2):
                        last = nc.tensor.matmul(tile[:, a * T:(a + 1) * T], M_v[:, kc, hd * P:(hd + 1) * P],
                                                M_pT[:, hd, kc, :], start=(kc == 0), stop=(kc == 1))
                return last

            attention("m", m_scores, m_transposes, m_values)
            for i in range(4):
                x_read(pe, f"m_v{i}")
            project_rows("m_out", (M_oTh, M_oTl), DC)
            experts(1)

        @block.scalar
        def _(act):
            def row(dst, name, loaded="rows_loaded", a=0, n=None):
                n = ROWN[name] if n is None else n
                src = rows_in[0:1, ROW0[name] + a:ROW0[name] + a + n]
                act.dma_start(dst, src.broadcast_to([P, n])).then_inc(sem(loaded), 16)

            def norm_weights(name):
                row(lnw[:, 0, :], name, "lnw_loaded", 0, D)
                row(lnw[:, 1, :], name, "lnw_loaded", D, D)

            act.dma_start(h[:, :, :], x_in.rearrange("(b p) d -> p b d", p=P)).then_inc(sem("x_loaded"), 16)
            act.dma_start(cols[:, :], cols_in).then_inc(sem("cols_loaded"), 16)
            act.dma_start(pos_i, pos_row.broadcast_to([P, T])).then_inc(sem("pos_loaded"), 16)
            act.dma_start(posc_i, pos_col).then_inc(sem("pos_loaded"), 16)
            row(R_decay, "decay")
            row(R_invf, "invf_row")
            row(A_lng, "ln_g")
            row(A_lnb, "ln_b")
            row(flat(A_bs), "bs")
            row(B_bq, "bq")
            row(B_bkv, "bkv")
            row(B_sink, "sinks")
            act.dma_start(flat(A_ws), ws_in).then_inc(sem("ws_loaded"), 16)
            act.dma_start(B_rope, rope_in.rearrange("p (a b c) -> p a b c", a=NB, b=2)).then_inc(sem("rope_loaded"), 16)

            def split(s, r=0):
                j = s % 2
                for half in range(2):
                    act.wait_ge(slab_loaded[j][half], r * 32 + 16 * (s // 2 + 1))
                    n = 2 * s + half - SPLIT
                    if n >= 0:
                        act.wait_ge(half_done, r * 8 + (n + 1))
                    nc.scalar.activation(w_hi[:, 2 * j + half, :], ring[j][:, half * 1024:(half + 1) * 1024],
                                         ACT.Copy).then_inc(hi_ready, 1)

            def slabs_of(stage, first=0, count=None):
                count = SLABS[stage] if count is None else count
                s0 = SLAB0[stage] + first
                if count % 4 or count < 8:
                    for j in range(count):
                        yield j, first + j
                        if s0 + j + RING < N_SLABS:
                            split(s0 + j + RING)
                else:
                    with act.Fori(0, count // 4) as it:
                        for j in range(4):
                            yield j, it * 4 + (first + j)
                            split(s0 + j + RING, it)

            def only_split(stage, first=0, count=None):
                for _ in slabs_of(stage, first, count):
                    pass

            def root(name, n):
                act.wait_ge(sem(f"var_{name}"), 1)
                nc.scalar.activation(rstd[:, 0:n], rstd[:, 0:n], ACT.Sqrt).then_inc(sem(f"std_{name}"), 1)

            def round_T(stage, to, scale=None, tiles=4):
                for i in range(tiles):
                    tile, _ = x_tile(act, stage, i)
                    for dst, g in zip(to, scale or [None]):
                        if g is None:
                            last = nc.scalar.activation(flat(dst[:, 2 * i:2 * i + 2, :]), tile[:, :], ACT.Copy)
                            continue
                        for a in range(min(2, dst.shape[1] - 2 * i)):
                            last = nc.scalar.activation(dst[:, 2 * i + a, :], tile[:, a * T:(a + 1) * T], ACT.Copy,
                                                        scale=col(g, 2 * i + a))
                    last.then_inc(sem(f"rounded_{stage}"), 1)

            def take_T(stage, dst, tiles=(0, 2)):
                for i in tiles:
                    tile, free = x_tile(act, stage, i)
                    nc.scalar.activation(flat(dst[:, 2 * i:2 * i + 2, :]), tile[:, :], ACT.Copy).then_inc(free, 1)

            def take_cols(stage, dst, func=ACT.Copy, every=1, first=0, count=None):
                for j, n in slabs_of(stage, first, count):
                    if j % every == 0:
                        tile, free = g_tile(act, stage, (first + j) % 4, n)
                        nc.scalar.activation(flat(dst)[:, at(n, 512)], tile[:, :], func).then_inc(free, 1)

            def take_rows(stage, dst, every=1):
                for j, n in slabs_of(stage):
                    if j % every == 0:
                        tile, free = g_tile(act, stage, j, n)
                        nc.scalar.activation(dst[:, :, at(n, 256)], tile[:, :].rearrange("p (b n) -> p b n", b=NB),
                                             ACT.Copy).then_inc(free, 1)

            def attention(name, sinks, from_psum=None, round_to=None):
                for kind, k in attention_order(name):
                    stage = f"{name}_{kind}{k}"
                    if kind == "s":
                        s, row = units[name][k]
                        act.wait_ge(sem(f"max_{name}"), k + 1)
                        n = s.shape[1]
                        if sinks:
                            nc.scalar.activation(esink[:, row:row + n], esink[:, row:row + n], ACT.Exp)
                        if from_psum:
                            tile, free = x_tile(act, stage, 0)
                        for u in range(n):
                            src = tile[:, u * T:(u + 1) * T] if from_psum else s[:, u, :]
                            last = nc.scalar.activation(s[:, u, :], src, ACT.Exp, bias=negm[:, row + u:row + u + 1],
                                                        scale=from_psum or 1.0,
                                                        accum_out=rsum[:, row + u:row + u + 1])
                        last.then_inc(free if from_psum else sem(f"exp_{name}"), 1)
                    elif kind == "t":
                        tile, free = x_tile(act, stage, 0)
                        nc.scalar.activation(probsT[name][k], tile[:, :], ACT.Copy).then_inc(free, 1)
                    elif round_to is not None:
                        tile, _ = x_tile(act, stage, 0)
                        nc.scalar.activation(flat(round_to[:, 2 * k:2 * k + 2, :]), tile[:, :], ACT.Copy
                                             ).then_inc(sem(f"rounded_{name}"), 1)

            for s in range(RING):
                split(s)
            root("a", 2)
            act.wait_ge(sem("cols_loaded"), 16)
            round_T("a_tr", [hT_hi], ["a_g"])
            act.wait_ge(sem("angles"), 1)
            nc.scalar.activation(sinT, R_a[:, 2, 0:T], ACT.Sin)
            nc.scalar.activation(cosT, R_a[:, 3, 0:T], ACT.Sin)
            nc.scalar.activation(rope_row[:, :, 1, :], R_a[:, 2, T:].rearrange("p (b f) -> p b f", b=NB), ACT.Sin)
            nc.scalar.activation(rope_row[:, :, 0, :], R_a[:, 3, T:].rearrange("p (b f) -> p b f", b=NB),
                                 ACT.Sin).then_inc(sem("rotary_ready"), 1)
            act.wait_ge(sem("rows_loaded"), 16 * 8)
            nc.scalar.activation(R_lg[:, 0, :], R_decay, ACT.Exp).then_inc(sem("decay_exp"), 1)
            act.wait_ge(sem("one_minus"), 1)
            nc.scalar.activation(R_lg[:, 2, :], R_lg[:, 1, :], ACT.Ln).then_inc(sem("decay_ln"), 1)
            take_rows("a_v", A_v, 2)
            take_cols("a_u", A_u, every=2, count=2)
            root("vn", 2)
            take_cols("a_u", A_u, every=2, first=2, count=6)
            take_cols("a_g", A_g, ACT.Silu)
            only_split("a_out")

            root("b", 2)
            round_T("b_tr", [hT_hi, hKV_hi], ["b_g", "kv_g"])
            only_split("b_kv")
            only_split("b_q")
            take_cols("b_g", B_gT, ACT.Silu)
            tile, free = x_tile(act, "b_ktr", 0)
            act.wait_ge(sem("pads_zero"), 2)
            nc.scalar.activation(flat(B_kTe)[0:64, :], tile[0:64, :], ACT.Copy)
            nc.scalar.activation(flat(B_kTo)[64:128, :], tile[64:128, :], ACT.Copy).then_inc(free, 1)
            act.dma_start(flat(R_diff), diff_in).then_inc(sem("diff_loaded"), 16)
            row(fin_g, "fin_g", "lnw_loaded")
            take_T("b_qtr", B_qT)
            attention("b", True)
            only_split("b_out")
            root("fin", 2)

            round_T("r_tr", [hT_hi])
            for i in range(RET_H):
                act.wait_ge(sem("decay_arg"), i + 1)
                nc.scalar.activation(R_D[:, i, :], R_D[:, i, :], ACT.Exp).then_inc(sem("decay_ready"), 1)
            norm_weights("mix0")
            only_split("r_qk")
            take_rows("r_v", R_v)
            for i in range(8):
                tile, free = x_tile(act, "r_y", i)
                nc.scalar.activation(R_y[:, i % 2, (i // 2) * RET_DV:(i // 2 + 1) * RET_DV], tile[:, :],
                                     ACT.Copy).then_inc(free, 1)
            take_cols("r_g", R_g, ACT.Silu, count=2)
            root("gn", 8)
            take_cols("r_g", R_g, ACT.Silu, first=2, count=6)
            only_split("r_out")
            root("mix0", 2)

            def experts(l):
                act.wait_ge(sem(f"h_mix{l}"), NB)
                act.dma_start(flat(keysT), keys_in[l]).then_inc(sem(f"keys_loaded{l}"), 16)
                act.dma_start(h_kept.rearrange("(b p) d -> p b d", p=P), h[:, :, :]).then_inc(sem(f"h_kept{l}"), 16)
                round_T(f"p_tr{l}", [hT_hi])
                take_cols(f"pq{l}", K_q)
                for i in range(8):
                    tile, free = x_tile(act, f"p_s{l}", i)
                    nc.scalar.activation(flat(K_s[:, i // 4, 4 * (i % 4):4 * (i % 4) + 4, :]), tile[:, :],
                                         ACT.Copy).then_inc(free, 1)

                def gelus(first, count):
                    for j, n in slabs_of(f"u{l}", first, count):
                        tile, free = g_tile(act, f"u{l}", j, n)
                        nc.scalar.activation(big[:, at(n, 512)], tile[:, :], ACT.Gelu).then_inc(free, 1)

                gelus(0, 12)
                for b, slabs_until in enumerate((24, GATED)):
                    act.wait_ge(sem(f"top{l}"), b + 1)
                    nc.scalar.activation(picks[:, b, 2, :], picks[:, b, 2, :], ACT.Exp).then_inc(sem(f"gates{l}"), 1)
                    gelus(12 if b == 0 else 24, slabs_until - (12 if b == 0 else 24))
                x_read(act, f"p_kt{l}")
                act.wait_ge(sem(f"h_kept{l}"), 16)
                w0 = X0[f"p_w{l}"]

                def hot1(g, group):
                    act.wait_ge(x_full, group + (w0 - 1))
                    for q in range(3):
                        last = nc.scalar.activation(hot[:, 0, g, q, :], iota[:, :], ACT.Abs,
                                                    bias=picksT[:, 0, bass.ds(group * 4 + q, 1)], scale=-1.0)
                    last.then_inc(sem(f"distance{l}"), 1)
                    act.wait_ge(sem(f"distance{l}"), group + 1)
                    nc.scalar.activation(hot[:, 0, g, 0:3, :], hot[:, 0, g, 0:3, :], ACT.Relu, bias=1.0,
                                         scale=-1.0).then_inc(sem(f"hot1_{l}"), 1)

                def gelu_in_place(j, n):
                    tile, _ = g_tile(act, f"u{l}", j, n)
                    nc.scalar.activation(tile[:, :], tile[:, :], ACT.Gelu).then_inc(sem(f"gelu{l}"), 1)

                s0 = SLAB0[f"u{l}"] + GATED
                with act.Fori(0, 8) as it:
                    for j in range(4):
                        hot1(0, it * 8 + 2 * j)
                        hot1(1, it * 8 + (2 * j + 1))
                        gelu_in_place(j, it * 4 + (GATED + j))
                        split(s0 + j + RING, it)
                act.wait_ge(x_full, w0 + GROUPS)
                act.dma_start(h[:, :, :], h_kept.rearrange("(b p) d -> p b d", p=P)).then_inc(sem(f"h_back{l}"), 16)
                for n in range(GATED + 32, 64):
                    gelu_in_place(n % 4, n)
                    split(SLAB0[f"u{l}"] + n + RING)
                only_split(f"v{l}", 0, 60)
                only_split(f"v{l}", 60, 4)
                take_T(f"p_y{l}", K_yT)
                norm_weights(f"ffn{l}")
                root(f"ffn{l}", 2)

            experts(0)

            round_T("m_tr", [hT_hi])
            norm_weights("mix1")
            take_rows("m_in", M_c)
            root("cn", 4)
            round_T("m_ct", [M_cTh], ["m_qg"], 3)
            tile, free = x_tile(act, "m_krt", 0)
            act.wait_ge(sem("pads_zero"), 5)
            nc.scalar.activation(M_krTe[0:64, :], tile[0:64, 0:T], ACT.Copy)
            nc.scalar.activation(M_krTo[64:128, :], tile[64:128, 0:T], ACT.Copy).then_inc(free, 1)
            split(SLAB0["m_q"] + RING)
            for i in range(4):
                tile, free = x_tile(act, "m_qn", i)
                nc.scalar.activation(flat(M_qn)[:, 512 * i:512 * (i + 1)], tile[:, :], ACT.Copy).then_inc(free, 1)
                if i % 2:
                    split(SLAB0["m_kv"] + i // 2)
            for i in range(MLA_H):
                tile, free = x_tile(act, "m_kv", i)
                nc.scalar.activation(M_kn[:, i, :], tile[:, 0:T], ACT.Copy)
                nc.scalar.activation(M_v[:, :, i * P:(i + 1) * P], tile[:, T:].rearrange("p (b n) -> p b n", b=NB),
                                     ACT.Copy).then_inc(free, 1)
                if i % 4 == 3:
                    split(SLAB0["m_out"] + i // 4)
            attention("m", False, float(P + ROPE) ** -0.5, M_oTh)
            only_split("m_out")
            root("mix1", 2)
            experts(1)

        @block.vector
        def _(dve):
            taken = [0]

            def link(ins):
                taken[0] += 1
                ins.then_inc(dve_step, 1)
                dve.wait_ge(dve_step, taken[0])

            V = nc.vector

            def stats(name, rows, centered, gathered=None, middle=None):
                k = 0
                parts = []
                for r in rows:
                    n = r.shape[1]
                    m = gathered or -(-n // 512)
                    for q in range(m if gathered is None else 0):
                        last = V.bn_stats(st[:, k + q, :], r[:, q * (n // m):(q + 1) * (n // m)])
                    parts.append((k, m))
                    k += m
                if gathered is None:
                    link(last)
                for i, (k, m) in enumerate(parts):
                    last = V.bn_aggr(mv[:, i, :], st[:, k:k + m, :].rearrange("p a b -> p (a b)"))
                link(last)
                n = len(rows)
                if centered:
                    V.tensor_scalar(rstd[:, 0:n], mv[:, 0:n, 1], EPS, None, ALU.add).then_inc(sem(f"var_{name}"), 1)
                else:
                    link(V.tensor_tensor(rstd[:, 0:n], mv[:, 0:n, 0], mv[:, 0:n, 0], ALU.mult))
                    V.scalar_tensor_tensor(rstd[:, 0:n], rstd[:, 0:n], EPS, mv[:, 0:n, 1], ALU.add,
                                           ALU.add).then_inc(sem(f"var_{name}"), 1)
                if middle is not None:
                    middle()
                dve.wait_ge(sem(f"std_{name}"), 1)
                link(V.reciprocal(rstd[:, 0:n], rstd[:, 0:n]))

            def layer_norm(name, count, gathered):
                def centre():
                    dve.wait_ge(sem("lnw_loaded"), 16 * count)
                    for b in range(NB):
                        last = V.scalar_tensor_tensor(h[:, b, :], h[:, b, :], mv[:, b, 0:1], lnw[:, 0, :],
                                                      ALU.subtract, ALU.mult)
                    link(last)

                stats(name, [h[:, b, :] for b in range(NB)], True, gathered, centre)
                for b in range(NB):
                    V.scalar_tensor_tensor(h[:, b, :], h[:, b, :], rstd[:, b:b + 1], lnw[:, 1, :], ALU.mult,
                                           ALU.add).then_inc(sem(f"h_{name}"), 1)
                dve.wait_ge(sem(f"h_{name}"), NB)

            def normed(name, dst, src):
                for b in range(NB):
                    V.tensor_scalar(dst[:, b, :], src[:, b, :], rstd[:, b:b + 1], None, ALU.mult).then_inc(sem(name), 1)

            def rest_T(stage, to, scale=None, tiles=4):
                for i in range(tiles):
                    tile, free = x_tile(dve, stage, i)
                    dve.wait_ge(sem(f"rounded_{stage}"), i + 1)
                    for (hi, lo), g in zip(to, scale or [None]):
                        if g is None:
                            last = V.tensor_tensor(flat(lo[:, 2 * i:2 * i + 2, :]), tile[:, :],
                                                   flat(hi[:, 2 * i:2 * i + 2, :]), ALU.subtract)
                            continue
                        for a in range(min(2, lo.shape[1] - 2 * i)):
                            last = V.scalar_tensor_tensor(lo[:, 2 * i + a, :], tile[:, a * T:(a + 1) * T],
                                                          col(g, 2 * i + a), hi[:, 2 * i + a, :], ALU.mult, ALU.subtract)
                    last.then_inc(free, 1)

            def split(hi, lo, x):
                link(V.tensor_copy(hi, x))
                return V.tensor_tensor(lo, x, hi, ALU.subtract)

            def take_T(stage, dst, tiles=(1, 3)):
                for i in tiles:
                    tile, free = x_tile(dve, stage, i)
                    V.tensor_copy(flat(dst[:, 2 * i:2 * i + 2, :]), tile[:, :]).then_inc(free, 1)

            def rotate(x, n, table, tmp, done):
                t = [tmp[:, q * (NB * n * 32):(q + 1) * (NB * n * 32)].rearrange("p (b n f) -> p b n f", b=NB, n=n)
                     for q in range(4)]
                x1, x2 = x[:, :, :, 0:32], x[:, :, :, 32:64]
                cos, sin = bc(table[:, :, 0, :], 2, n), bc(table[:, :, 1, :], 2, n)
                V.tensor_tensor(t[0], x1, cos, ALU.mult)
                V.tensor_tensor(t[1], x2, sin, ALU.mult)
                V.tensor_tensor(t[2], x2, cos, ALU.mult)
                link(V.tensor_tensor(t[3], x1, sin, ALU.mult))
                V.tensor_tensor(x1, t[0], t[1], ALU.subtract)
                V.tensor_tensor(x2, t[2], t[3], ALU.add).then_inc(done, 1)

            def attention(name, sinks, prepare, take_values):
                def maximum(k):
                    s, row = units[name][k]
                    m = slice(row, row + s.shape[1])
                    link(V.tensor_reduce(mx[:, m], prepare(k), AX.X, ALU.max))
                    if sinks:
                        head = row % 16
                        sink = B_sink[:, head:head + s.shape[1]]
                        link(V.tensor_tensor(mx[:, m], mx[:, m], sink, ALU.max))
                        V.tensor_tensor(esink[:, m], sink, mx[:, m], ALU.subtract)
                    scale = 1.0 if sinks else float(P + ROPE) ** -0.5
                    V.tensor_scalar(negm[:, m], mx[:, m], -scale, None, ALU.mult).then_inc(sem(f"max_{name}"), 1)

                def normalize(k):
                    s, row = units[name][k]
                    m = slice(row, row + s.shape[1])
                    if sinks:
                        dve.wait_ge(sem(f"exp_{name}"), k + 1)
                        link(V.tensor_tensor(rsum[:, m], rsum[:, m], esink[:, m], ALU.add))
                    else:
                        x_read(dve, f"{name}_s{k}")
                    link(V.reciprocal(rden[:, m], rsum[:, m]))
                    for u in range(s.shape[1]):
                        last = V.tensor_scalar(s[:, u, :], s[:, u, :], rden[:, row + u:row + u + 1], None, ALU.mult)
                    last.then_inc(sem(f"p_{name}"), 1)

                maximum(0)
                maximum(1)
                for kind, k in attention_order(name):
                    if kind == "t":
                        normalize(k)
                        if k + 2 < UNITS[name]:
                            maximum(k + 2)
                    elif kind == "v":
                        take_values(k)

            hT = (hT_hi, hT_lo)

            dve.wait_ge(sem("x_loaded"), 16)
            stats("a", [h[:, b, :] for b in range(NB)], False)
            normed("xs_a", xs, h)
            dve.wait_ge(sem("cols_loaded"), 16)
            rest_T("a_tr", [hT], ["a_g"])
            dve.wait_ge(sem("pos_loaded"), 32)
            dve.wait_ge(sem("rows_loaded"), 16 * 8)
            V.tensor_copy(R_a[:, 1, 0:T], pos_i[:, :])
            link(V.tensor_copy(mx[:, 0:NB], posc_i[:, :]))
            V.tensor_scalar(R_a[:, 0, 0:T], R_a[:, 1, 0:T], col("invf", 0), None, ALU.mult)
            for b in range(NB):
                last = V.tensor_scalar(R_a[:, 0, T + 32 * b:T + 32 * b + 32], R_invf, mx[:, b:b + 1], None, ALU.mult)
            link(last)
            link(V.tensor_scalar(R_a[:, 1, :], R_a[:, 0, :], 1.0 / (2 * np.pi), 12582912.0, ALU.mult, ALU.add))
            link(V.tensor_scalar(R_a[:, 1, :], R_a[:, 1, :], 12582912.0, None, ALU.subtract))
            src = 0
            for part in (6.28125, 0.0019350051879882812, 3.019916050561733e-07):
                link(V.scalar_tensor_tensor(R_a[:, 2, :], R_a[:, 1, :], -part, R_a[:, src, :], ALU.mult, ALU.add))
                src = 2
            link(V.tensor_scalar(R_a[:, 3, :], R_a[:, 2, :], np.pi / 2, None, ALU.add))
            link(V.tensor_scalar(R_a[:, 1, :], R_a[:, 3, :], np.pi, -2 * np.pi, ALU.is_gt, ALU.mult))
            link(V.tensor_tensor(R_a[:, 3, :], R_a[:, 3, :], R_a[:, 1, :], ALU.add))
            V.tensor_scalar(R_a[:, 2:4, :], R_a[:, 2:4, :], 3.1415925, -3.1415925, ALU.min, ALU.max
                            ).then_inc(sem("angles"), 1)
            dve.wait_ge(sem("decay_exp"), 1)
            V.tensor_scalar(R_lg[:, 1, :], R_lg[:, 0, :], -1.0, 1.0, ALU.mult, ALU.add).then_inc(sem("one_minus"), 1)
            dve.wait_ge(sem("one_minus"), 1)
            link(V.tensor_scalar(R_lg[:, 3, :], R_lg[:, 1, :], -1.0, None, ALU.add))
            link(V.tensor_scalar(R_lg[:, 4, :], R_lg[:, 3, :], 0.0, None, ALU.is_equal))
            link(V.tensor_tensor(R_lg[:, 3, :], R_lg[:, 3, :], R_lg[:, 4, :], ALU.add))
            link(V.reciprocal(R_lg[:, 5, :], R_lg[:, 3, :]))
            dve.wait_ge(sem("decay_ln"), 1)
            link(V.tensor_tensor(R_lg[:, 5, :], R_lg[:, 5, :], R_lg[:, 2, :], ALU.mult))
            link(V.tensor_tensor(R_lg[:, 5, :], R_lg[:, 5, :], R_lg[:, 4, :], ALU.add))
            link(V.scalar_tensor_tensor(R_lg[:, 5, :], R_lg[:, 0, :], -1.0, R_lg[:, 5, :], ALU.mult, ALU.mult))

            for j, n in fours(dve, 8):
                if j % 2:
                    tile, free = g_tile(dve, "a_v", j, n)
                    V.tensor_copy(A_v[:, :, at(n, 256)], tile[:, :].rearrange("p (b n) -> p b n", b=NB)).then_inc(free, 1)
            g_read(dve, "a_v")
            stats("vn", [A_v[:, b, :] for b in range(NB)], True)
            for b in range(NB):
                last = V.tensor_scalar(A_v[:, b, :], A_v[:, b, :], mv[:, b, 0:1], rstd[:, b:b + 1], ALU.subtract, ALU.mult)
            link(last)
            for b in range(NB):
                last = V.tensor_tensor(A_v[:, b, :], A_v[:, b, :], A_lng, ALU.mult)
            link(last)
            for b in range(NB):
                last = V.tensor_tensor(A_v[:, b, :], A_v[:, b, :], A_lnb, ALU.add)
            last.then_inc(sem("vn_ready"), 1)
            for j, n in fours(dve, 8):
                if j % 2:
                    tile, free = g_tile(dve, "a_u", j, n)
                    V.tensor_copy(flat(A_u)[:, at(n, 512)], tile[:, :]).then_inc(free, 1)
            g_read(dve, "a_u")
            for i in range(8):
                tile, free = x_tile(dve, "a_sv", i)
                y = A_y[:, 2 * i:2 * i + 2, :].rearrange("p a (b t) -> p a b t", b=NB)
                V.tensor_tensor(y, tile[:, :].rearrange("p (a b t) -> p a b t", a=2, b=NB),
                                bc(A_bs[:, 2 * i:2 * i + 2, :], 2, NB), ALU.add).then_inc(free, 1)
                x_read(dve, "a_sv", i)
                last = V.tensor_tensor(flat(A_y[:, 2 * i:2 * i + 2, :]), flat(A_y[:, 2 * i:2 * i + 2, :]),
                                       flat(A_u[:, 2 * i:2 * i + 2, :]), ALU.mult)
            link(last)
            for i in range(8):
                s = SLAB0["a_g"] + i
                dve.wait_ge(g_free[s % 4], tiles_before(s) + 1)
                two = slice(2 * i, 2 * i + 2)
                link(V.tensor_tensor(flat(A_y[:, two, :]), flat(A_y[:, two, :]), flat(A_g[:, two, :]), ALU.mult))
                split(flat(A_yh[:, two, :]), flat(A_yl[:, two, :]), flat(A_y[:, two, :])).then_inc(sem("a_y_ready"), 1)

            def add_out(stage, alpha, pairs=False):
                for i in range(4):
                    n = 2 * i + 1 if pairs else i
                    s = SLAB0[stage] + n
                    cols256 = slice(i * 256, (i + 1) * 256)
                    tile, _ = g_tile(dve, stage, n % 4, n)
                    V.scalar_tensor_tensor(h[:, :, cols256], h[:, :, cols256], alpha,
                                           tile[:, :].rearrange("p (b n) -> p b n", b=NB),
                                           ALU.mult, ALU.add).then_inc(g_free[s % 4], 1)
                    dve.wait_ge(g_free[s % 4], tiles_before(s) + 1)
                    for b in range(NB):
                        last = V.bn_stats(st[:, 4 * b + i, :], h[:, b, cols256])
                link(last)

            add_out("a_out", 1.0, pairs=True)

            stats("b", [h[:, b, :] for b in range(NB)], False, 4)
            normed("xs_b", xs, h)
            rest_T("b_tr", [hT, (hKV_hi, hKV_lo)], ["b_g", "kv_g"])
            tile, free = g_tile(dve, "b_kv", 0, 0)
            V.tensor_tensor(B_kv, tile[:, :].rearrange("p (b n) -> p b n", b=NB), bc(B_bkv, 1, NB),
                            ALU.add).then_inc(free, 1)
            g_read(dve, "b_kv")
            dve.wait_ge(sem("rope_loaded"), 16)
            k4 = B_kv[:, :, 0:P].rearrange("p b (g d) -> p b g d", g=KVH)
            rotate(k4, KVH, B_rope, TMP, sem("k_rot"))
            dve.wait_ge(sem("k_rot"), 1)
            for a in range(2):
                last = V.tensor_copy(B_kdup[:, :, :, a, :], k4)
            last.then_inc(sem("k_rotated"), 1)
            dve.wait_ge(sem("pads_zero"), 3)
            V.tensor_copy(B_vz[:, :, :, 64:128], B_kv[:, :, P:2 * P].rearrange("p b (g d) -> p b g d", g=KVH)
                          ).then_inc(sem("vz_ready"), 1)
            for i in range(4):
                tile, free = g_tile(dve, "b_q", i, i)
                link(V.tensor_tensor(B_q[:, :, i * 256:(i + 1) * 256], tile[:, :].rearrange("p (b n) -> p b n", b=NB),
                                     bc(B_bq[:, i * 256:(i + 1) * 256], 1, NB), ALU.add))
                dve.sem_inc(free, 1)
                rotate(B_q[:, :, i * 256:(i + 1) * 256].rearrange("p b (n d) -> p b n d", n=4), 4, B_rope, TMP,
                       sem("q_rotated"))
                dve.wait_ge(sem("q_rotated"), i + 1)
            take_T("b_qtr", B_qT)
            dve.wait_ge(sem("b_mask_ready"), 1)

            def b_masked(k):
                s, _ = units["b"][k]
                n, keys = s.shape[1:]
                tile, free = x_tile(dve, f"b_s{k}", 0)
                V.scalar_tensor_tensor(s, tile[:, :].rearrange("p (a k) -> p a k", a=n), DH ** -0.5,
                                       bc(B_mask[:, T - keys:], 1, n), ALU.mult, ALU.add).then_inc(free, 1)
                x_read(dve, f"b_s{k}")
                return s

            def b_gated(k):
                b, i = k // 2, k % 2
                tile, free = x_tile(dve, f"b_v{k}", 0)
                V.tensor_tensor(B_yT[:, 4 * i:4 * i + 4, b * P:(b + 1) * P], tile[:, :].rearrange("p (a t) -> p a t", a=4),
                                B_gT[:, 4 * i:4 * i + 4, b * P:(b + 1) * P], ALU.mult).then_inc(free, 1)
                x_read(dve, f"b_v{k}")
                split(*[x[:, 4 * i:4 * i + 4, b * P:(b + 1) * P] for x in (B_yh, B_yl, B_yT)]
                      ).then_inc(sem("b_y_ready"), 1)

            g_read(dve, "b_g")
            attention("b", True, b_masked, b_gated)
            add_out("b_out", 1.0)
            stats("fin", [h[:, b, :] for b in range(NB)], False, 4)
            dve.wait_ge(sem("lnw_loaded"), 16)
            for b in range(NB):
                V.scalar_tensor_tensor(h[:, b, :], h[:, b, :], rstd[:, b:b + 1], fin_g, ALU.mult,
                                       ALU.mult).then_inc(sem("h_b"), 1)
            dve.wait_ge(sem("h_b"), 2)

            rest_T("r_tr", [hT])
            dve.wait_ge(sem("diff_loaded"), 16)
            for i in range(RET_H):
                link(V.tensor_scalar(R_D[:, i, :], R_diff[:, 0, :], R_lg[:, 5, i:i + 1], None, ALU.mult))
                V.scalar_tensor_tensor(R_D[:, i, :], R_diff[:, 1, :], R_lg[:, 5, 4 + i:5 + i], R_D[:, i, :], ALU.mult,
                                       ALU.add).then_inc(sem("decay_arg"), 1)
            dve.wait_ge(sem("rotary_ready"), 1)
            for i in range(8):
                tile, free = g_tile(dve, "r_qk", i, i)
                halves = tile[:, :].rearrange("p (a t) -> p a t", a=2)
                V.tensor_tensor(R_tmp[:, 0, :].rearrange("p (a t) -> p a t", a=2), halves, bc(cosT, 1, 2), ALU.mult)
                V.tensor_tensor(R_tmp[:, 1, :].rearrange("p (a t) -> p a t", a=2), halves, bc(sinT, 1, 2),
                                ALU.mult).then_inc(free, 1)
                s = SLAB0["r_qk"] + i
                dve.wait_ge(free, tiles_before(s) + 1)
                V.tensor_tensor(R_qk[:, 2 * i, :], R_tmp[:, 0, 0:T], R_tmp[:, 1, T:], ALU.subtract)
                link(V.tensor_tensor(R_qk[:, 2 * i + 1, :], R_tmp[:, 0, T:], R_tmp[:, 1, 0:T], ALU.add))
            dve.sem_inc(sem("r_qk_ready"), 8)
            for i in range(RET_H):
                tile, free = x_tile(dve, "r_s", i)
                dve.wait_ge(sem("decay_ready"), i + 1)
                V.scalar_tensor_tensor(flat(R_s[:, i, :, :]), tile[:, :], RET_DK ** -0.5, R_D[:, i, :], ALU.mult,
                                       ALU.mult).then_inc(free, 1)
            x_read(dve, "r_y")
            groups = [R_y[:, i % 2, (i // 2) * RET_DV:(i // 2 + 1) * RET_DV] for i in range(8)]
            stats("gn", groups, True)
            for i, g in enumerate(groups):
                last = V.tensor_scalar(g, g, mv[:, i, 0:1], rstd[:, i:i + 1], ALU.subtract, ALU.mult)
            last.then_inc(sem("r_yn_ready"), 1)
            for i in range(8):
                s = SLAB0["r_g"] + i
                dve.wait_ge(g_free[s % 4], tiles_before(s) + 1)
                tile, free = x_tile(dve, "r_yt", i)
                for a in range(2):
                    c = 2 * i + a
                    last = V.tensor_scalar(R_yT[:, c, :], tile[:, a * T:(a + 1) * T], col("gn_g", c), col("gn_b", c),
                                           ALU.mult, ALU.add)
                last.then_inc(free, 1)
                x_read(dve, "r_yt", i)
                two = slice(2 * i, 2 * i + 2)
                link(V.tensor_tensor(flat(R_yT[:, two, :]), flat(R_yT[:, two, :]), flat(R_g[:, two, :]), ALU.mult))
                split(flat(R_yh[:, two, :]), flat(R_yl[:, two, :]), flat(R_yT[:, two, :])).then_inc(sem("r_y_ready"), 1)
            add_out("r_out", ALPHA, pairs=True)
            layer_norm("mix0", 3, 4)

            def top16(src, best, index):
                n = len(src)
                for k in range(2):
                    for i in range(n):
                        last = V.max(best[:, i, 8 * k:8 * k + 8], src[i])
                    link(last)
                    for i in range(n):
                        last = V.max_index(index[:, i, 8 * k:8 * k + 8], best[:, i, 8 * k:8 * k + 8], src[i])
                    link(last)
                    if k == 0:
                        for i in range(n):
                            last = V.match_replace(src[i], best[:, i, 0:8], src[i], LOWEST)
                        link(last)

            def experts(l):
                rest_T(f"p_tr{l}", [hT])
                for b in range(NB):
                    for i in range(4):
                        x_read(dve, f"p_s{l}", 4 * b + i)
                    top16([K_s[:, b, i, :] for i in range(16)], K_top, K_iu)
                    V.tensor_copy(K_if, K_iu)
                    tops = K_top.rearrange("p (n c) k -> p n c k", c=2)
                    link(V.tensor_tensor(K_cand.rearrange("p n (a b) -> p n a b", a=16), bc(tops[:, :, 0, :], 3, 16),
                                         bc(tops[:, :, 1, :], 2, 16), ALU.add))
                    top16([K_cand[:, i, :] for i in range(PK_H)], K_ts, K_pu)
                    index = K_if.rearrange("p (n c) k -> p n c k", c=2)
                    x_tile(dve, f"p_s{l}", 7)
                    for c, (op, amount) in enumerate([(ALU.logical_shift_right, 4), (ALU.bitwise_and, 15)]):
                        link(V.tensor_scalar(K_au, K_pu, amount, None, op))
                        link(V.tensor_copy(K_af, K_au))
                        link(V.tensor_tensor(K_eq, bc(K_af, 3, 16), bc(bc(iota[:, 0:16], 1, 16), 1, PK_H), ALU.is_equal))
                        link(V.tensor_tensor(K_eq, K_eq, bc(index[:, :, c, :], 2, 16), ALU.mult))
                        link(V.tensor_reduce(picks[:, b, c, :].rearrange("p (n k) -> p n k", k=TOPK), K_eq, AX.X, ALU.add))
                    gate = picks[:, b, 2, :].rearrange("p (n k) -> p n k", k=TOPK)
                    V.tensor_tensor(gate, K_ts, K_ts[:, :, 0:1].broadcast_to([P, PK_H, TOPK]), ALU.subtract
                                    ).then_inc(sem(f"top{l}"), 1)
                    dve.wait_ge(sem(f"top{l}"), b + 1)
                for b in range(NB):
                    gate = picks[:, b, 2, :].rearrange("p (n k) -> p n k", k=TOPK)
                    dve.wait_ge(sem(f"gates{l}"), b + 1)
                    link(V.tensor_reduce(K_sum, gate, AX.X, ALU.add))
                    link(V.reciprocal(K_sum, K_sum))
                    V.tensor_tensor(gate, gate, bc(K_sum, 2, TOPK), ALU.mult).then_inc(sem(f"picks{l}"), 1)
                    dve.wait_ge(sem(f"picks{l}"), b + 1)
                V.memset(K_ungated, 1.0).then_inc(sem(f"ungated{l}"), 1)
                dve.wait_ge(sem(f"ungated{l}"), 1)
                x_tile(dve, f"p_kt{l}", 1)
                for b in range(NB):
                    tile, free = x_tile(dve, f"p_kt{l}", b)
                    V.tensor_copy(picksT[:, :, b * P:(b + 1) * P], tile[:, 0:3 * P].rearrange("p (a t) -> p a t", a=3)
                                  ).then_inc(free, 1)
                x_read(dve, f"p_kt{l}")
                for n in range(GATED - 4, GATED):
                    s = SLAB0[f"u{l}"] + n
                    dve.wait_ge(g_free[s % 4], tiles_before(s) + 1)
                dve.wait_ge(sem(f"h_kept{l}"), 16)
                w0 = X0[f"p_w{l}"]
                experts_by_token = big[:, :].rearrange("p (i t) -> p i t", t=T)

                def hot2(g, group):
                    dve.wait_ge(x_full, group + (w0 - 1))
                    V.tensor_scalar(hot[:, 0, g, 3, :], iota[:, :], picksT[:, 0, bass.ds(group * 4 + 3, 1)], None,
                                    ALU.is_equal)
                    for q in range(4):
                        t = bass.ds(group * 4 + q, 1)
                        last = V.tensor_scalar(hot[:, 1, g, q, :], iota[:, :], picksT[:, 1, t], picksT[:, 2, t],
                                               ALU.is_equal, ALU.mult)
                    last.then_inc(sem(f"hot2_{l}"), 1)

                def times_gelu(j, n, r):
                    s = SLAB0[f"u{l}"] + GATED + j
                    dve.wait_ge(sem(f"gelu{l}"), n + (1 - GATED))
                    V.tensor_tensor(big[:, at(n, 512)], G[s % 4][:, :], big[:, at(n, 512)], ALU.mult
                                    ).then_inc(g_free[s % 4], 1)
                    dve.wait_ge(g_free[s % 4], r + (tiles_before(s) + 1))

                def times_gates(j, g, it):
                    x = w0 + 2 * j + g
                    dve.wait_ge(x_full, it * 8 + (x + 1))
                    t = bass.ds(it * 32 + 4 * (2 * j + g), 4)
                    V.tensor_tensor(experts_by_token[:, :, t], X[x % 4][:, :].rearrange("p (q i) -> p i q", q=4),
                                    experts_by_token[:, :, t], ALU.mult).then_inc(x_free[x % 4], 1)

                with dve.Fori(0, 8) as it:
                    for j in range(4):
                        for g in range(2):
                            hot2(g, it * 8 + (2 * j + g))
                        for g in range(2):
                            x = w0 + 2 * j + g - 2
                            dve.wait_ge(x_free[x % 4], it * 2 + (x // 4 + 1))
                        times_gelu(j, it * 4 + (GATED + j), it)
                        for g in range(2):
                            times_gates(j, g, it)
                x_read(dve, f"p_w{l}")
                for j in range(64 - GATED - 32):
                    times_gelu(j, GATED + 32 + j, 8)
                s0 = SLAB0[f"v{l}"]

                def gated(j, key):
                    x = big[:, at(key, T)]
                    V.tensor_copy(hT_hi[:, j, :], x).then_inc(sem(f"gated_hi{l}"), 1)
                    dve.wait_ge(sem(f"gated_hi{l}"), key + 1)
                    V.tensor_tensor(hT_lo[:, j, :], x, hT_hi[:, j, :], ALU.subtract).then_inc(sem(f"gated_split{l}"), 1)

                for j in range(4):
                    gated(j, j)
                with dve.Fori(1, 32) as it:
                    for j in range(4):
                        dve.wait_ge(half_done, it * 4 + (2 * s0 + j - 3))
                        gated(j, it * 4 + j)
                take_T(f"p_y{l}", K_yT)
                dve.wait_ge(sem(f"h_back{l}"), 16)
                for i in range(4):
                    tile, free = x_tile(dve, f"p_yr{l}", i)
                    part = h[:, i // 2, (i % 2) * 512:(i % 2 + 1) * 512]
                    V.scalar_tensor_tensor(part, part, ALPHA, tile[:, :], ALU.mult, ALU.add).then_inc(free, 1)
                    x_read(dve, f"p_yr{l}", i)
                    last = V.bn_stats(st[:, i, :], part)
                link(last)
                layer_norm(f"ffn{l}", 5 if l == 0 else 9, 2)

            experts(0)

            rest_T("m_tr", [hT])
            g_read(dve, "m_in")
            latents = [M_c[:, b, a:z] for a, z in ((0, Q_RANK), (Q_RANK, Q_RANK + KV_RANK)) for b in range(NB)]
            stats("cn", latents, False)
            for i, (a, z) in enumerate(((0, Q_RANK), (Q_RANK, Q_RANK + KV_RANK))):
                for b in range(NB):
                    last = V.tensor_scalar(M_cn[:, b, a:z], M_c[:, b, a:z], rstd[:, 2 * i + b:2 * i + b + 1], None,
                                           ALU.mult)
            last.then_inc(sem("cn_ready"), 1)
            kr = M_c[:, :, 640:704].unsqueeze(2)
            rotate(kr, 1, rope_row, M_tmp, sem("kr_rot"))
            dve.wait_ge(sem("kr_rot"), 1)
            for a in range(2):
                last = V.tensor_copy(M_kr[:, :, a, :], M_c[:, :, 640:704])
            last.then_inc(sem("kr_rotated"), 1)
            rest_T("m_ct", [(M_cTh, M_cTl)], ["m_qg"], 3)
            for i in range(2):
                tile, free = x_tile(dve, "m_qr", i)
                link(V.tensor_copy(M_qr[:, :, i * 256:(i + 1) * 256], tile[:, :].rearrange("p (b n) -> p b n", b=NB)))
                dve.sem_inc(free, 1)
                rotate(M_qr[:, :, i * 256:(i + 1) * 256].rearrange("p b (n d) -> p b n d", n=4), 4, rope_row, M_tmp,
                       sem("mq_rotated"))
                dve.wait_ge(sem("mq_rotated"), i + 1)
            take_T("m_qrt", M_qrT, (0, 1))

            def m_rest(i):
                tile, free = x_tile(dve, f"m_v{i}", 0)
                dve.wait_ge(sem("rounded_m"), i + 1)
                two = slice(2 * i, 2 * i + 2)
                V.tensor_tensor(flat(M_oTl[:, two, :]), tile[:, :], flat(M_oTh[:, two, :]), ALU.subtract).then_inc(free, 1)

            def m_unit(k):
                tile, _ = x_tile(dve, f"m_s{k}", 0)
                return tile[:, :].rearrange("p (b k) -> p b k", b=NB)

            attention("m", False, m_unit, m_rest)
            add_out("m_out", ALPHA)
            layer_norm("mix1", 7, 4)
            experts(1)

        @block.gpsimd
        def _(pool):
            taken = [0]

            def link(ins):
                taken[0] += 1
                ins.then_inc(pool_step, 1)
                pool.wait_ge(pool_step, taken[0])

            Q = nc.gpsimd

            link(Q.memset(ident[:, :], 0.0))
            Q.affine_select(out=ident[:, :], in_=ident[:, :], compare_op=ALU.not_equal, fill=1.0, base=0,
                            pattern=[[-1, P]], channel_multiplier=1).then_inc(sem("ident_ready"), 1)
            link(Q.iota(iota_i[:, :], pattern=[[1, P]], base=0, channel_multiplier=0))
            Q.tensor_copy(iota[:, :], iota_i[:, :]).then_inc(sem("ident_ready"), 1)

            def split(first, last):
                def one(s, r):
                    j = s % 2
                    for half in range(2):
                        pool.wait_ge(hi_ready, r * 8 + (2 * s + half + 1))
                        Q.tensor_tensor(w_lo[:, 2 * j + half, :], ring[j][:, half * 1024:(half + 1) * 1024],
                                        w_hi[:, 2 * j + half, :], ALU.subtract).then_inc(split_ready, 1)

                n = (last - first) // 4
                if n > 1:
                    with pool.Fori(0, n) as it:
                        for j in range(4):
                            one(first + j, it)
                    first += 4 * n
                for s in range(first, last):
                    one(s, 0)

            split(0, 4)
            pool.wait_ge(sem("ws_loaded"), 16)
            Q.affine_select(out=A_ws, in_=A_ws, compare_op=ALU.is_ge, fill=0.0, base=0,
                            pattern=[[0, 16], [1, P]], channel_multiplier=-1).then_inc(sem("ws_masked"), 1)
            link(Q.memset(B_mask, 0.0))
            link(Q.affine_select(out=B_mask, in_=B_mask, compare_op=ALU.is_ge, fill=NEG, base=-1,
                                 pattern=[[1, T]], channel_multiplier=-1))
            Q.affine_select(out=B_mask, in_=B_mask, compare_op=ALU.is_ge, fill=NEG, base=P,
                            pattern=[[-1, T]], channel_multiplier=1).then_inc(sem("b_mask_ready"), 1)
            pool.wait_ge(sem("b_mask_ready"), 1)
            split(4, SLAB0["b_kv"] + RING)
            pool.wait_ge(half_done, 2 * SLAB0["b_kv"])
            pool.wait_ge(split_ready, 2 * (SLAB0["b_kv"] + RING))
            for i, (a, part) in enumerate(((B_kTe, slice(64, P)), (B_kTo, slice(0, 64)), (B_vz, slice(0, P)))):
                Q.memset(flat(a)[part, :], 0.0).then_inc(sem("pads_zero"), 1)
                pool.wait_ge(sem("pads_zero"), i + 1)
            split(SLAB0["b_kv"] + RING, SLAB0["m_in"] + RING)
            pool.wait_ge(half_done, 2 * SLAB0["m_in"])
            pool.wait_ge(split_ready, 2 * (SLAB0["m_in"] + RING))
            for i, (a, part) in enumerate(((M_krTe, slice(64, P)), (M_krTo, slice(0, 64)))):
                Q.memset(a[part, :], 0.0).then_inc(sem("pads_zero"), 1)
                pool.wait_ge(sem("pads_zero"), i + 4)
            split(SLAB0["m_in"] + RING, N_SLABS)


def kernel(**inputs):
    import concourse.bacc as bacc
    from concourse.bass_utils import run_bass_kernel_spmd

    a = {k: np.asarray(v) for k, v in inputs.items()}
    f32 = np.float32

    def halves(s):
        n, _, k, width = s.shape
        out = np.zeros((n, P, 2, 1024), f32)
        kh = (k + 1) // 2
        out[:, :, 0, :kh * width] = s[:, :, :kh].reshape(n, P, -1)
        out[:, :, 1, :(k - kh) * width] = s[:, :, kh:].reshape(n, P, -1)
        return out.reshape(n, P, 2048)

    def slabs_of(w):
        k, n = w.shape
        chunks = min(DC, k // P)
        s = w.reshape(k // (P * chunks), chunks, P, n // 256, 256).transpose(3, 0, 2, 1, 4)
        return halves(s.reshape(-1, P, chunks, 256))

    def packed(w, blocks):
        k, n = w.shape
        s = w.reshape(k // P, P, n // (512 * blocks), 2, blocks, 256).transpose(2, 1, 3, 4, 0, 5)
        out = np.zeros((s.shape[0], P, 2, 1024), f32)
        out[:, :, :, :blocks * k // P * 256] = s.reshape(s.shape[0], P, 2, -1)
        return out.reshape(-1, P, 2048)

    w_in = a["a_w_in"][0]
    b_in = a["b_w_in"][0]
    ret = a["ret_w_in_2"][0]
    uq = a["mla_w_uq_2"][0].reshape(Q_RANK, MLA_H, P + ROPE)
    mla_in = np.pad(a["mla_w_in_2"][0], ((0, 0), (0, 64)))

    def u_slabs(l):
        return slabs_of(a["peer_u_2"][l].T)

    def v_slabs(l):
        return a["peer_v_2"][l].reshape(64, 2, P, D).transpose(0, 2, 1, 3).reshape(64, P, 2048)

    stages = {
        "a_v": slabs_of(w_in[:, W_A:2 * W_A]), "a_u": slabs_of(w_in[:, :W_A]),
        "a_g": slabs_of(w_in[:, 2 * W_A:]), "a_out": slabs_of(a["a_w_out"][0]),
        "b_kv": slabs_of(a["w_kv"]), "b_q": slabs_of(b_in[:, :D]), "b_g": slabs_of(b_in[:, D:]),
        "b_out": slabs_of(a["b_w_out"][0]),
        "r_qk": slabs_of(ret[:, :2048]), "r_v": slabs_of(ret[:, 2048:4096]),
        "r_g": slabs_of(ret[:, 4096:]), "r_out": slabs_of(a["ret_w_out_2"][0]),
        "m_in": slabs_of(mla_in),
        "m_q": packed(np.concatenate([uq[:, :, P:].reshape(Q_RANK, -1), uq[:, :, :P].reshape(Q_RANK, -1)], 1), 1),
        "m_kv": packed(a["mla_w_ukv_2"][0], 2),
        "m_out": slabs_of(a["mla_w_out_2"][0]),
    }
    slabs = np.empty((N_SLABS, P, 2048), f32)
    for name, n in SLAB_STAGES:
        if name[0] in "uv" and name[1] in "01":
            part = (u_slabs if name[0] == "u" else v_slabs)(int(name[1]))
        elif name.startswith("pq"):
            part = slabs_of(a["peer_w_q_2"][int(name[2])])
        else:
            part = stages[name]
        assert part.shape[0] == n, name
        slabs[SLAB0[name]:SLAB0[name] + n] = part

    def inv_freq(dh):
        return (np.float32(10000.0) ** (-np.arange(0, dh, 2, dtype=f32) / np.float32(dh))).astype(f32)

    angle = np.arange(T, dtype=f32)[:, None] * inv_freq(DH)[None, :]
    rope = np.stack([np.cos(angle), np.sin(angle)], 1).astype(f32).reshape(NB, P, 64).transpose(1, 0, 2).reshape(P, P)
    m, n = np.arange(T)[:, None], np.arange(T)[None, :]
    diff = np.stack([np.maximum(n - m, 0), np.maximum(m - n, 0)]).astype(f32)
    diff = diff.reshape(2, NB, P, T).transpose(2, 0, 1, 3).reshape(P, 1024)

    def columns(v):
        return v.reshape(-1, P).T

    cols = np.concatenate([columns(a["a_norm_g"]), columns(a["kv_norm_g"]), columns(a["b_norm_g"]),
                           columns(a["ret_gn_g_2"]), columns(a["ret_gn_b_2"]), columns(a["mla_q_norm_2"]),
                           columns(a["mla_kv_norm_2"]), inv_freq(RET_DK)[:, None]], 1)

    def pair(w, b, l):
        return np.concatenate([a[w][l], a[b][l]])

    row_parts = {
        "ln_g": a["a_ln_g"], "ln_b": a["a_ln_b"], "bs": a["a_bs"], "bq": a["b_bq"], "bkv": a["b_kv"],
        "sinks": a["b_sinks"], "decay": a["ret_log1m_decay_2"], "invf_row": inv_freq(ROPE), "fin_g": a["final_norm_g"],
        "mix0": pair("ln_mix_g_2", "ln_mix_b_2", 0), "ffn0": pair("ln_ffn_g_2", "ln_ffn_b_2", 0),
        "mix1": pair("ln_mix_g_2", "ln_mix_b_2", 1), "ffn1": pair("ln_ffn_g_2", "ln_ffn_b_2", 1),
    }
    rows = np.concatenate([row_parts[name].ravel() for name, _ in ROWS])[None, :]
    pos = a["positions_2"].reshape(T)
    arrays = {
        "slabs": slabs,
        "x": a["x"].reshape(T, D),
        "cols": cols,
        "rows": rows,
        "ws": a["a_ws"][0].transpose(2, 0, 1).reshape(P, 16 * P),
        "keys": a["peer_sub_keys_2"].reshape(2, 16, NKEYS, P).transpose(0, 3, 1, 2).reshape(2, P, 16 * NKEYS),
        "pos_row": pos.reshape(1, T),
        "pos_col": pos.reshape(NB, P).T,
        "rope": rope,
        "diff": diff,
    }
    arrays = {f"{k}_in": np.ascontiguousarray(v) for k, v in arrays.items()}
    nc = bacc.Bacc("TRN2", target_bir_lowering=False, num_devices=1)
    args = [nc.dram_tensor(k, v.shape, mybir.dt.from_np(v.dtype), kind="ExternalInput").ap() for k, v in arrays.items()]
    out = nc.dram_tensor("out", (T, D), mybir.dt.float32, kind="ExternalOutput").ap()
    h_kept = nc.dram_tensor("h_kept", (T, D), mybir.dt.float32, kind="Internal").ap()
    build(nc, h_kept, *args, out)
    r = run_bass_kernel_spmd(nc, [arrays], core_ids=[0])
    return r.results[0]["out"].reshape(1, T, D)
```
